# Optimizing a Trainium2 kernel written in Bass

```python
import math
import jax, jax.numpy as jnp
from jax import lax
import numpy as np
import jax
import jax.numpy as jnp

D_MODEL = 1024
BATCH = 1
SEQ = 512
DEPTH = 2

N_MEM = 256
BLOCK_Q = 128
MIX_WIDTH = D_MODEL
MEM_WIDTH = D_MODEL // 4
MAIN_WIDTH = MIX_WIDTH - MEM_WIDTH
MEM_HEADS = 4
MEM_DIM = MEM_WIDTH // MEM_HEADS
MLA_V = 64
MLA_HEADS = MAIN_WIDTH // MLA_V
MLA_NOPE = 64
MLA_ROPE = 32
MLA_QK = MLA_NOPE + MLA_ROPE
Q_LORA = 384
KV_LORA = 256
ROPE_THETA = 10000.0
MAX_POS_OFFSET = 4096
FOX_DIM = 64
FOX_HEADS = MAIN_WIDTH // FOX_DIM
EPS = 1e-6
N_A = (DEPTH + 1) // 2
N_B = DEPTH // 2
A_IN = Q_LORA + KV_LORA + MLA_ROPE + MEM_WIDTH + MIX_WIDTH
B_IN = 3 * MAIN_WIDTH + FOX_HEADS + MEM_WIDTH + MIX_WIDTH


def rms_norm(x, g):
    xf = x.astype(jnp.float32)
    y = xf * lax.rsqrt(jnp.mean(xf * xf, axis=-1, keepdims=True) + EPS)
    return (y * g.astype(jnp.float32)).astype(x.dtype)

def split_cols(a, sizes):
    idx = np.cumsum(sizes)[:-1].tolist()
    return jnp.split(a, idx, axis=-1)

def rope(x, pos):
    half = x.shape[-1] // 2
    inv = ROPE_THETA ** (-jnp.arange(half, dtype=jnp.float32) / half)
    ang = pos.astype(jnp.float32)[..., None] * inv
    if x.ndim == 4:
        ang = ang[:, :, None, :]
    cos, sin = jnp.cos(ang), jnp.sin(ang)
    x1 = x[..., :half].astype(jnp.float32)
    x2 = x[..., half:].astype(jnp.float32)
    return jnp.concatenate([x1 * cos - x2 * sin, x2 * cos + x1 * sin], axis=-1).astype(x.dtype)

def causal_block_attention(q, k, v, scale, log_f_cum=None):
    B, S, H, Dk = q.shape
    nb = S // BLOCK_Q
    qb = q.reshape(B, nb, BLOCK_Q, H, Dk).swapaxes(0, 1)
    blk = jnp.arange(nb)
    key_pos = jnp.arange(S)
    if log_f_cum is not None:
        f_t = log_f_cum.transpose(0, 2, 1)
        fb = jnp.moveaxis(f_t.reshape(B, H, nb, BLOCK_Q), 2, 0)
        xs = (blk, qb, fb)
    else:
        xs = (blk, qb)

    def one_block(args):
        i, q_i = args[0], args[1]
        s = jnp.einsum('bqhd,bkhd->bhqk', q_i, k,
                       preferred_element_type=jnp.float32) * scale
        if log_f_cum is not None:
            s = s + (args[2][..., None].astype(jnp.float32) - f_t[:, :, None, :].astype(jnp.float32))
        q_pos = i * BLOCK_Q + jnp.arange(BLOCK_Q)
        mask = key_pos[None, :] <= q_pos[:, None]
        s = jnp.where(mask, s, -jnp.inf)
        p = jax.nn.softmax(s, axis=-1)
        return jnp.einsum('bhqk,bkhd->bqhd', p.astype(v.dtype), v)

    out = lax.map(one_block, xs)
    return out.swapaxes(0, 1).reshape(B, S, H, v.shape[-1])

def memory_attention(q, k, v):
    s = jnp.einsum('bshd,bmhd->bhsm', q, k,
                   preferred_element_type=jnp.float32) * (MEM_DIM ** -0.5)
    p = jax.nn.softmax(s, axis=-1)
    return jnp.einsum('bhsm,bmhd->bshd', p.astype(v.dtype), v)

def mla_mixer(c_q, c_kv, k_r, pos, q_norm, kv_norm, w_q_up, w_kv_up):
    B, S, _ = c_q.shape
    q = (rms_norm(c_q, q_norm) @ w_q_up).reshape(B, S, MLA_HEADS, MLA_QK)
    q_nope, q_rope = q[..., :MLA_NOPE], rope(q[..., MLA_NOPE:], pos)
    kv = (rms_norm(c_kv, kv_norm) @ w_kv_up).reshape(B, S, MLA_HEADS, MLA_NOPE + MLA_V)
    k_nope, v = kv[..., :MLA_NOPE], kv[..., MLA_NOPE:]
    k_rope = jnp.broadcast_to(rope(k_r, pos)[:, :, None, :], (B, S, MLA_HEADS, MLA_ROPE))
    qf = jnp.concatenate([q_nope, q_rope], axis=-1)
    kf = jnp.concatenate([k_nope, k_rope], axis=-1)
    out = causal_block_attention(qf, kf, v, MLA_QK ** -0.5)
    return out.reshape(B, S, MAIN_WIDTH)

def fox_mixer(q, k, v, f_logit, b_f):
    B, S, _ = q.shape
    log_f = jax.nn.log_sigmoid(f_logit.astype(jnp.float32) + b_f.astype(jnp.float32))
    log_f_cum = jnp.cumsum(log_f, axis=1)
    qh = q.reshape(B, S, FOX_HEADS, FOX_DIM)
    kh = k.reshape(B, S, FOX_HEADS, FOX_DIM)
    vh = v.reshape(B, S, FOX_HEADS, FOX_DIM)
    out = causal_block_attention(qh, kh, vh, FOX_DIM ** -0.5, log_f_cum)
    return out.reshape(B, S, MAIN_WIDTH)

def first_inputs(seed: int = 0) -> dict:
    key = jax.random.key(seed)
    ks = jax.random.split(key, 16)
    f32 = jnp.float32

    def nrm(k, shape, fan_in):
        return jax.random.normal(k, shape, f32) * (fan_in ** -0.5)

    def gain(k, shape):
        return 1.0 + 0.01 * jax.random.normal(k, shape, f32)

    x = jax.random.normal(ks[0], (BATCH, SEQ, D_MODEL), f32)
    mem = jax.random.normal(ks[1], (BATCH, N_MEM, D_MODEL), f32)
    positions = (jax.random.randint(ks[2], (BATCH, 1), 0, MAX_POS_OFFSET, dtype=jnp.int32)
                 + jnp.arange(SEQ, dtype=jnp.int32)[None, :])
    return {
        "x": x,
        "mem": mem,
        "positions": positions,
        "norm_pre": gain(ks[3], (DEPTH, D_MODEL)),
        "norm_post": gain(ks[4], (DEPTH, D_MODEL)),
        "mem_norm": gain(ks[5], (D_MODEL,)),
        "w_mem_kv": nrm(ks[6], (DEPTH, D_MODEL, 2 * MEM_WIDTH), D_MODEL),
        "w_out": nrm(ks[7], (DEPTH, MIX_WIDTH, D_MODEL), MIX_WIDTH),
        "w_in_a": nrm(ks[8], (N_A, D_MODEL, A_IN), D_MODEL),
        "q_norm_a": gain(ks[9], (N_A, Q_LORA)),
        "kv_norm_a": gain(ks[10], (N_A, KV_LORA)),
        "w_q_up_a": nrm(ks[11], (N_A, Q_LORA, MLA_HEADS * MLA_QK), Q_LORA),
        "w_kv_up_a": nrm(ks[12], (N_A, KV_LORA, MLA_HEADS * (MLA_NOPE + MLA_V)), KV_LORA),
        "w_in_b": nrm(ks[13], (N_B, D_MODEL, B_IN), D_MODEL),
        "b_f": jax.random.uniform(ks[14], (N_B, FOX_HEADS), f32, 1.0, 4.0),
    }

def first_block(x, mem, positions, norm_pre, norm_post, mem_norm, w_mem_kv, w_out,
              w_in_a, q_norm_a, kv_norm_a, w_q_up_a, w_kv_up_a, w_in_b, b_f):
    B, S, _ = x.shape
    M = mem.shape[1]
    mem_n = rms_norm(mem, mem_norm)
    h = x
    for i in range(DEPTH):
        j = i // 2
        hn = rms_norm(h, norm_pre[i])
        mkv = (mem_n @ w_mem_kv[i]).reshape(M, 2, MEM_HEADS, MEM_DIM) if False else \
            (mem_n @ w_mem_kv[i]).reshape(B, M, 2, MEM_HEADS, MEM_DIM)
        k_m, v_m = mkv[:, :, 0], mkv[:, :, 1]
        if i % 2 == 0:
            proj = hn @ w_in_a[j]
            c_q, c_kv, k_r, q_m, gate = split_cols(
                proj, [Q_LORA, KV_LORA, MLA_ROPE, MEM_WIDTH, MIX_WIDTH])
            main = mla_mixer(c_q, c_kv, k_r, positions, q_norm_a[j], kv_norm_a[j],
                             w_q_up_a[j], w_kv_up_a[j])
        else:
            proj = hn @ w_in_b[j]
            q, k, v, f_logit, q_m, gate = split_cols(
                proj, [MAIN_WIDTH, MAIN_WIDTH, MAIN_WIDTH, FOX_HEADS, MEM_WIDTH, MIX_WIDTH])
            main = fox_mixer(q, k, v, f_logit, b_f[j])
        mem_out = memory_attention(q_m.reshape(B, S, MEM_HEADS, MEM_DIM), k_m, v_m)
        y = jnp.concatenate([main, mem_out.reshape(B, S, MEM_WIDTH)], axis=-1) * jax.nn.silu(gate)
        h = h + rms_norm(y @ w_out[i], norm_post[i])
    return h


CHUNK = 64
HGRN_BLOCK = 16
SB_BLOCK = 128
N_EVEN = (DEPTH + 1) // 2
N_ODD = DEPTH // 2
A_HEADS = 4
A_DK = 128
A_DV = 128
A_QK = A_HEADS * A_DK
A_V = A_HEADS * A_DV
B_HEADS = 4
B_HD = 128
B_WIDTH = B_HEADS * B_HD
P_EVEN = 2 * A_QK + 2 * A_V + 3 * B_WIDTH
MIX_EVEN = A_V + B_WIDTH
C_HEADS = 8
C_DQK = 64
C_DV = 128
C_QK = C_HEADS * C_DQK
C_V = C_HEADS * C_DV
C_CONV = 4
P_ODD = 2 * C_QK + 2 * C_V + 2 * C_HEADS
FFN_DIM = 2816
FFN_CONV = 3


def rmsnorm(x, g):
    xf = x.astype(jnp.float32)
    y = xf * lax.rsqrt(jnp.mean(xf * xf, axis=-1, keepdims=True) + EPS)
    return y * g.astype(jnp.float32)

def modulate(x, g, shift, scale):
    return (rmsnorm(x, g) * (1.0 + scale) + shift).astype(x.dtype)

def head_rmsnorm(o, g):
    b, t, h, d = o.shape
    y = o * lax.rsqrt(jnp.mean(o * o, axis=-1, keepdims=True) + EPS)
    return y.reshape(b, t, h * d) * g.astype(jnp.float32)

def causal_dwconv(x, w, b):
    k = w.shape[0]
    y = lax.conv_general_dilated(x, w[:, None, :].astype(x.dtype), window_strides=(1,),
                                 padding=[(k - 1, 0)], dimension_numbers=('NWC', 'WIO', 'NWC'),
                                 feature_group_count=x.shape[-1])
    return y + b.astype(x.dtype)

def to_chunks(a, size):
    bsz, t = a.shape[0], a.shape[1]
    a = a.reshape((bsz, t // size, size) + a.shape[2:])
    return jnp.swapaxes(jnp.moveaxis(a, 1, 0), 2, 3)

def from_chunks(o):
    n, bsz, h, l, d = o.shape
    return jnp.moveaxis(jnp.swapaxes(o, 2, 3), 0, 1).reshape(bsz, n * l, h, d)

def hgrn2_scan(q, log_f, k, v):
    bsz = q.shape[0]
    mask = jnp.tril(jnp.ones((HGRN_BLOCK, HGRN_BLOCK), dtype=bool))

    def step(state, inp):
        qc, lf, kc, vc = inp
        b = jnp.cumsum(lf, axis=2)
        rel = jnp.where(mask[:, :, None], b[:, :, :, None, :] - b[:, :, None, :, :], -jnp.inf)
        scores = jnp.einsum('bhtd,bhsd,bhtsd->bhts', qc, kc, jnp.exp(rel))
        o = (jnp.einsum('bhts,bhse->bhte', scores, vc)
             + jnp.einsum('bhtd,bhde->bhte', qc * jnp.exp(b), state))
        b_end = b[:, :, -1:, :]
        state = (jnp.exp(b_end[:, :, 0, :])[..., None] * state
                 + jnp.einsum('bhsd,bhse->bhde', kc * jnp.exp(b_end - b), vc))
        return state, o

    s0 = jnp.zeros((bsz, A_HEADS, A_DK, A_DV), jnp.float32)
    xs = (to_chunks(q, HGRN_BLOCK), to_chunks(log_f, HGRN_BLOCK),
          to_chunks(k, HGRN_BLOCK), to_chunks(v, HGRN_BLOCK))
    _, o = lax.scan(step, s0, xs)
    return from_chunks(o)

def stick_breaking(q, k, v):
    bsz, t, h, hd = q.shape
    nb = t // SB_BLOCK

    def blocks(a):
        return a.reshape(bsz, nb, SB_BLOCK, h, hd).transpose(0, 3, 1, 2, 4)

    qb = blocks(q * (hd ** -0.5))
    kb = blocks(k)
    vb = blocks(v)
    incl = jnp.tril(jnp.ones((SB_BLOCK, SB_BLOCK), jnp.float32))
    strict = jnp.tril(jnp.ones((SB_BLOCK, SB_BLOCK), dtype=bool), k=-1)
    out = jnp.zeros((bsz, h, nb, SB_BLOCK, hd), jnp.float32)
    acc = jnp.zeros((bsz, h, nb, SB_BLOCK), jnp.float32)
    for d in range(nb):
        z = jnp.einsum('bhnqd,bhnkd->bhnqk', qb[:, :, d:], kb[:, :, :nb - d]).astype(jnp.float32)
        lk = jax.nn.log_sigmoid(-z)
        if d == 0:
            lk = jnp.where(strict, lk, 0.0)
        r = jnp.einsum('bhnqj,js->bhnqs', lk, incl) + acc[:, :, d:, :, None]
        a = jnp.exp(z + r)
        if d == 0:
            a = jnp.where(strict, a, 0.0)
        out = out.at[:, :, d:].add(
            jnp.einsum('bhnqk,bhnkd->bhnqd', a, vb[:, :, :nb - d].astype(jnp.float32)))
        acc = acc.at[:, :, d:].set(r[..., 0])
    return out.transpose(0, 2, 3, 1, 4).reshape(bsz, t, h, hd)

def mlstm_scan(q, k, v, ig, lf):
    bsz = q.shape[0]
    mask = jnp.tril(jnp.ones((CHUNK, CHUNK), dtype=bool))

    def step(carry, inp):
        cmem, nvec, m = carry
        qc, kc, vc, igc, lfc = inp
        b = jnp.cumsum(lfc, axis=-1)
        log_d = jnp.where(mask, b[..., :, None] - b[..., None, :] + igc[..., None, :], -jnp.inf)
        log_inter = b + m[..., None]
        m_t = jnp.maximum(log_inter, jnp.max(log_d, axis=-1))
        w = jnp.einsum('bhtd,bhsd->bhts', qc, kc) * jnp.exp(log_d - m_t[..., None])
        w_inter = jnp.exp(log_inter - m_t)
        num = (jnp.einsum('bhts,bhse->bhte', w, vc)
               + w_inter[..., None] * jnp.einsum('bhtd,bhde->bhte', qc, cmem))
        den = jnp.sum(w, axis=-1) + w_inter * jnp.einsum('bhtd,bhd->bht', qc, nvec)
        hc = num / jnp.maximum(jnp.abs(den), jnp.exp(-m_t))[..., None]
        m_new = m_t[..., -1]
        w_end = jnp.exp(b[..., -1:] - b + igc - m_new[..., None])
        decay = jnp.exp(b[..., -1] + m - m_new)
        cmem = decay[..., None, None] * cmem + jnp.einsum('bhs,bhsd,bhse->bhde', w_end, kc, vc)
        nvec = decay[..., None] * nvec + jnp.einsum('bhs,bhsd->bhd', w_end, kc)
        return (cmem, nvec, m_new), hc

    init = (jnp.zeros((bsz, C_HEADS, C_DQK, C_DV), jnp.float32),
            jnp.zeros((bsz, C_HEADS, C_DQK), jnp.float32),
            jnp.zeros((bsz, C_HEADS), jnp.float32))
    xs = (to_chunks(q, CHUNK), to_chunks(k, CHUNK), to_chunks(v, CHUNK),
          to_chunks(ig, CHUNK), to_chunks(lf, CHUNK))
    _, hc = lax.scan(step, init, xs)
    return from_chunks(hc)

def even_mixer(h, w_in, lb, norm_g, w_out):
    bsz, t, _ = h.shape
    p = jnp.matmul(h, w_in).astype(jnp.float32)
    splits = [A_QK, 2 * A_QK, 2 * A_QK + A_V, 2 * A_QK + 2 * A_V,
              2 * A_QK + 2 * A_V + B_WIDTH, 2 * A_QK + 2 * A_V + 2 * B_WIDTH]
    qa, fa, ia, ga, qb, kb, vb = jnp.split(p, splits, axis=-1)
    lb_h = lb.astype(jnp.float32).reshape(A_HEADS, A_DK)
    zf = fa.reshape(bsz, t, A_HEADS, A_DK)
    log_f = jnp.logaddexp(jnp.log(lb_h), jnp.log1p(-lb_h) + jax.nn.log_sigmoid(zf))
    k_a = (1.0 - lb_h) * jax.nn.sigmoid(-zf)
    o_a = hgrn2_scan(qa.reshape(bsz, t, A_HEADS, A_DK), log_f, k_a, ia.reshape(bsz, t, A_HEADS, A_DV))
    o_a = head_rmsnorm(o_a, norm_g) * jax.nn.silu(ga)
    o_b = stick_breaking(qb.reshape(bsz, t, B_HEADS, B_HD), kb.reshape(bsz, t, B_HEADS, B_HD),
                         vb.reshape(bsz, t, B_HEADS, B_HD)).reshape(bsz, t, B_WIDTH)
    o = jnp.concatenate([o_a, o_b], axis=-1).astype(h.dtype)
    return jnp.matmul(o, w_out)

def odd_mixer(h, w_in, conv_w, conv_b, gate_b, norm_g, w_out):
    bsz, t, _ = h.shape
    p = jnp.matmul(h, w_in).astype(jnp.float32)
    qk, v, og, gates = jnp.split(p, [2 * C_QK, 2 * C_QK + C_V, 2 * C_QK + 2 * C_V], axis=-1)
    qk = jax.nn.silu(causal_dwconv(qk, conv_w.astype(jnp.float32), conv_b.astype(jnp.float32)))
    q, k = jnp.split(qk, 2, axis=-1)
    q = q.reshape(bsz, t, C_HEADS, C_DQK)
    k = k.reshape(bsz, t, C_HEADS, C_DQK) * (C_DQK ** -0.5)
    gates = gates + gate_b.astype(jnp.float32)
    ig = gates[..., :C_HEADS]
    lf = jax.nn.log_sigmoid(gates[..., C_HEADS:])
    hc = mlstm_scan(q, k, v.reshape(bsz, t, C_HEADS, C_DV), ig, lf)
    o = head_rmsnorm(hc, norm_g) * jax.nn.sigmoid(og)
    return jnp.matmul(o.astype(h.dtype), w_out)

def conv_glu_ffn(h, w_in, conv_w, conv_b, w_out):
    u = jnp.matmul(h, w_in)
    a, g = jnp.split(u, 2, axis=-1)
    a = causal_dwconv(a, conv_w, conv_b)
    return jnp.matmul(jax.nn.gelu(a) * g, w_out)

def second_inputs(seed: int = 0) -> dict:
    key = jax.random.key(seed)
    ks = jax.random.split(key, 24)

    def nrm(k, shape, scale):
        return jax.random.normal(k, shape, jnp.float32) * scale

    d = D_MODEL
    gate_b = jnp.concatenate([
        nrm(ks[13], (N_ODD, C_HEADS), 0.1),
        jnp.linspace(3.0, 6.0, C_HEADS, dtype=jnp.float32)[None, :] + nrm(ks[14], (N_ODD, C_HEADS), 0.1)], axis=-1)
    return {
        'x': nrm(ks[0], (BATCH, SEQ, d), 1.0),
        'c': nrm(ks[1], (BATCH, d), 1.0),
        'ada_w': nrm(ks[2], (DEPTH, d, 6 * d), 0.5 * d ** -0.5),
        'ada_b': nrm(ks[3], (DEPTH, 6 * d), 0.02),
        'norm_mix_g': 1.0 + nrm(ks[4], (DEPTH, d), 0.02),
        'norm_ffn_g': 1.0 + nrm(ks[5], (DEPTH, d), 0.02),
        'even_w_in': nrm(ks[6], (N_EVEN, d, P_EVEN), d ** -0.5),
        'even_w_out': nrm(ks[7], (N_EVEN, MIX_EVEN, d), MIX_EVEN ** -0.5),
        'hgrn_lb': nrm(ks[8], (N_EVEN, A_QK), 0.5),
        'hgrn_norm_g': 1.0 + nrm(ks[9], (N_EVEN, A_V), 0.02),
        'odd_w_in': nrm(ks[10], (N_ODD, d, P_ODD), d ** -0.5),
        'odd_conv_w': nrm(ks[11], (N_ODD, C_CONV, 2 * C_QK), C_CONV ** -0.5),
        'odd_conv_b': nrm(ks[12], (N_ODD, 2 * C_QK), 0.02),
        'odd_gate_b': gate_b,
        'odd_norm_g': 1.0 + nrm(ks[15], (N_ODD, C_V), 0.02),
        'odd_w_out': nrm(ks[16], (N_ODD, C_V, d), C_V ** -0.5),
        'ffn_w_in': nrm(ks[17], (DEPTH, d, 2 * FFN_DIM), d ** -0.5),
        'ffn_conv_w': nrm(ks[18], (DEPTH, FFN_CONV, FFN_DIM), FFN_CONV ** -0.5),
        'ffn_conv_b': nrm(ks[19], (DEPTH, FFN_DIM), 0.02),
        'ffn_w_out': nrm(ks[20], (DEPTH, FFN_DIM, d), FFN_DIM ** -0.5),
        'final_g': 1.0 + nrm(ks[21], (d,), 0.02),
    }

def second_block(x, c, ada_w, ada_b, norm_mix_g, norm_ffn_g, even_w_in, even_w_out, hgrn_lb,
              hgrn_norm_g, odd_w_in, odd_conv_w, odd_conv_b, odd_gate_b, odd_norm_g, odd_w_out,
              ffn_w_in, ffn_conv_w, ffn_conv_b, ffn_w_out, final_g):
    lb_all = jnp.cumsum(jax.nn.softmax(hgrn_lb.astype(jnp.float32), axis=0), axis=0)
    lb_all = lb_all - lb_all[:1]
    cs = jax.nn.silu(c)
    for layer in range(DEPTH):
        j = layer // 2
        mod = jnp.matmul(cs, ada_w[layer]) + ada_b[layer]
        sh_m, sc_m, g_m, sh_f, sc_f, g_f = [m[:, None, :] for m in jnp.split(mod, 6, axis=-1)]
        h = modulate(x, norm_mix_g[layer], sh_m, sc_m)
        if layer % 2 == 0:
            y = even_mixer(h, even_w_in[j], lb_all[j], hgrn_norm_g[j], even_w_out[j])
        else:
            y = odd_mixer(h, odd_w_in[j], odd_conv_w[j], odd_conv_b[j], odd_gate_b[j],
                          odd_norm_g[j], odd_w_out[j])
        x = x + (g_m * y).astype(x.dtype)
        h = modulate(x, norm_ffn_g[layer], sh_f, sc_f)
        x = x + (g_f * conv_glu_ffn(h, ffn_w_in[layer], ffn_conv_w[layer], ffn_conv_b[layer],
                                    ffn_w_out[layer])).astype(x.dtype)
    return rmsnorm(x, final_g).astype(x.dtype)


def setup_inputs(seed=0):
    out = dict(first_inputs(seed))
    for name, value in second_inputs(seed + 1).items():
        if name != "x":
            out[name + "_2"] = value
    return out


def reference(
    x, mem, positions, norm_pre, norm_post, mem_norm, w_mem_kv, w_out, w_in_a, q_norm_a,
    kv_norm_a, w_q_up_a, w_kv_up_a, w_in_b, b_f, c_2, ada_w_2, ada_b_2, norm_mix_g_2,
    norm_ffn_g_2, even_w_in_2, even_w_out_2, hgrn_lb_2, hgrn_norm_g_2, odd_w_in_2, odd_conv_w_2,
    odd_conv_b_2, odd_gate_b_2, odd_norm_g_2, odd_w_out_2, ffn_w_in_2, ffn_conv_w_2,
    ffn_conv_b_2, ffn_w_out_2, final_g_2,
):
    x = first_block(
        x, mem, positions, norm_pre, norm_post, mem_norm, w_mem_kv, w_out, w_in_a, q_norm_a,
        kv_norm_a, w_q_up_a, w_kv_up_a, w_in_b, b_f,
    )
    return second_block(
        x, c_2, ada_w_2, ada_b_2, norm_mix_g_2, norm_ffn_g_2, even_w_in_2, even_w_out_2,
        hgrn_lb_2, hgrn_norm_g_2, odd_w_in_2, odd_conv_w_2, odd_conv_b_2, odd_gate_b_2,
        odd_norm_g_2, odd_w_out_2, ffn_w_in_2, ffn_conv_w_2, ffn_conv_b_2, ffn_w_out_2,
        final_g_2,
    )


_drawn_inputs = setup_inputs


def setup_inputs(seed=0):
    import zlib

    import numpy as np

    out = dict(_drawn_inputs(seed))
    spreads = {}
    factors = {'norm_pre': 2.839,
     'norm_post': 4.898,
     'mem_norm': 8.0,
     'q_norm_a': 6.825,
     'kv_norm_a': 4.431,
     'ada_b_2': 2.892,
     'norm_mix_g_2': 8.0,
     'norm_ffn_g_2': 8.0,
     'hgrn_norm_g_2': 8.0,
     'odd_conv_b_2': 64.0,
     'odd_norm_g_2': 64.0,
     'ffn_conv_b_2': 21.402,
     'final_g_2': 8.195,
     'odd_conv_w_2': 5.505}
    for name, (base, spread) in spreads.items():
        noise = np.random.default_rng([zlib.crc32(name.encode()), seed]).standard_normal(out[name].shape)
        drawn = base * np.exp(spread * noise) if base else spread * noise
        out[name] = jnp.asarray(drawn.astype(out[name].dtype))
    for name, factor in factors.items():
        out[name] = (out[name] * factor).astype(out[name].dtype)
    return out
```

```python
from contextlib import ExitStack

import numpy as np

import concourse.bass as bass
from concourse import mybir

P = 128
S = 512
NB = S // P
D = 1024
KT = D // P
M = 256
DEPTH = 2
EPS = 1e-6
HEADS = 12
MEM_HEADS = 4
Q_LORA, KV_LORA, ROPE, NOPE = 384, 256, 32, 64
MLA_SCALE = float(NOPE + ROPE) ** -0.5
HD = 64
MAIN = HEADS * HD
FFN = 2816
FT = FFN // P
HG_HEADS = 4
ML_HEADS = 8
RING = 4
CHUNK = 256
ROT = 6
ACC = 4

ALU = mybir.AluOpType
ACT = mybir.ActivationFunctionType
AX_X = mybir.AxisListType.X
F32 = mybir.dt.float32
BF16 = mybir.dt.bfloat16
I32 = mybir.dt.int32
U8 = mybir.dt.uint8

WIDE = [S - P * j for j in range(NB)]
OFF = [0, 512, 896, 1152]
PACK = sum(WIDE)
TRI_BANK = [(0, 0), (1, 0), (2, 0), (2, 256)]

VEC_ROWS = {}
for _tile, _names in enumerate([
        [("c_2", 8), ("norm_pre", 16), ("norm_post", 16), ("mem_norm", 8), ("q_norm_a", 3), ("kv_norm_a", 2),
         ("norm_mix_g_2", 16), ("norm_ffn_g_2", 16), ("hgrn_norm_g_2", 4), ("odd_norm_g_2", 8), ("final_g_2", 8),
         ("odd_conv_b_2", 8), ("hgrn_lb_2", 4)],
        [("ada_b_2", 96), ("odd_conv_w_2", 32)],
        [("ffn_conv_b_2", 44), ("ffn_conv_w_2/0", 66)],
        [("ffn_conv_w_2/1", 66)]]):
    _at = 0
    for _n, _k in _names:
        VEC_ROWS[_n] = (_tile, _at, _k)
        _at += _k
VEC_TILES = 4

C_ID, C_ONE, C_NINCL, C_NONE, C_CAUSAL, C_ROT, C_FREQ = 0, 128, 256, 384, 512, 640, 672
C_COLS = 673
HG_LEVELS = [1, 2, 4, 8, 16, 32, 64]


def constants():
    c = np.zeros((P, C_COLS), np.float32)
    i = np.arange(P)
    c[:, C_ID:C_ID + P] = np.eye(P)
    c[:, C_ONE:C_ONE + P] = 1.0
    c[:, C_NINCL:C_NINCL + P] = -(i[None, :] <= i[:, None]).astype(np.float32)
    c[:, C_NONE:C_NONE + P] = -1.0
    c[:, C_CAUSAL:C_CAUSAL + P] = np.where(i[None, :] <= i[:, None], 0.0, -1e30)
    half = ROPE // 2
    for r in range(half):
        c[NOPE + r + half, C_ROT + r] = -1.0
        c[NOPE + r, C_ROT + r + half] = 1.0
    freq = np.float32(10000.0) ** (-np.arange(half, dtype=np.float32) / np.float32(half))
    c[NOPE:NOPE + ROPE, C_FREQ] = np.concatenate([freq, freq])
    m = np.zeros((P, len(HG_LEVELS) + 1, P), np.float32)
    s, t = i[:, None], i[None, :]
    m[:, 0] = s == t
    for n, h in enumerate(HG_LEVELS):
        m[:, n + 1] = (s // (2 * h) == t // (2 * h)) & (s // h % 2 == 0) & (t // h % 2 == 1)
    before = np.where(t <= s, -1e30, 0.0).astype(np.float32)
    return np.concatenate([c, m.reshape(P, -1), before], axis=1)


def weight_plan(a):
    def k8(name, w, lo, hi):
        v = w.rearrange("(t p) n -> p t n", p=P)
        return [(name, v[:, :, c:min(c + CHUNK, hi)], KT, min(CHUNK, hi - c)) for c in range(lo, hi, CHUNK)]

    plan = []
    ada = [("ada", c[1], KT, CHUNK) for l in range(DEPTH) for c in k8("ada", a["ada_w_2"][l], 0, 6 * D)]

    def add(chunks, per=0):
        for n, c in enumerate(chunks):
            plan.append(c)
            for _ in range((n + 1) * per // len(chunks) - n * per // len(chunks)):
                plan.append(ada.pop(0))

    for l in range(DEPTH):
        add(k8(f"mem{l}", a["w_mem_kv"][l], 0, 512), 3)
    w = a["w_in_a"][0]
    add(k8("in_a.cq", w, 0, 256) + k8("in_a.cq", w, 256, 512) + k8("in_a.kr", w, 512, 672)
        + k8("in_a.qm", w, 672, 928) + k8("in_a.gate", w, 928, 1952), 12)
    q = a["w_q_up_a"][0].rearrange("(t p) n -> p t n", p=P)
    add([("q_up", q[:, :, n * 576:(n + 1) * 576], 3, 576) for n in range(2)])
    kv = a["w_kv_up_a"][0].rearrange("(t p) (h n) -> p t h n", p=P, n=NOPE + HD)
    add([("kv_up", kv[:, :, :, 0:NOPE], 2, MAIN), ("kv_up", kv[:, :, :, NOPE:NOPE + HD], 2, MAIN)])
    add(k8("out_a", a["w_out"][0], 0, D), 6)
    w = a["w_in_b"][0]
    add(k8("in_b.f", w, 3 * MAIN, 3 * MAIN + HEADS) + k8("in_b.q", w, 0, MAIN) + k8("in_b.k", w, MAIN, 2 * MAIN)
        + k8("in_b.v", w, 2 * MAIN, 3 * MAIN) + k8("in_b.qm", w, 2316, 2572) + k8("in_b.gate", w, 2572, 3596), 18)
    add(k8("out_b", a["w_out"][1], 0, D), 6)
    assert not ada
    w = a["even_w_in_2"][0]
    for name, lo in (("qa", 0), ("fa", 512), ("ia", 1024), ("ga", 1536), ("qb", 2048), ("kb", 2560), ("vb", 3072)):
        add(k8("even." + name, w, lo, lo + 512))
    add(k8("even_out", a["even_w_out_2"][0], 0, D))

    def ffn(l):
        w = a["ffn_w_in_2"][l]
        for x, g in zip(k8(f"ffn{l}.a", w, 0, FFN), k8(f"ffn{l}.g", w, FFN, 2 * FFN)):
            add([x, g])
        v = a["ffn_w_out_2"][l].rearrange("(t p) n -> p t n", p=P)
        for c in range(0, D, CHUNK):
            add([(f"ffn{l}.out", v[:, t:min(t + KT, FT), c:c + CHUNK], min(KT, FT - t), CHUNK)
                 for t in range(0, FT, KT)])

    ffn(0)
    w = a["odd_w_in_2"][0]
    add(k8("odd.gates", w, 3072, 3088) + k8("odd.qk", w, 0, 1024) + k8("odd.v", w, 1024, 2048)
        + k8("odd.og", w, 2048, 3072))
    add(k8("odd_out", a["odd_w_out_2"][0], 0, D))
    ffn(1)
    return plan


class Engine:

    def __init__(self, eng):
        self.eng, self.seen = eng, {}

    def wait_ge(self, sem, value):
        if self.seen.get(sem.name, 0) < value:
            self.eng.wait_ge(sem, value)
            self.seen[sem.name] = value


class Chain:

    def __init__(self, eng, sem):
        self.eng, self.sem, self.n = eng, sem, 0

    def step(self, ins):
        ins.then_inc(self.sem, 1)
        self.n += 1

    def settle(self):
        self.eng.wait_ge(self.sem, self.n)

    def link(self, ins):
        self.step(ins)
        self.settle()


def two_block_kernel(nc, a, out):
    plan = weight_plan(a)
    landing = []
    for n, (_, src, kt, _) in enumerate(plan):
        landing.append((landing[n - RING] if n >= RING else 0) + 16 * (kt if len(src.shape) == 4 else 1))
    with ExitStack() as ctx:
        def sb(name, shape, dt=F32):
            return ctx.enter_context(nc.sbuf_tensor(name, shape, dt))

        def sem(name):
            return ctx.enter_context(nc.semaphore(name))

        banks = [ctx.enter_context(nc.psum_tensor(f"bank{n}", [P, S], F32)) for n in range(8)]
        ssq_bank, mod_bank = banks[ROT], banks[ROT + 1]

        x = sb("x", [P, KT, S])
        hn = sb("hn", [P, KT, S])
        ring = sb("ring", [P, RING, KT * CHUNK])
        arena = sb("arena", [P, 29696])
        consts = sb("consts", [P, C_COLS])
        masks = sb("masks", [P, (len(HG_LEVELS) + 1) * P], U8)
        identb = sb("identb", [P, P], BF16)
        causal = sb("causal", [P, P], BF16)
        not_before = sb("not_before", [P, P], BF16)
        vecs = sb("vecs", [P, VEC_TILES * P])
        cs = sb("cs", [P, KT])
        acc = sb("acc", [P, ACC, CHUNK])
        mod = sb("mod", [P, 6 * KT * DEPTH])
        gmod = sb("gmod", [P, 4, KT])
        sq = sb("sq", [P, 2, S])
        var = sb("var", [P, S])
        rstd = sb("rstd", [P, S])
        km = sb("km", [P, DEPTH, 2, M])
        vm = sb("vm", [P, DEPTH, 2, M])
        mx = sb("mx", [P, 2, NB])
        nmx = sb("nmx", [P, 2, NB])
        rsum = sb("rsum", [P, 2, NB])
        rinv = sb("rinv", [P, 2, NB])
        bf = sb("bf", [16, 2])
        lbt = sb("lbt", [P, 4, HG_HEADS])

        ident = consts[:, C_ID:C_ID + P]
        ones = consts[:, C_ONE:C_ONE + P]
        nincl = consts[:, C_NINCL:C_NINCL + P]
        nones = consts[:, C_NONE:C_NONE + P]
        ropes = slice(NOPE, NOPE + ROPE)
        rot = consts[ropes, C_ROT:C_ROT + ROPE]
        freq = consts[ropes, C_FREQ:C_FREQ + 1]

        def region(at, *shape):
            n = int(np.prod(shape))
            v = arena[:, at:at + n]
            if len(shape) == 1:
                return v
            names = " ".join("abc"[:len(shape)])
            return v.rearrange(f"p ({names}) -> p {names}", **{k: s for k, s in zip("abc", shape)})

        x_tok = region(0, NB, D)
        m_tok = region(4096, 2, D)
        vec_tok = region(6144, VEC_TILES, P)
        masks_f = region(10240, (len(HG_LEVELS) + 2) * P)
        qf, kf = region(0, HEADS, S), region(6144, HEADS, S)
        v1 = region(12288, NB, MAIN)
        mem_n = region(12288, KT, M)
        gate = region(15360, KT, S)
        qm = region(23552, 2, S)
        cq, ckv, kr = region(24576, 3, S), region(26112, 2, S), region(27136, S)
        probs = region(24576, 2, PACK)
        cos, sin = region(27648, S), region(28160, S)
        posf, turn = region(8192, S), region(8704, S)
        pos_i = region(9216, S)
        frow = region(24576, 6, S)
        rt = hn[:, 0:4, :]
        o1 = region(0, KT, S)
        probsT = hn[:, :, :].rearrange("p (a b) s -> p a b s", a=2)
        hq, hk, pf, pb = (region(2048 * n, HG_HEADS, S) for n in range(4))
        hx = [region(8192 + 2048 * n, HG_HEADS, S) for n in range(2)]
        va = region(12288, NB, 512)
        y2 = region(14336, KT, S)
        at_d, at_1, at_2 = region(18432, HG_HEADS, S), region(20480, HG_HEADS, 256), region(21504, HG_HEADS, 512)
        qb, kb, vb = region(23552, 4, S), region(25600, 4, S), region(27648, NB, 512)
        soft = [region(18432 + PACK * n, PACK) for n in range(2)]
        lnb = region(18432 + PACK * 2, PACK)
        stick = [region(PACK * n, PACK) for n in range(2)]
        qk_raw = region(0, KT, S + 3)
        hsq = region(0, KT, S)
        qkc = region(4160, KT, S)
        vo = region(8256, NB, D)
        og = region(12352, KT, S)
        dec = [region(16448 + PACK * n, PACK) for n in range(2)]
        floor_b = [region(19008 + S * n, S) for n in range(2)]
        ho = region(20032, KT, S)
        grow = region(24128, 8, S)
        ngcol = region(28224, NB, ML_HEADS)
        den = region(28288, S)
        deni = region(28800, S)
        out_tok = region(0, NB, D)
        hact = region(0, FT, S)
        a_raw = [region(11264 + 514 * n, 514) for n in range(2)]
        conv = [region(12320 + S * n, S) for n in range(2)]
        gel = [region(13344 + S * n, S) for n in range(2)]

        def vec(name, n=0):
            tile, row, _ = VEC_ROWS[name]
            return vecs[:, tile * P + row + n:tile * P + row + n + 1]

        loaded_x, loaded_m = sem("loaded_x"), sem("loaded_m")
        loaded_c, loaded_v, loaded_p = sem("loaded_constants"), sem("loaded_vectors"), sem("loaded_positions")
        landed = [sem(f"chunk_landed{n}") for n in range(RING)]
        filled = sem("banks_filled")
        emptied = {"act": sem("emptied_by_act"), "dve": sem("emptied_by_dve")}
        sq_ready, sq_used = sem("square_ready"), sem("square_summed")
        ssq_taken, var_ready, rstd_ready = sem("ssq_taken"), sem("inverse_ready"), sem("rstd_ready")
        hn_ready, scaled = sem("normed_ready"), sem("normed_scaled")
        x_ready = sem("x_tile_ready")
        ada_done, ada_summed = sem("ada_partial"), sem("ada_summed")
        cs_ready, mod_ready, const_ready = sem("silu_c_ready"), sem("mod_ready"), sem("bf16_constants")
        nmx_ready, rinv_ready, probs_ready = sem("neg_max_ready"), sem("inverse_sum_ready"), sem("probs_ready")
        angle_ready, sin_ready = sem("angle_ready"), sem("sin_ready")
        kr_ready, rope_done, kf_ready = sem("rotary_key_ready"), sem("rope_done"), sem("keys_ready")
        f_log, frows_ready, frows_moved = sem("forget_log"), sem("forget_rows"), sem("forget_rows_moved")
        frows_set = sem("unit_rows_set")
        dve_step, act_step, pool_step = sem("dve_step"), sem("act_step"), sem("pool_step")
        hx_ready, levels_up, hg_ready = sem("level_ready"), sem("level_updated"), sem("decay_ready")
        lb_diff, lb_exp, lb_ready, hg_set = (sem("lb_difference"), sem("lb_exp"), sem("lb_ready"), sem("hgrn_set"))
        soft_log, soft_ready, soft_masked = sem("softplus_log"), sem("softplus_ready"), sem("softplus_masked")
        stick_sums = sem("stick_sums")
        sq_heads, head_inv, rstd_heads, y_heads = (sem("head_squares"), sem("head_inverse"), sem("head_rstd"),
                                                   sem("head_output_ready"))
        gates_moved, g_log = sem("gates_moved"), sem("gate_log")
        grows_ready, m_ready = sem("gate_rows_ready"), sem("gate_maxima_ready")
        floor_rows = sem("floor_rows")
        dec_exp, dec_masked = sem("decay_exp"), sem("decay_masked")
        qk_conv, qk_silu, qk_pads, pads = sem("qk_conv"), sem("qk_ready"), sem("qk_pads"), sem("conv_pads")
        post_scaled = sem("post_scaled")
        conv_ready, gelu_ready = sem("conv_ready"), sem("gelu_ready")
        stored = sem("stored")

        tiles, index, chunks = [], {}, []

        def wait_emptied(eng, key):
            owner, nth = tiles[index[key]][1:]
            eng.wait_ge(emptied[owner], nth + 1)

        block = ctx.enter_context(nc.Block())

        @block.tensor
        def _(eng):
            pe = Engine(eng)
            owned = {"act": 0, "dve": 0}
            counts = {"sq": 0, "ada": 0, "sum": 0, "hn": 0}

            def bank(key, owner):
                n = len(tiles)
                if n >= ROT:
                    _, who, nth = tiles[n - ROT]
                    pe.wait_ge(emptied[who], nth + 1)
                tiles.append((key, owner, owned[owner]))
                index[key] = n
                owned[owner] += 1
                return banks[n % ROT]

            def done(ins):
                ins.then_inc(filled, 1)

            def chunk(stage):
                n = len(chunks)
                name, _, kt, cols = plan[n]
                assert name == stage, (name, stage)
                chunks.append(None)
                while len(chunks) < len(plan) and plan[len(chunks)][0] == "ada":
                    chunks.append(("dve", counts["ada"]))
                    counts["ada"] += 1
                pe.wait_ge(landed[n % RING], landing[n])
                return n, ring[:, n % RING, 0:kt * cols].rearrange("p (t n) -> p t n", t=kt)

            def chunk_done(n):
                chunks[n] = ("pe", len(tiles))

            def ada_sums(lag):
                while counts["sum"] < counts["ada"] - lag:
                    j = counts["sum"]
                    pe.wait_ge(ada_done, j + 1)
                    for half in range(2):
                        mm = eng.matmul(mod_bank[:, 2 * j + half:2 * j + half + 1],
                                        acc[:, j % ACC, half * P:(half + 1) * P], ones[:, 0:1], start=True, stop=True)
                    mm.then_inc(ada_summed, 1)
                    counts["sum"] += 1

            def features(key, owner, w, cols, src, kts, out_rows=None, ready=None, n=S):
                b = bank(key, owner)
                o = b[0:w[:, 0, cols].shape[1], 0:n] if out_rows is None else b[out_rows, 0:n]
                for k in range(kts):
                    if ready is not None:
                        pe.wait_ge(hn_ready, ready + k + 1)
                    mm = eng.matmul(o, w[:, k, cols], src[:, k, 0:n], start=(k == 0), stop=(k == kts - 1))
                done(mm)

            def tokens(key, owner, w, cols, src, kts, blk, ready=None):
                b = bank(key, owner)
                if ready is not None:
                    pe.wait_ge(hn_ready, ready + kts)
                width = w[:, 0, cols].shape[1]
                for k in range(kts):
                    mm = eng.matmul(b[:, 0:width], src[:, k, blk * P:(blk + 1) * P], w[:, k, cols],
                                    start=(k == 0), stop=(k == kts - 1))
                done(mm)

            def ssq(t, total):
                i = counts["sq"]
                pe.wait_ge(sq_ready, i + 1)
                if t == 0:
                    pe.wait_ge(ssq_taken, counts["hn"])
                    counts["hn"] += 1
                eng.matmul(ssq_bank[:, :], ones, sq[:, i % 2, :], start=(t == 0), stop=(t == total - 1)
                           ).then_inc(sq_used, 1)
                counts["sq"] += 1

            def project(stage, nchunks, owner, ready, tok=False, src=hn, kts=KT, lag=None):
                t = 0
                for _ in range(nchunks):
                    n, w = chunk(stage)
                    cols = w.shape[2]
                    if tok:
                        for b in range(NB):
                            tokens((stage, t, b), owner, w, slice(0, cols), src, kts, b, ready)
                        t += 1
                    else:
                        for c in range(0, cols, P):
                            features((stage, t), owner, w, slice(c, min(c + P, cols)), src, kts, ready=ready)
                            t += 1
                    chunk_done(n)
                    if lag is not None:
                        ada_sums(lag)

            pe.wait_ge(loaded_c, 32)
            pe.wait_ge(loaded_v, 16 * len(VEC_ROWS))
            for n in range(VEC_TILES):
                rows = max(r + k for t, r, k in VEC_ROWS.values() if t == n)
                b = bank(("vec", n), "dve")
                done(eng.transpose(b[:, 0:rows], vec_tok[0:rows, n, :], ident[0:rows, 0:rows]))
            pe.wait_ge(loaded_m, 16)
            for k in range(0, KT, 2):
                b = bank(("mT", k), "dve")
                for j in range(4):
                    t = eng.transpose(b[:, j * P:(j + 1) * P],
                                      m_tok[:, j % 2, (k + j // 2) * P:(k + j // 2 + 1) * P], ident)
                done(t)
            pe.wait_ge(loaded_x, 16)
            for k in range(KT):
                b = bank(("xT", k), "dve")
                for j in range(NB):
                    t = eng.transpose(b[:, j * P:(j + 1) * P], x_tok[:, j, k * P:(k + 1) * P], ident)
                done(t)
            for k in range(4):
                i = counts["sq"]
                pe.wait_ge(sq_ready, i + 1)
                eng.matmul(ssq_bank[:, 0:M], ones, sq[:, i % 2, 0:M], start=(k == 0), stop=False)
                eng.matmul(ssq_bank[:, 0:M], ones, sq[:, i % 2, M:2 * M], start=False, stop=(k == 3)
                           ).then_inc(sq_used, 1)
                counts["sq"] += 1
            counts["hn"] += 1
            for k in range(KT):
                ssq(k, KT)
            for l in range(DEPTH):
                n, w = chunk(f"mem{l}")
                for c in range(2):
                    features(("km", l, c), "act", w, slice(c * P, (c + 1) * P), mem_n, KT, ready=0, n=M)
                chunk_done(n)
                n, w = chunk(f"mem{l}")
                for b in range(2):
                    tokens(("vm", l, b), "act", w, slice(0, M), mem_n, KT, b)
                chunk_done(n)
                ada_sums(2)
            R0 = KT
            for c in range(2):
                n, w = chunk("in_a.cq")
                for t in range(2):
                    features(("cq", 2 * c + t), "act", w, slice(t * P, (t + 1) * P), hn, KT, ready=R0)
                chunk_done(n)
                ada_sums(2)
            n, w = chunk("in_a.kr")
            features(("cq", 4), "act", w, slice(0, P), hn, KT)
            features(("kr",), "act", w, slice(P, P + ROPE), hn, KT, out_rows=ropes)
            chunk_done(n)
            ada_sums(2)
            project("in_a.qm", 1, "act", R0, lag=2)
            for t in range(3):
                ssq(t, 3)
            for t in range(2):
                ssq(t, 2)
            project("in_a.gate", 4, "act", R0, lag=2)
            b = bank(("krot",), "dve")
            wait_emptied(pe, ("kr",))
            done(eng.matmul(b[ropes, :], rot, kr[ropes, :], start=True, stop=True))
            R1 = R0 + KT
            h = 0
            for _ in range(2):
                n, w = chunk("q_up")
                for j in range(6):
                    features(("q", h), "act", w, slice(96 * j, 96 * (j + 1)), cq, 3, ready=R1)
                    if h >= 1:
                        rotate = h - 1
                        b = bank(("qrot", rotate), "dve")
                        wait_emptied(pe, ("q", rotate))
                        done(eng.matmul(b[ropes, :], rot, qf[ropes, rotate, :], start=True, stop=True))
                    h += 1
                chunk_done(n)
            b = bank(("qrot", HEADS - 1), "dve")
            wait_emptied(pe, ("q", HEADS - 1))
            done(eng.matmul(b[ropes, :], rot, qf[ropes, HEADS - 1, :], start=True, stop=True))
            R2 = R1 + 3
            n, w = chunk("kv_up")
            for t in range(6):
                features(("k", 2 * t), "act", w, slice(t * P, (t + 1) * P), ckv, 2, ready=R2)
            chunk_done(n)
            n, w = chunk("kv_up")
            for c in range(2):
                for blk in range(NB):
                    tokens(("v", c, blk), "act", w, slice(384 * c, 384 * (c + 1)), ckv, 2, blk)
            chunk_done(n)

            def attention(l):
                def scores(h):
                    if h == HEADS:
                        wait_emptied(pe, (("in_a.qm", "in_b.qm")[l], 1))
                        wait_emptied(pe, ("km", l, 1))
                    for i in range(NB):
                        b = bank(("s", l, h, i), "act")
                        if h < HEADS:
                            kd, n = (NOPE + ROPE, HD + 2)[l], (i + 1) * P
                            eng.matmul(b[:, 0:n], qf[0:kd, h, i * P:n], kf[0:kd, h, 0:n], start=True, stop=False)
                            done(eng.matmul(b[:, i * P:n], identb[:, :], causal[:, :], start=False, stop=True))
                        else:
                            g = h - HEADS
                            rows = slice(HD * (g % 2), HD * (g % 2) + HD)
                            done(eng.matmul(b[:, 0:M], qm[rows, g // 2, i * P:(i + 1) * P], km[rows, l, g // 2, :],
                                            start=True, stop=True))

                def apply(h):
                    par = h % 2
                    for i in range(NB):
                        nk = i + 1 if h < HEADS else 2
                        po = 128 * (i * (i + 1) // 2) if h < HEADS else i * M
                        b = bank(("t", l, h, i), "dve" if i % 2 else "act")
                        pe.wait_ge(probs_ready, (l * 16 + h) * NB + i + 1)
                        for j in range(nk):
                            t = eng.transpose(b[:, j * P:(j + 1) * P], probs[:, par, po + j * P:po + (j + 1) * P], ident)
                        done(t)
                    b = bank(("o", l, h), "dve")
                    o = b[HD * par:HD * par + HD, :]
                    for i in range(NB):
                        wait_emptied(pe, ("t", l, h, i))
                    nk = NB if h < HEADS else 2
                    for j in range(nk):
                        first = j * P if h < HEADS else 0
                        v = v1[:, j, h * HD:(h + 1) * HD] if h < HEADS else vm[:, l, j, (h - HEADS) * HD:(h - HEADS + 1) * HD]
                        mm = eng.matmul(o[:, first:S], v, probsT[:, par, j, first:S], start=(j == 0), stop=(j == nk - 1))
                    done(mm)

                for h in range(16 + 1):
                    if h < 16:
                        scores(h)
                    if h >= 1:
                        apply(h - 1)

            pe.wait_ge(const_ready, 4)
            pe.wait_ge(kf_ready, 1)
            pe.wait_ge(rope_done, HEADS)
            for c in range(2):
                wait_emptied(pe, ("v", c, NB - 1))
            attention(0)

            def out_first(l):
                stage = ("out_a", "out_b")[l]
                for c in range(4):
                    n, w = chunk(stage)
                    for t in range(2):
                        b = bank((stage, 2 * c + t), "act")
                        for k in range(KT):
                            wait_emptied(pe, ("o", l, 2 * k + 1))
                            mm = eng.matmul(b[:, :], w[:, k, t * P:(t + 1) * P], gate[:, k, :],
                                            start=(k == 0), stop=(k == KT - 1))
                        done(mm)
                        if 2 * c + t >= 1:
                            ssq(2 * c + t - 1, KT)
                    chunk_done(n)
                    ada_sums(2)
                ssq(KT - 1, KT)
                for t in range(KT):
                    ssq(t, KT)

            out_first(0)
            R3 = R2 + 2
            n, w = chunk("in_b.f")
            features(("f",), "act", w, slice(0, HEADS), hn, KT, ready=R3)
            chunk_done(n)
            project("in_b.q", 3, "act", R3, lag=2)
            project("in_b.k", 3, "act", R3, lag=2)
            project("in_b.v", 3, "act", R3, tok=True, lag=2)
            project("in_b.qm", 1, "act", R3, lag=2)
            project("in_b.gate", 4, "act", R3, lag=2)
            for s in range(3):
                wait_emptied(pe, ("in_b.v", s, NB - 1))
            pe.wait_ge(frows_moved, 16 * 2 * HEADS)
            attention(1)
            out_first(1)
            ada_sums(0)

            R4 = R3 + KT
            project("even.qa", 2, "act", R4)
            project("even.fa", 2, "act", R4)
            project("even.ia", 2, "act", R4, tok=True)
            project("even.ga", 2, "act", R4)
            project("even.qb", 2, "act", R4)
            project("even.kb", 2, "act", R4)
            project("even.vb", 2, "act", R4, tok=True)
            def level(name, lhs, rhs):
                for h in range(HG_HEADS):
                    b = bank(name + (h,), "dve")
                    for j in range(NB):
                        c = slice(j * P, (j + 1) * P)
                        mm = eng.matmul(b[:, c], lhs[:, h, c], rhs[:, h, c], start=(j == 0), stop=(j == NB - 1),
                                        skip_group_check=True)
                    done(mm)

            wait_emptied(pe, ("even.vb", 1, NB - 1))
            pe.wait_ge(hg_ready, HG_HEADS)
            level(("diag",), hk, hq)
            for n in range(len(HG_LEVELS)):
                pe.wait_ge(hx_ready, n + 1)
                level(("lv", n), hx[n % 2], hx[n % 2])
            n = len(HG_LEVELS)
            pe.wait_ge(hx_ready, n + 1)
            for h in range(HG_HEADS):
                b = bank(("lv", n, h), "dve")
                X = hx[n % 2]
                eng.matmul(b[:, 0:P], X[:, h, 0:P], X[:, h, P:2 * P], start=True, stop=False, skip_group_check=True)
                done(eng.matmul(b[:, P:2 * P], X[:, h, 2 * P:3 * P], X[:, h, 3 * P:4 * P], start=False, stop=True,
                                skip_group_check=True))
            pe.wait_ge(hx_ready, n + 2)
            for h in range(HG_HEADS):
                b = bank(("lv", n + 1, h), "dve")
                X = hx[(n + 1) % 2]
                eng.matmul(b[:, 0:M], X[:, h, 0:P], X[:, h, M:S], start=True, stop=False, skip_group_check=True)
                done(eng.matmul(b[:, M:S], X[:, h, P:2 * P], X[:, h, M:S], start=False, stop=True,
                                skip_group_check=True))
            for h in range(HG_HEADS):
                b = bank(("ho", h), "act")
                wait_emptied(pe, ("lv", n + 1, h))
                hs = slice(h * P, (h + 1) * P)
                for j in range(NB):
                    c = slice(j * P, (j + 1) * P)
                    eng.matmul(b[:, c], va[:, j, hs], at_d[:, h, c], start=(j == 0), stop=False, skip_group_check=True)
                eng.matmul(b[:, P:2 * P], va[:, 0, hs], at_1[:, h, 0:P], start=False, stop=False, skip_group_check=True)
                eng.matmul(b[:, 3 * P:S], va[:, 2, hs], at_1[:, h, P:2 * P], start=False, stop=False,
                           skip_group_check=True)
                eng.matmul(b[:, M:S], va[:, 0, hs], at_2[:, h, 0:M], start=False, stop=False, skip_group_check=True)
                done(eng.matmul(b[:, M:S], va[:, 1, hs], at_2[:, h, M:S], start=False, stop=True,
                                skip_group_check=True))
            for h in range(HG_HEADS):
                b = bank(("hs", h), "dve")
                pe.wait_ge(sq_heads, h + 1)
                done(eng.matmul(b[:, :], ones, pf[:, h, :], start=True, stop=True))

            def stick_scores(h):
                for j in range(3):
                    zs[h % 2][j] = bank(("z", h, j), "act")
                    for i in range(j, NB):
                        nb, c0 = TRI_BANK[i]
                        if nb == j:
                            mm = eng.matmul(zs[h % 2][j][:, c0:c0 + WIDE[i]], kb[:, h, i * P:(i + 1) * P],
                                            qb[:, h, i * P:S], start=(c0 == 0), stop=(i == NB - 1 or j < 2),
                                            skip_group_check=True)
                    done(mm)

            def stick_later_keys(h):
                pe.wait_ge(soft_masked, h + 1)
                sp = soft[h % 2]
                for j in range(NB):
                    src = sp[:, OFF[j]:OFF[j] + WIDE[j]]
                    nb, c0 = TRI_BANK[j]
                    eng.matmul(zs[h % 2][nb][:, c0:c0 + P], identb[:, :], not_before[:, :], start=False,
                               stop=False, skip_group_check=True)
                    mm = eng.matmul(zs[h % 2][nb][:, c0:c0 + WIDE[j]], nincl, src, start=False, stop=(j == NB - 1),
                                    skip_group_check=True)
                    for i in range(j):
                        nb, c0 = TRI_BANK[i]
                        lo = c0 + (j - i) * P
                        mm = eng.matmul(zs[h % 2][nb][:, lo:lo + WIDE[j]], nones, src, start=False,
                                        stop=(j == NB - 1), skip_group_check=True)
                mm.then_inc(stick_sums, 1)

            def stick_apply(h):
                b = bank(("so", h), "act")
                wait_emptied(pe, ("z", h, 2))
                for j in range(NB):
                    mm = eng.matmul(b[:, j * P:S], vb[:, j, h * P:(h + 1) * P],
                                    stick[h % 2][:, OFF[j]:OFF[j] + WIDE[j]], start=(j == 0), stop=(j == NB - 1))
                done(mm)

            zs = [[None] * 3 for _ in range(2)]
            for h in range(5):
                if h < 4:
                    stick_scores(h)
                if h >= 1:
                    stick_apply(h - 1)
                if h < 4:
                    stick_later_keys(h)

            def out_second(stage, src, nk, wait_src):
                for c in range(4):
                    parts = [chunk(stage) for _ in range(-(-nk // KT))]
                    for t in range(2):
                        b = bank((stage, 2 * c + t), "dve")
                        for k in range(nk):
                            wait_src(k)
                            mm = eng.matmul(b[:, :], parts[k // KT][1][:, k % KT, t * P:(t + 1) * P], src[:, k, :],
                                            start=(k == 0), stop=(k == nk - 1))
                        done(mm)
                        if 2 * c + t >= 1:
                            ssq(2 * c + t - 1, KT)
                    for n, _ in parts:
                        chunk_done(n)
                ssq(KT - 1, KT)

            def wait_even(k):
                if k < 4:
                    pe.wait_ge(y_heads, k + 1)
                else:
                    wait_emptied(pe, ("so", k - 4))

            out_second("even_out", y2, KT, wait_even)

            def ffn(l, ready):
                for t0 in range(0, FT, 2):
                    na, wa = chunk(f"ffn{l}.a")
                    ng, wg = chunk(f"ffn{l}.g")
                    for t in range(2):
                        c = slice(t * P, (t + 1) * P)
                        features(("fa", l, t0 + t), "act", wa, c, hn, KT, ready=ready)
                        features(("fg", l, t0 + t), "dve", wg, c, hn, KT)
                    chunk_done(na)
                    chunk_done(ng)
                out_second(f"ffn{l}.out", hact, FT, lambda k: wait_emptied(pe, ("fg", l, k)))

            R5 = R4 + KT
            ffn(0, R5)
            R6 = R5 + KT
            n, w = chunk("odd.gates")
            features(("og_rows",), "act", w, slice(0, 16), hn, KT, ready=R6)
            chunk_done(n)
            project("odd.qk", 4, "act", R6)
            project("odd.v", 4, "act", R6, tok=True)
            project("odd.og", 4, "act", R6)
            pe.wait_ge(grows_ready, 1)
            b = bank(("gcol",), "dve")
            for j in range(NB):
                t = eng.transpose(b[:, j * ML_HEADS:(j + 1) * ML_HEADS], grow[0:8, 4, j * P:(j + 1) * P],
                                  ident[0:8, 0:8])
            done(t)

            def ml_weights(h):
                pick = ident[0:8, h:h + 1].to_broadcast([8, P])
                b = bank(("mb", h), "act")
                done(eng.matmul(b[:, :], pick, grow[0:8, 5, :], start=True, stop=True))
                b = bank(("eb", h), "act")
                pe.wait_ge(floor_rows, 1)
                done(eng.matmul(b[:, :], pick, grow[0:8, 7, :], start=True, stop=True))
                rows = slice(64 * (h % 2), 64 * (h % 2) + 64)
                for j in range(3):
                    b = bank(("qk", h, j), "dve")
                    for i in range(j, NB):
                        nb, c0 = TRI_BANK[i]
                        if nb == j:
                            mm = eng.matmul(b[:, c0:c0 + WIDE[i]], qkc[rows, 4 + h // 2, i * P:(i + 1) * P],
                                            qkc[rows, h // 2, i * P:S], start=(c0 == 0), stop=(i == NB - 1 or j < 2),
                                            skip_group_check=True)
                    done(mm)

            def ml_apply(h):
                W = dec[h % 2]
                bd = bank(("den", h), "dve")
                wait_emptied(pe, ("qk", h, 2))
                for j in range(NB):
                    mm = eng.matmul(bd[:, j * P:S], ones, W[:, OFF[j]:OFF[j] + WIDE[j]], start=(j == 0),
                                    stop=(j == NB - 1))
                done(mm)
                bn = bank(("num", h), "dve")
                for j in range(NB):
                    mm = eng.matmul(bn[:, j * P:S], vo[:, j, h * P:(h + 1) * P], W[:, OFF[j]:OFF[j] + WIDE[j]],
                                    start=(j == 0), stop=(j == NB - 1))
                done(mm)

            pe.wait_ge(qk_silu, KT)
            wait_emptied(pe, ("odd.og", KT - 1))
            for h in range(ML_HEADS + 1):
                if h < ML_HEADS:
                    ml_weights(h)
                if h >= 1:
                    ml_apply(h - 1)
            for h in range(ML_HEADS):
                b = bank(("ms", h), "dve")
                pe.wait_ge(sq_heads, HG_HEADS + h + 1)
                done(eng.matmul(b[:, :], ones, hsq[:, h, :], start=True, stop=True))
            out_second("odd_out", og, KT, lambda k: pe.wait_ge(y_heads, HG_HEADS + k + 1))
            ffn(1, R6 + KT)
            R7 = R6 + 2 * KT
            for j in range(NB):
                for half in range(2):
                    b = bank(("out", j, half), "dve")
                    pe.wait_ge(hn_ready, R7 + KT)
                    for k in range(4):
                        t = eng.transpose(b[:, k * P:(k + 1) * P], hn[:, 4 * half + k, j * P:(j + 1) * P], ident)
                    done(t)
            assert len(chunks) == len(plan)

        def take(eng, key, owner):
            n = index[key]
            assert tiles[n][1] == owner
            eng.wait_ge(filled, n + 1)
            return banks[n % ROT]

        def peek(eng, key):
            n = index[key]
            eng.wait_ge(filled, n + 1)
            return banks[n % ROT]

        def transposed(eng, who, l, h, odd, owner):
            par = h % 2
            for i in range(odd, NB, 2):
                nk = i + 1 if h < HEADS else 2
                b = take(who, ("t", l, h, i), owner)
                if h >= 2:
                    peek(who, ("o", l, h - 2))
                src = b[:, 0:nk * P].rearrange("p (j q) -> p j q", q=P)
                dst = probsT[:, par, 0:nk, i * P:(i + 1) * P]
                if owner == "act":
                    eng.activation(dst, src, ACT.Copy).then_inc(emptied[owner], 1)
                else:
                    eng.tensor_copy(dst, src).then_inc(emptied[owner], 1)

        @block.sync
        def _(eng):
            sp = Engine(eng)
            eng.dma_start(consts[:, :], a["const_f32"][:, 0:C_COLS]).then_inc(loaded_c, 16)
            eng.dma_start(masks_f, a["const_f32"][:, C_COLS:]).then_inc(loaded_c, 16)
            eng.dma_start(m_tok, a["mem"][0].rearrange("(b p) d -> p b d", p=P)).then_inc(loaded_m, 16)
            eng.dma_start(x_tok, a["x"][0].rearrange("(b p) d -> p b d", p=P)).then_inc(loaded_x, 16)
            for n, (name, src, kt, cols) in enumerate(plan):
                if n >= RING:
                    user, count = chunks[n - RING]
                    if user == "pe":
                        sp.wait_ge(filled, count)
                    else:
                        sp.wait_ge(ada_done, count + 1)
                dst = ring[:, n % RING, 0:kt * cols].rearrange("p (t n) -> p t n", t=kt)
                if len(src.shape) == 4:
                    for t in range(kt):
                        eng.dma_start(dst[:, t, :].rearrange("p (h n) -> p h n", h=HEADS), src[:, t]
                                      ).then_inc(landed[n % RING], 16)
                    continue
                eng.dma_start(dst, src).then_inc(landed[n % RING], 16)
            for j in range(NB):
                wait_emptied(sp, ("out", j, 1))
                eng.dma_start(out[0, j * P:(j + 1) * P, :], out_tok[:, j, :]).then_inc(stored, 16)
            eng.wait_ge(stored, 16 * NB)

        @block.scalar
        def _(eng):
            act = Engine(eng)
            chain = Chain(eng, act_step)
            used = {"sq": 0, "norm": 0}

            for name, (tile, row, k) in VEC_ROWS.items():
                base, _, l = name.partition("/")
                src = a[base][int(l)] if l else a[base]
                if len(src.shape) > 1:
                    dims = " ".join("abc"[:len(src.shape)])
                    src = src.rearrange(f"{dims} -> ({dims})")
                eng.dma_start(vec_tok[row:row + k, tile, :], src.rearrange("(r p) -> r p", p=P)).then_inc(loaded_v, 16)
            eng.dma_start(bf[0:HEADS, 0:1], a["b_f"].rearrange("a h -> h a")).then_inc(loaded_p, 16)
            eng.dma_start(bf[0:16, 1:2], a["odd_gate_b_2"].rearrange("a h -> h a")).then_inc(loaded_p, 16)
            eng.dma_start(pos_i.bitcast(I32)[ropes, :], a["positions"][0].partition_broadcast(ROPE)).then_inc(loaded_p, 16)

            def empty(key, out, func=ACT.Copy, part=None, **kw):
                b = take(act, key, "act")
                eng.activation(out, b[:, :] if part is None else b[part], func, **kw).then_inc(emptied["act"], 1)

            def square(src):
                i = used["sq"]
                if i >= 2:
                    act.wait_ge(sq_used, i - 1)
                eng.activation(sq[:, i % 2, :], src, ACT.Square).then_inc(sq_ready, 1)
                used["sq"] += 1

            def root(n=S):
                k = used["norm"]
                act.wait_ge(var_ready, k + 1)
                eng.activation(rstd[:, 0:n], var[:, 0:n], ACT.Sqrt).then_inc(rstd_ready, 1)
                used["norm"] += 1

            wait_emptied(act, ("vec", 0))
            eng.activation(cs[:, :], vecs[:, 0:KT], ACT.Silu).then_inc(cs_ready, 1)
            for k in range(4):
                wait_emptied(act, ("mT", 2 * k))
                square(mem_n[:, 2 * k:2 * k + 2, :])
            for k in range(KT):
                wait_emptied(act, ("xT", k))
                square(x[:, k, :])
                if k == 1:
                    root(M)
            root()
            act.wait_ge(angle_ready, 1)
            eng.activation(sin[ropes, :], sin[ropes, :], ACT.Sin).then_inc(sin_ready, 1)
            eng.activation(cos[ropes, :], cos[ropes, :], ACT.Sin).then_inc(sin_ready, 1)
            for l in range(DEPTH):
                for c in range(2):
                    empty(("km", l, c), km[:, l, c, :], part=(slice(0, P), slice(0, M)))
                for b in range(2):
                    empty(("vm", l, b), vm[:, l, b, :], part=(slice(0, P), slice(0, M)))
            for t in range(5):
                dst = cq[:, t, :] if t < 3 else ckv[:, t - 3, :]
                empty(("cq", t), dst)
            empty(("kr",), kr[ropes, :], part=(ropes, slice(0, S)))
            for t in range(2):
                empty(("in_a.qm", t), qm[:, t, :])
            for t in range(5):
                wait_emptied(act, ("cq", t))
                square(cq[:, t, :] if t < 3 else ckv[:, t - 3, :])
                if t == 2:
                    root()
            root()
            for t in range(KT):
                empty(("in_a.gate", t), gate[:, t, :], ACT.Silu)
            for h in range(HEADS):
                empty(("q", h), qf[0:96, h, :], part=(slice(0, 96), slice(0, S)))
            for h in range(0, HEADS, 2):
                b = take(act, ("k", h), "act")
                eng.activation(kf[0:NOPE, h, :], b[0:NOPE, :], ACT.Copy)
                eng.activation(kf[0:NOPE, h + 1, :], b[NOPE:P, :], ACT.Copy).then_inc(emptied["act"], 1)
            for c in range(2):
                for blk in range(NB):
                    empty(("v", c, blk), v1[:, blk, 384 * c:384 * (c + 1)], part=(slice(0, P), slice(0, 384)))

            def attention(l):
                for h in range(16 + 1):
                    if h < 16:
                        par = h % 2
                        for i in range(NB):
                            n = (i + 1) * P if h < HEADS else M
                            po = P * (i * (i + 1) // 2) if h < HEADS else i * M
                            scale = (MLA_SCALE, 1.0)[l] if h < HEADS else HD ** -0.5
                            b = take(act, ("s", l, h, i), "act")
                            act.wait_ge(nmx_ready, (l * 16 + h) * NB + i + 1)
                            if h >= 2:
                                peek(act, ("t", l, h - 2, NB - 1))
                            eng.activation(probs[:, par, po:po + n], b[:, 0:n], ACT.Exp, bias=nmx[:, par, i:i + 1],
                                           scale=scale, accum_out=rsum[:, par, i:i + 1]).then_inc(emptied["act"], 1)
                    if h >= 1:
                        transposed(eng, act, l, h - 1, 0, "act")

            attention(0)

            def out_first(l):
                stage = ("out_a", "out_b")[l]
                for t in range(KT):
                    b = take(act, (stage, t), "act")
                    square(b[:, :])
                    eng.activation(o1[:, t, :], b[:, :], ACT.Copy).then_inc(emptied["act"], 1)
                root()
                for t in range(KT):
                    act.wait_ge(x_ready, l * KT + t + 1)
                    square(x[:, t, :])
                root()

            out_first(0)

            def log_of(z, rows, sem_out):
                chain.link(eng.activation(rows, z, ACT.Abs))
                chain.link(eng.activation(rows, rows, ACT.Exp, scale=-1.0))
                eng.activation(rows, rows, ACT.Ln, bias=1.0).then_inc(sem_out, 1)

            act.wait_ge(loaded_p, 48)
            empty(("f",), frow[0:HEADS, 0, :], ACT.Identity, part=(slice(0, HEADS), slice(0, S)), bias=bf[0:HEADS, 0:1])
            wait_emptied(act, ("f",))
            log_of(frow[0:HEADS, 0, :], frow[0:HEADS, 1, :], f_log)
            for t in range(6):
                b = take(act, ("in_b.q", t), "act")
                eng.activation(qf[0:HD, 2 * t, :], b[0:HD, :], ACT.Copy, scale=HD ** -0.5)
                eng.activation(qf[0:HD, 2 * t + 1, :], b[HD:P, :], ACT.Copy, scale=HD ** -0.5
                               ).then_inc(emptied["act"], 1)
            for t in range(6):
                b = take(act, ("in_b.k", t), "act")
                eng.activation(kf[0:HD, 2 * t, :], b[0:HD, :], ACT.Copy)
                eng.activation(kf[0:HD, 2 * t + 1, :], b[HD:P, :], ACT.Copy).then_inc(emptied["act"], 1)
            half_bank = (slice(0, P), slice(0, CHUNK))
            for s in range(3):
                for b in range(NB):
                    empty(("in_b.v", s, b), v1[:, b, CHUNK * s:CHUNK * (s + 1)], part=half_bank)
            for t in range(2):
                empty(("in_b.qm", t), qm[:, t, :])
            for t in range(KT):
                empty(("in_b.gate", t), gate[:, t, :], ACT.Silu)
            attention(1)
            out_first(1)
            act.wait_ge(mod_ready, 4)

            def shift(l, part, base):
                for t in range(KT):
                    act.wait_ge(scaled, base + t + 1)
                    col = 48 * l + 8 * part + t
                    eng.activation(hn[:, t, :], hn[:, t, :], ACT.Identity, bias=mod[:, col:col + 1]
                                   ).then_inc(hn_ready, 1)

            shift(0, 0, 0)
            act.wait_ge(lb_diff, 1)
            eng.activation(lbt[:, 1, :], lbt[:, 0, :], ACT.Exp).then_inc(lb_exp, 1)
            for t in range(4):
                empty(("even.qa", t), hq[:, t, :])
            for t in range(4):
                b = take(act, ("even.fa", t), "act")
                eng.activation(pf[:, t, :], b[:, :], ACT.Sigmoid)
                eng.activation(hk[:, t, :], b[:, :], ACT.Sigmoid, scale=-1.0).then_inc(emptied["act"], 1)
            for s in range(2):
                for b in range(NB):
                    empty(("even.ia", s, b), va[:, b, CHUNK * s:CHUNK * (s + 1)], part=half_bank)
            for t in range(4):
                empty(("even.ga", t), y2[:, t, :], ACT.Silu)
            for t in range(4):
                empty(("even.qb", t), qb[:, t, :], scale=float(P) ** -0.5)
            for t in range(4):
                empty(("even.kb", t), kb[:, t, :])
            for s in range(2):
                for b in range(NB):
                    empty(("even.vb", s, b), vb[:, b, CHUNK * s:CHUNK * (s + 1)], part=half_bank)
            for h in range(HG_HEADS):
                b = take(act, ("ho", h), "act")
                eng.activation(pf[:, h, :], b[:, :], ACT.Square).then_inc(sq_heads, 1)
                eng.activation(pb[:, h, :], b[:, :], ACT.Copy).then_inc(emptied["act"], 1)
            for h in range(HG_HEADS):
                act.wait_ge(head_inv, h + 1)
                eng.activation(hx[0][:, h, :], hx[0][:, h, :], ACT.Sqrt).then_inc(rstd_heads, 1)
            for h in range(5):
                if h < 4:
                    if h >= 1:
                        act.wait_ge(soft_ready, h)
                    for j in range(3):
                        b = peek(act, ("z", h, j))
                        n = S if j == 0 else 384
                        chain.step(eng.activation(lnb[:, OFF[j]:OFF[j] + n], b[:, 0:n], ACT.Abs))
                    chain.settle()
                    chain.link(eng.activation(lnb, lnb, ACT.Exp, scale=-1.0))
                    eng.activation(lnb, lnb, ACT.Ln, bias=1.0).then_inc(soft_log, 1)
                    act.wait_ge(stick_sums, h + 1)
                    if h >= 2:
                        peek(act, ("so", h - 2))
                    for j in range(3):
                        n = S if j == 0 else 384
                        empty(("z", h, j), stick[h % 2][:, OFF[j]:OFF[j] + n], ACT.Exp,
                              part=(slice(0, P), slice(0, n)))
                if h >= 1:
                    empty(("so", h - 1), y2[:, 4 + h - 1, :])

            def out_second(stage):
                for t in range(KT):
                    wait_emptied(act, (stage, t))
                    square(x[:, t, :])
                root()

            out_second("even_out")
            shift(0, 3, KT)

            def ffn(l):
                for t in range(FT):
                    i = l * FT + t
                    if i >= 2:
                        act.wait_ge(conv_ready, i - 1)
                    empty(("fa", l, t), a_raw[t % 2][:, 2:2 + S])
                    if t >= 1:
                        gelu(l, t - 1)
                gelu(l, FT - 1)
                out_second(f"ffn{l}.out")

            def gelu(l, t):
                act.wait_ge(conv_ready, l * FT + t + 1)
                if t >= 2:
                    wait_emptied(act, ("fg", l, t - 2))
                eng.activation(gel[t % 2], conv[t % 2], ACT.Gelu_apprx_tanh).then_inc(gelu_ready, 1)

            ffn(0)
            shift(1, 0, 2 * KT)
            empty(("og_rows",), grow[0:16, 0, :], ACT.Identity, part=(slice(0, 16), slice(0, S)), bias=bf[0:16, 1:2])
            act.wait_ge(gates_moved, 16)
            log_of(grow[0:8, 1, :], grow[0:8, 2, :], g_log)
            for t in range(KT):
                empty(("odd.qk", t), qk_raw[:, t, 3:3 + S])
            act.wait_ge(m_ready, 1)
            eng.activation(grow[0:8, 7, :], grow[0:8, 6, :], ACT.Exp, scale=-1.0).then_inc(floor_rows, 1)
            for s in range(4):
                for b in range(NB):
                    empty(("odd.v", s, b), vo[:, b, CHUNK * s:CHUNK * (s + 1)], part=half_bank)
            for t in range(KT):
                act.wait_ge(qk_conv, t + 1)
                eng.activation(qkc[:, t, :], qkc[:, t, :], ACT.Silu).then_inc(qk_silu, 1)
            for t in range(KT):
                empty(("odd.og", t), og[:, t, :], ACT.Sigmoid)
            wait_emptied(act, ("gcol",))
            for h in range(ML_HEADS):
                b = take(act, ("mb", h), "act")
                if h >= 2:
                    peek(act, ("num", h - 2))
                for j in range(NB):
                    ins = eng.activation(dec[h % 2][:, OFF[j]:OFF[j] + WIDE[j]], b[:, j * P:S], ACT.Relu,
                                         bias=ngcol[:, j, h:h + 1])
                ins.then_inc(emptied["act"], 1)
                wait_emptied(act, ("mb", h))
                eng.activation(dec[h % 2], dec[h % 2], ACT.Exp, scale=-1.0).then_inc(dec_exp, 1)
                if h >= 2:
                    wait_emptied(act, ("den", h - 2))
                empty(("eb", h), floor_b[h % 2])
                if h >= 1:
                    wait_emptied(act, ("num", h - 1))
                    eng.activation(hsq[:, h - 1, :], ho[:, h - 1, :], ACT.Square).then_inc(sq_heads, 1)
            wait_emptied(act, ("num", ML_HEADS - 1))
            eng.activation(hsq[:, 7, :], ho[:, 7, :], ACT.Square).then_inc(sq_heads, 1)
            for h in range(ML_HEADS):
                act.wait_ge(head_inv, HG_HEADS + h + 1)
                eng.activation(qkc[:, h, :], qkc[:, h, :], ACT.Sqrt).then_inc(rstd_heads, 1)
            out_second("odd_out")
            shift(1, 3, 3 * KT)
            ffn(1)

        @block.vector
        def _(eng):
            dve = Engine(eng)
            chain = Chain(eng, dve_step)
            used = {"sq": 0, "norm": 0, "ada": 0}
            ada_at = [n for n, c in enumerate(plan) if c[0] == "ada"]

            def ada_steps(count):
                for _ in range(count):
                    j = used["ada"]
                    n = ada_at[j]
                    w = ring[:, n % RING, :].rearrange("p (t n) -> p t n", t=KT)
                    dve.wait_ge(cs_ready, 1)
                    dve.wait_ge(landed[n % RING], landing[n])
                    if j >= ACC:
                        dve.wait_ge(ada_summed, j - ACC + 1)
                    s = acc[:, j % ACC, :]
                    chain.link(eng.tensor_scalar(s, w[:, 0, :], cs[:, 0:1], None, ALU.mult))
                    for k in range(1, KT):
                        ins = eng.scalar_tensor_tensor(out=s, in0=w[:, k, :], scalar=cs[:, k:k + 1], in1=s,
                                                       op0=ALU.mult, op1=ALU.add)
                        if k < KT - 1:
                            chain.link(ins)
                        else:
                            ins.then_inc(ada_done, 1)
                    used["ada"] += 1

            def inverse(count, width, n=S):
                k = used["norm"]
                used["sq"] += count
                dve.wait_ge(sq_used, used["sq"])
                dve.wait_ge(rstd_ready, k)
                eng.tensor_scalar(var[:, 0:n], ssq_bank[:, 0:n], 1.0 / width, EPS, ALU.mult, ALU.add
                                  ).then_inc(ssq_taken, 1)
                dve.wait_ge(ssq_taken, k + 1)
                eng.reciprocal(var[:, 0:n], var[:, 0:n]).then_inc(var_ready, 1)
                used["norm"] += 1

            def normed(count, width, src, dst, gains, n=S):
                inverse(count, width, n)
                dve.wait_ge(rstd_ready, used["norm"])
                for t, g in enumerate(gains):
                    eng.scalar_tensor_tensor(out=dst[:, t, 0:n], in0=src[:, t, 0:n], scalar=g, in1=rstd[:, 0:n],
                                             op0=ALU.mult, op1=ALU.mult).then_inc(hn_ready, 1)

            def empty(key, out, part=None):
                b = take(dve, key, "dve")
                eng.tensor_copy(out, b[:, :] if part is None else b[part]).then_inc(emptied["dve"], 1)

            for n in range(VEC_TILES):
                rows = max(r + k for t, r, k in VEC_ROWS.values() if t == n)
                empty(("vec", n), vecs[:, n * P:n * P + rows], (slice(0, P), slice(0, rows)))
            wait_emptied(dve, ("vec", VEC_TILES - 1))
            dve.wait_ge(loaded_c, 32)
            eng.tensor_copy(masks[:, :], masks_f[:, 0:(len(HG_LEVELS) + 1) * P]).then_inc(const_ready, 1)
            eng.tensor_copy(not_before[:, :], masks_f[:, (len(HG_LEVELS) + 1) * P:]).then_inc(const_ready, 1)
            eng.tensor_copy(identb[:, :], ident).then_inc(const_ready, 1)
            eng.tensor_copy(causal[:, :], consts[:, C_CAUSAL:C_CAUSAL + P]).then_inc(const_ready, 1)
            for k in range(0, KT, 2):
                empty(("mT", k), mem_n[:, k:k + 2, :].rearrange("p k m -> p (k m)"))
            for k in range(KT):
                empty(("xT", k), x[:, k, :])
            normed(4, D, mem_n, mem_n, [vec("mem_norm", t) for t in range(KT)], M)
            normed(KT, D, x, hn, [vec("norm_pre", t) for t in range(KT)])
            dve.wait_ge(loaded_p, 48)
            pr = posf[ropes, :]
            tr = turn[ropes, :]
            sr, cr = sin[ropes, :], cos[ropes, :]
            chain.link(eng.tensor_copy(pr, pos_i.bitcast(I32)[ropes, :]))
            chain.link(eng.tensor_scalar(pr, pr, freq, None, ALU.mult))
            magic = 12582912.0
            chain.link(eng.tensor_scalar(tr, pr, float(1 / (2 * np.pi)), magic, ALU.mult, ALU.add))
            chain.link(eng.tensor_scalar(tr, tr, magic, None, ALU.subtract))
            rest = 2 * np.pi - 6.28125
            mid = float(np.float32(np.round(rest * 2 ** 20) / 2 ** 20))
            chain.link(eng.scalar_tensor_tensor(out=sr, in0=tr, scalar=-6.28125, in1=pr, op0=ALU.mult, op1=ALU.add))
            chain.link(eng.scalar_tensor_tensor(out=sr, in0=tr, scalar=-mid, in1=sr, op0=ALU.mult, op1=ALU.add))
            chain.link(eng.scalar_tensor_tensor(out=sr, in0=tr, scalar=-float(rest - mid), in1=sr, op0=ALU.mult,
                                                op1=ALU.add))
            lim = 3.1415925
            chain.link(eng.tensor_scalar(cr, sr, float(np.pi / 2), None, ALU.add))
            chain.link(eng.tensor_scalar(tr, cr, float(np.pi), 2 * float(np.pi), ALU.is_gt, ALU.mult))
            chain.link(eng.tensor_tensor(cr, cr, tr, ALU.subtract))
            eng.tensor_scalar(cr, cr, lim, -lim, ALU.min, ALU.max)
            eng.tensor_scalar(sr, sr, lim, -lim, ALU.min, ALU.max).then_inc(angle_ready, 1)
            ada_steps(6 + 6)
            normed(3, Q_LORA, cq, cq, [vec("q_norm_a", t) for t in range(3)])
            normed(2, KV_LORA, ckv, ckv, [vec("kv_norm_a", t) for t in range(2)])
            ada_steps(6)

            def rotate(key, dst, par):
                b = take(dve, key, "dve")
                dve.wait_ge(sin_ready, 2)
                eng.tensor_tensor(rt[ropes, par, :], b[ropes, :], sr, ALU.mult).then_inc(emptied["dve"], 1)
                chain.link(eng.tensor_tensor(rt[ropes, 2 + par, :], dst, cr, ALU.mult))
                wait_emptied(dve, key)
                return eng.tensor_tensor(dst, rt[ropes, par, :], rt[ropes, 2 + par, :], ALU.add)

            rotate(("krot",), kr[ropes, :], 1).then_inc(kr_ready, 1)
            for h in range(HEADS):
                if h == 1:
                    dve.wait_ge(kr_ready, 1)
                if h >= 2:
                    dve.wait_ge(rope_done, h - 1)
                rotate(("qrot", h), qf[ropes, h, :], h % 2).then_inc(rope_done, 1)

            def attention(l):
                for h in range(16 + 1):
                    par = h % 2
                    if h < 16:
                        for i in range(NB):
                            n = (i + 1) * P if h < HEADS else M
                            scale = (MLA_SCALE, 1.0)[l] if h < HEADS else HD ** -0.5
                            b = peek(dve, ("s", l, h, i))
                            chain.link(eng.reduce_max(mx[:, par, i:i + 1], b[:, 0:n], AX_X))
                            eng.tensor_scalar(nmx[:, par, i:i + 1], mx[:, par, i:i + 1], -scale, None, ALU.mult
                                              ).then_inc(nmx_ready, 1)
                    if h >= 1:
                        transposed(eng, dve, l, h - 1, 1, "dve")
                    if h < 16:
                        wait_emptied(dve, ("s", l, h, NB - 1))
                        eng.reciprocal(rinv[:, par, :], rsum[:, par, :]).then_inc(rinv_ready, 1)
                    if h >= 1:
                        g = h - 1
                        b = take(dve, ("o", l, g), "dve")
                        rows = slice(HD * (g % 2), HD * (g % 2) + HD)
                        wait_emptied(dve, (("in_a.gate", "in_b.gate")[l], KT - 1))
                        ins = eng.tensor_tensor(gate[rows, g // 2, :], b[rows, :], gate[rows, g // 2, :], ALU.mult)
                        ins.then_inc(emptied["dve"], 1)

            attention(0)

            def out_first(l):
                ada_steps(6)
                inverse(KT, D)
                dve.wait_ge(rstd_ready, used["norm"])
                for t in range(KT):
                    eng.scalar_tensor_tensor(out=o1[:, t, :], in0=o1[:, t, :], scalar=vec("norm_post", KT * l + t),
                                             in1=rstd[:, :], op0=ALU.mult, op1=ALU.mult).then_inc(post_scaled, 1)

            out_first(0)
            normed(KT, D, x, hn, [vec("norm_pre", KT + t) for t in range(KT)])

            def log_sigmoid(z, t, lf, s_log):
                dve.wait_ge(s_log, 1)
                chain.link(eng.scalar_tensor_tensor(out=lf, in0=z, scalar=0.0, in1=t, op0=ALU.min, op1=ALU.subtract))

            ada_steps(2)
            wait_emptied(dve, ("f",))
            fr = [frow[0:HEADS, n, :] for n in range(6)]
            log_sigmoid(fr[0], fr[1], fr[2], f_log)
            chain.link(eng.memset(fr[5], 1.0))
            chain.link(eng.tensor_tensor_scan(fr[3], fr[5], fr[2], 0.0, ALU.mult, ALU.add))
            eng.tensor_scalar(fr[4], fr[3], -1.0, None, ALU.mult).then_inc(frows_ready, 1)
            ada_steps(16)
            attention(1)
            out_first(1)
            dve.wait_ge(ada_summed, 48)
            chain.link(eng.tensor_tensor(mod[:, :], mod_bank[:, 0:96], vecs[:, P:P + 96], ALU.add))
            for j, (l, part, name) in enumerate([(0, 1, "norm_mix_g_2"), (0, 4, "norm_ffn_g_2"),
                                                 (1, 1, "norm_mix_g_2"), (1, 4, "norm_ffn_g_2")]):
                tile, row, _ = VEC_ROWS[name]
                g = vecs[:, tile * P + row + 8 * l:tile * P + row + 8 * l + 8]
                c = 48 * l + 8 * part
                eng.scalar_tensor_tensor(out=gmod[:, j, :], in0=mod[:, c:c + 8], scalar=1.0, in1=g,
                                         op0=ALU.add, op1=ALU.mult).then_inc(mod_ready, 1)
            dve.wait_ge(mod_ready, 4)

            def modulated(j):
                inverse(KT, D)
                dve.wait_ge(rstd_ready, used["norm"])
                for t in range(KT):
                    eng.scalar_tensor_tensor(out=hn[:, t, :], in0=x[:, t, :], scalar=gmod[:, j, t:t + 1],
                                             in1=rstd[:, :], op0=ALU.mult, op1=ALU.mult).then_inc(scaled, 1)

            modulated(0)
            tile, row, _ = VEC_ROWS["hgrn_lb_2"]
            lb_in = vecs[:, tile * P + row:tile * P + row + 4]
            eng.tensor_tensor(lbt[:, 0, :], lb_in, lb_in, ALU.subtract).then_inc(lb_diff, 1)
            dve.wait_ge(lb_exp, 1)
            chain.link(eng.reciprocal(lbt[:, 2, :], lbt[:, 1, :]))
            chain.link(eng.tensor_tensor(lbt[:, 2, :], lbt[:, 1, :], lbt[:, 2, :], ALU.mult))
            chain.link(eng.tensor_tensor(lbt[:, 2, :], lbt[:, 2, :], lbt[:, 2, :], ALU.subtract))
            eng.tensor_scalar(lbt[:, 3, :], lbt[:, 2, :], -1.0, 1.0, ALU.mult, ALU.add).then_inc(lb_ready, 1)

            def masked(key, n, last=None):
                for h in range(HG_HEADS):
                    if last is not None:
                        wait_emptied(dve, last + (h,))
                    b = take(dve, key + (h,), "dve")
                    mk = masks[:, n * P:(n + 1) * P].unsqueeze(1).to_broadcast([P, NB, P])
                    eng.copy_predicated(at_d[:, h, :].rearrange("p (b t) -> p b t", b=NB), mk,
                                        b[:, :].rearrange("p (b t) -> p b t", b=NB)).then_inc(emptied["dve"], 1)

            def halves(v, half):
                u = v.rearrange("p h (n two m) -> p (h n) two m", two=2, m=half)
                return u[:, :, 0, :], u[:, :, 1, :]

            def level(n):
                half = 1 << n
                X = hx[n % 2]
                xl, xr = halves(X, half)
                kl, _ = halves(hk, half)
                _, qr = halves(hq, half)
                pbl, _ = halves(pb, half)
                _, pfr = halves(pf, half)
                dve.wait_ge(levels_up, n)
                if n >= 2:
                    peek(dve, ("lv", n - 2, HG_HEADS - 1))
                chain.step(eng.tensor_tensor(xl, kl, pbl, ALU.mult))
                eng.tensor_tensor(xr, qr, pfr, ALU.mult).then_inc(hx_ready, 1)

            dve.wait_ge(hg_ready, HG_HEADS)
            dve.wait_ge(hg_set, 2)
            wait_emptied(dve, ("even.qa", 3))
            level(0)
            masked(("diag",), 0)
            for n in range(len(HG_LEVELS)):
                level(n + 1)
                masked(("lv", n), n + 1, ("lv", n - 1) if n else ("diag",))
            n = len(HG_LEVELS)
            level(n + 1)
            for h in range(HG_HEADS):
                empty(("lv", n, h), at_1[:, h, :], (slice(0, P), slice(0, 256)))
            for h in range(HG_HEADS):
                empty(("lv", n + 1, h), at_2[:, h, :])

            def head_norms(key, base, count, src, rs, name, g0, gated):
                for h in range(count):
                    b = take(dve, (key, h), "dve")
                    eng.tensor_scalar(rs[:, h, :], b[:, :], 1.0 / P, EPS, ALU.mult, ALU.add
                                      ).then_inc(emptied["dve"], 1)
                    wait_emptied(dve, (key, h))
                    eng.reciprocal(rs[:, h, :], rs[:, h, :]).then_inc(head_inv, 1)
                for h in range(count):
                    dve.wait_ge(rstd_heads, base + h + 1)
                    chain.link(eng.scalar_tensor_tensor(out=src[:, h, :], in0=src[:, h, :], scalar=vec(name, h),
                                                        in1=rs[:, h, :], op0=ALU.mult, op1=ALU.mult))
                    eng.tensor_tensor(gated[:, h, :], gated[:, h, :], src[:, h, :], ALU.mult).then_inc(y_heads, 1)

            for h in range(HG_HEADS):
                wait_emptied(dve, ("ho", h))
            head_norms("hs", 0, HG_HEADS, pb, hx[0], "hgrn_norm_g_2", 0, y2)
            for h in range(4):
                dve.wait_ge(soft_log, h + 1)
                if h >= 2:
                    dve.wait_ge(stick_sums, h - 1)
                for j in range(3):
                    b = peek(dve, ("z", h, j))
                    n = S if j == 0 else 384
                    c = slice(OFF[j], OFF[j] + n)
                    ins = eng.scalar_tensor_tensor(out=soft[h % 2][:, c], in0=b[:, 0:n], scalar=0.0, in1=lnb[:, c],
                                                   op0=ALU.max, op1=ALU.add)
                ins.then_inc(soft_ready, 1)

            def out_second(stage, l, part):
                for t in range(KT):
                    b = take(dve, (stage, t), "dve")
                    col = 48 * l + 8 * part + t
                    eng.scalar_tensor_tensor(out=x[:, t, :], in0=b[:, :], scalar=mod[:, col:col + 1],
                                             in1=x[:, t, :], op0=ALU.mult, op1=ALU.add).then_inc(emptied["dve"], 1)

            out_second("even_out", 0, 2)
            modulated(1)

            def ffn(l):
                name = f"ffn_conv_w_2/{l}"
                for t in range(FT + 1):
                    if t < FT:
                        i = l * FT + t
                        dve.wait_ge(pads, l + 1)
                        wait_emptied(dve, ("fa", l, t))
                        if i >= 2:
                            dve.wait_ge(gelu_ready, i - 1)
                        r, u = a_raw[t % 2], conv[t % 2]
                        chain.link(eng.tensor_scalar(u, r[:, 0:S], vec(name, t), vec("ffn_conv_b_2", FT * l + t),
                                                     ALU.mult, ALU.add))
                        chain.link(eng.scalar_tensor_tensor(out=u, in0=r[:, 1:1 + S], scalar=vec(name, FT + t),
                                                            in1=u, op0=ALU.mult, op1=ALU.add))
                        eng.scalar_tensor_tensor(out=u, in0=r[:, 2:2 + S], scalar=vec(name, 2 * FT + t), in1=u,
                                                 op0=ALU.mult, op1=ALU.add).then_inc(conv_ready, 1)
                    if t >= 1:
                        g = t - 1
                        b = take(dve, ("fg", l, g), "dve")
                        dve.wait_ge(gelu_ready, l * FT + g + 1)
                        eng.tensor_tensor(hact[:, g, :], b[:, :], gel[g % 2], ALU.mult).then_inc(emptied["dve"], 1)
                out_second(f"ffn{l}.out", l, 5)

            ffn(0)
            modulated(2)
            gr = [grow[0:8, n, :] for n in range(8)]
            dve.wait_ge(gates_moved, 16)
            log_sigmoid(gr[1], gr[2], gr[3], g_log)
            chain.link(eng.memset(gr[2], 1.0))
            chain.link(eng.tensor_tensor_scan(gr[6], gr[2], gr[3], 0.0, ALU.mult, ALU.add))
            eng.tensor_tensor(gr[4], gr[0], gr[6], ALU.subtract).then_inc(grows_ready, 1)
            dve.wait_ge(grows_ready, 1)
            chain.link(eng.tensor_tensor_scan(gr[5], gr[2], gr[4], 0.0, ALU.mult, ALU.max))
            eng.tensor_tensor(gr[6], gr[6], gr[5], ALU.add).then_inc(m_ready, 1)
            def wcol(k, t):
                return vec("odd_conv_w_2", KT * k + t)

            dve.wait_ge(qk_pads, 1)
            for t in range(KT):
                wait_emptied(dve, ("odd.qk", t))
                u = qkc[:, t, :]
                chain.link(eng.tensor_scalar(u, qk_raw[:, t, 0:S], wcol(0, t), vec("odd_conv_b_2", t),
                                             ALU.mult, ALU.add))
                for k in range(1, 4):
                    ins = eng.scalar_tensor_tensor(out=u, in0=qk_raw[:, t, k:k + S], scalar=wcol(k, t), in1=u,
                                                   op0=ALU.mult, op1=ALU.add)
                    if k < 3:
                        chain.link(ins)
                    else:
                        ins.then_inc(qk_conv, 1)
            b = take(dve, ("gcol",), "dve")
            eng.tensor_scalar(ngcol.rearrange("p a b -> p (a b)"), b[:, 0:NB * ML_HEADS], -1.0, None, ALU.mult
                              ).then_inc(emptied["dve"], 1)
            for h in range(ML_HEADS + 1):
                if h < ML_HEADS:
                    dve.wait_ge(dec_masked, h + 1)
                    W = dec[h % 2]
                    for j in range(3):
                        b = take(dve, ("qk", h, j), "dve")
                        n = S if j == 0 else 384
                        c = slice(OFF[j], OFF[j] + n)
                        eng.scalar_tensor_tensor(out=W[:, c], in0=b[:, 0:n], scalar=64.0 ** -0.5, in1=W[:, c],
                                                 op0=ALU.mult, op1=ALU.mult).then_inc(emptied["dve"], 1)
                if h >= 1:
                    g = h - 1
                    b = take(dve, ("den", g), "dve")
                    wait_emptied(dve, ("eb", g))
                    chain.link(eng.tensor_tensor(den, b[:, :], floor_b[g % 2], ALU.max))
                    eng.scalar_tensor_tensor(out=den, in0=b[:, :], scalar=-1.0, in1=den, op0=ALU.mult, op1=ALU.max
                                             ).then_inc(emptied["dve"], 1)
                    wait_emptied(dve, ("den", g))
                    if g >= 1:
                        wait_emptied(dve, ("num", g - 1))
                    chain.link(eng.reciprocal(deni, den))
                    b = take(dve, ("num", g), "dve")
                    eng.tensor_tensor(ho[:, g, :], b[:, :], deni, ALU.mult).then_inc(emptied["dve"], 1)
            head_norms("ms", HG_HEADS, ML_HEADS, ho, qkc, "odd_norm_g_2", 0, og)
            out_second("odd_out", 1, 2)
            modulated(3)
            ffn(1)
            normed(KT, D, x, hn, [vec("final_g_2", t) for t in range(KT)])
            for j in range(NB):
                for half in range(2):
                    empty(("out", j, half), out_tok[:, j, half * S:(half + 1) * S])

        @block.gpsimd
        def _(eng):
            pool = Engine(eng)
            pool.wait_ge(kr_ready, 1)
            eng.tensor_copy(kf[ropes, :, :], kr[ropes, :].unsqueeze(1).to_broadcast([ROPE, HEADS, S])
                            ).then_inc(kf_ready, 1)

            def attention(l):
                for h in range(16):
                    par = h % 2
                    pool.wait_ge(rinv_ready, l * 16 + h + 1)
                    for i in range(NB):
                        n = (i + 1) * P if h < HEADS else M
                        po = P * (i * (i + 1) // 2) if h < HEADS else i * M
                        w = probs[:, par, po:po + n]
                        eng.tensor_scalar(w, w, rinv[:, par, i:i + 1], None, ALU.mult).then_inc(probs_ready, 1)

            def add_x(l):
                for t in range(KT):
                    pool.wait_ge(post_scaled, l * KT + t + 1)
                    eng.tensor_tensor(x[:, t, :], x[:, t, :], o1[:, t, :], ALU.add).then_inc(x_ready, 1)

            attention(0)
            add_x(0)
            pool.wait_ge(hn_ready, 29)
            eng.memset(qf[HD:HD + 2, :, :], 1.0).then_inc(frows_set, 1)
            eng.memset(kf[HD:HD + 2, :, :], 1.0).then_inc(frows_set, 1)
            pool.wait_ge(frows_set, 2)
            pool.wait_ge(frows_ready, 1)
            for h in range(HEADS):
                eng.dma_start(qf[HD:HD + 1, h, :], frow[h:h + 1, 3, :]).then_inc(frows_moved, 16)
                eng.dma_start(kf[HD + 1:HD + 2, h, :], frow[h:h + 1, 4, :]).then_inc(frows_moved, 16)
            attention(1)
            add_x(1)
            pool.wait_ge(lb_ready, 1)
            pool.wait_ge(hn_ready, 37)
            eng.memset(pb[:, :, :], 1.0).then_inc(hg_set, 1)
            eng.memset(at_d[:, :, :], 0.0).then_inc(hg_set, 1)
            for h in range(HG_HEADS):
                wait_emptied(pool, ("even.fa", h))
                eng.tensor_scalar(pf[:, h, :], pf[:, h, :], lbt[:, 3, h:h + 1], lbt[:, 2, h:h + 1], ALU.mult, ALU.add)
                eng.tensor_scalar(hk[:, h, :], hk[:, h, :], lbt[:, 3, h:h + 1], None, ALU.mult).then_inc(hg_ready, 1)
            pool.wait_ge(hg_ready, HG_HEADS)
            pool.wait_ge(hg_set, 2)
            for n in range(8):
                half = 1 << n
                u = pf.rearrange("p h (n two m) -> p (h n) two m", two=2, m=half)
                v = pb.rearrange("p h (n two m) -> p (h n) two m", two=2, m=half)
                pool.wait_ge(hx_ready, n + 1)
                shape = [P, HG_HEADS * S // (2 * half), half]
                chain_n = 2 * n
                eng.tensor_tensor(v[:, :, 0, :], v[:, :, 0, :], u[:, :, 1, half - 1:half].to_broadcast(shape),
                                  ALU.mult).then_inc(pool_step, 1)
                pool.wait_ge(pool_step, n + 1)
                eng.tensor_tensor(u[:, :, 1, :], u[:, :, 1, :], u[:, :, 0, half - 1:half].to_broadcast(shape),
                                  ALU.mult).then_inc(levels_up, 1)
                pool.wait_ge(levels_up, n + 1)

            def triangle(v, op, last):
                for j in range(NB):
                    d = v[:, OFF[j]:OFF[j] + P]
                    ins = eng.affine_select(out=d, in_=d, compare_op=op, fill=0.0, base=0, pattern=[[1, P]],
                                            channel_multiplier=-1)
                ins.then_inc(last, 1)

            for h in range(4):
                pool.wait_ge(soft_ready, h + 1)
                triangle(soft[h % 2], ALU.is_gt, soft_masked)
            pool.wait_ge(hn_ready, 45)
            for n in range(2):
                ins = eng.memset(a_raw[n][:, 0:2], 0.0)
            ins.then_inc(pads, 1)
            pool.wait_ge(hn_ready, 53)
            eng.memset(qk_raw[:, :, 0:3], 0.0).then_inc(qk_pads, 1)
            wait_emptied(pool, ("og_rows",))
            eng.dma_start(grow[0:8, 1, :], grow[8:16, 0, :]).then_inc(gates_moved, 16)
            for h in range(ML_HEADS):
                pool.wait_ge(dec_exp, h + 1)
                triangle(dec[h % 2], ALU.is_ge, dec_masked)
            pool.wait_ge(hn_ready, 61)
            for n in range(2):
                ins = eng.memset(a_raw[n][:, 0:2], 0.0)
            ins.then_inc(pads, 1)


def kernel(**inputs):
    import concourse.bacc as bacc
    from concourse.bass_utils import run_bass_kernel_spmd as run

    arrays = {name: np.ascontiguousarray(v) for name, v in inputs.items()}
    arrays["const_f32"] = constants()
    nc = bacc.Bacc("TRN2", target_bir_lowering=False, num_devices=1)
    aps = {name: nc.dram_tensor(f"in_{name}", v.shape, mybir.dt.from_np(v.dtype), kind="ExternalInput").ap()
           for name, v in arrays.items()}
    out = nc.dram_tensor("out", (1, S, D), F32, kind="ExternalOutput").ap()
    two_block_kernel(nc, aps, out)
    r = run(nc, [{f"in_{name}": v for name, v in arrays.items()}], core_ids=[0])
    return r.results[0]["out"]
```

```python
from contextlib import ExitStack

import numpy as np

import concourse.bass as bass
from concourse import mybir

P = 128
S = 512
NB = S // P
D = 1024
KT = D // P
M = 256
DEPTH = 2
EPS = 1e-6
HEADS = 12
MEM_HEADS = 4
Q_LORA, KV_LORA, ROPE, NOPE = 384, 256, 32, 64
MLA_SCALE = float(NOPE + ROPE) ** -0.5
HD = 64
MAIN = HEADS * HD
FFN = 2816
FT = FFN // P
FFN_PARTS = [(0, 12), (12, 22)]
HG_HEADS = 4
ML_HEADS = 8
RING = 3
SPLIT = 2
CHUNK = 256
ROT = 6
ACC = 2

ALU = mybir.AluOpType
ACT = mybir.ActivationFunctionType
AX_X = mybir.AxisListType.X
F32 = mybir.dt.float32
BF16 = mybir.dt.bfloat16
F32R = mybir.dt.float32r
I32 = mybir.dt.int32
U8 = mybir.dt.uint8

WIDE = [S - P * j for j in range(NB)]
OFF = [0, 512, 896, 1152]
PACK = sum(WIDE)
TRI_BANK = [(0, 0), (1, 0), (2, 0), (2, 256)]

VEC_ROWS = {}
for _tile, _names in enumerate([
        [("c_2", 8), ("norm_pre", 16), ("norm_post", 16), ("mem_norm", 8), ("q_norm_a", 3), ("kv_norm_a", 2),
         ("norm_mix_g_2", 16), ("norm_ffn_g_2", 16), ("hgrn_norm_g_2", 4), ("odd_norm_g_2", 8), ("final_g_2", 8),
         ("odd_conv_b_2", 8), ("hgrn_lb_2", 4)],
        [("ada_b_2", 96), ("odd_conv_w_2", 32)],
        [("ffn_conv_b_2", 44), ("ffn_conv_w_2/0", 66)],
        [("ffn_conv_w_2/1", 66)]]):
    _at = 0
    for _n, _k in _names:
        VEC_ROWS[_n] = (_tile, _at, _k)
        _at += _k
VEC_TILES = 4

SPLIT_AT, _at = {}, 0
for _n, _k in [("mem", 8), ("x_a", 8), ("cq", 3), ("ckv", 2), ("y_a", 8), ("x_b", 8), ("y_b", 8), ("x_even", 8),
               ("y_even", 8), ("x_ffn0", 8), ("ffn0/0", 12), ("ffn0/1", 10), ("x_odd", 8), ("y_odd", 8),
               ("x_ffn1", 8), ("ffn1/0", 12), ("ffn1/1", 10)]:
    SPLIT_AT[_n] = _at
    _at += _k

C_ID, C_ONE, C_NINCL, C_NONE, C_CAUSAL, C_ROT, C_FREQ = 0, 128, 256, 384, 512, 640, 672
C_COLS = 673
HG_LEVELS = [1, 2, 4, 8, 16, 32, 64]


def constants():
    c = np.zeros((P, C_COLS), np.float32)
    i = np.arange(P)
    c[:, C_ID:C_ID + P] = np.eye(P)
    c[:, C_ONE:C_ONE + P] = 1.0
    c[:, C_NINCL:C_NINCL + P] = -(i[None, :] <= i[:, None]).astype(np.float32)
    c[:, C_NONE:C_NONE + P] = -1.0
    c[:, C_CAUSAL:C_CAUSAL + P] = np.where(i[None, :] <= i[:, None], 0.0, -1e30)
    half = ROPE // 2
    for r in range(half):
        c[NOPE + r + half, C_ROT + r] = -1.0
        c[NOPE + r, C_ROT + r + half] = 1.0
    freq = np.float32(10000.0) ** (-np.arange(half, dtype=np.float32) / np.float32(half))
    c[NOPE:NOPE + ROPE, C_FREQ] = np.concatenate([freq, freq])
    m = np.zeros((P, len(HG_LEVELS) + 1, P), np.float32)
    s, t = i[:, None], i[None, :]
    m[:, 0] = s == t
    for n, h in enumerate(HG_LEVELS):
        m[:, n + 1] = (s // (2 * h) == t // (2 * h)) & (s // h % 2 == 0) & (t // h % 2 == 1)
    before = np.where(t <= s, -1e30, 0.0).astype(np.float32)
    return np.concatenate([c, m.reshape(P, -1), before], axis=1)


def weight_plan(a):
    def k8(name, w, lo, hi):
        v = w.rearrange("(t p) n -> p t n", p=P)
        return [(name, v[:, :, c:min(c + CHUNK, hi)], KT, min(CHUNK, hi - c)) for c in range(lo, hi, CHUNK)]

    plan = []
    ada = [("ada", c[1], KT, CHUNK) for l in range(DEPTH) for c in k8("ada", a["ada_w_2"][l], 0, 6 * D)]

    def add(chunks, per=0):
        for n, c in enumerate(chunks):
            plan.append(c)
            for _ in range((n + 1) * per // len(chunks) - n * per // len(chunks)):
                plan.append(ada.pop(0))

    for l in range(DEPTH):
        add(k8(f"mem{l}", a["w_mem_kv"][l], 0, 512))
    w = a["w_in_a"][0]
    add(k8("in_a.cq", w, 0, 256) + k8("in_a.cq", w, 256, 512) + k8("in_a.kr", w, 512, 672)
        + k8("in_a.qm", w, 672, 928))
    add(k8("in_a.gate", w, 928, 1952), 5)
    q = a["w_q_up_a"][0].rearrange("(t p) n -> p t n", p=P)
    add([("q_up", q[:, :, n * 576:(n + 1) * 576], 3, 576) for n in range(2)])
    kv = a["w_kv_up_a"][0].rearrange("(t p) (h n) -> p t h n", p=P, n=NOPE + HD)
    add([("kv_up", kv[:, :, :, 0:NOPE], 2, MAIN), ("kv_up", kv[:, :, :, NOPE:NOPE + HD], 2, MAIN)])
    add(k8("out_a", a["w_out"][0], 0, D), 3)
    w = a["w_in_b"][0]
    add(k8("in_b.f", w, 3 * MAIN, 3 * MAIN + P) + k8("in_b.v", w, 2 * MAIN, 3 * MAIN)
        + k8("in_b.qm", w, 2316, 2572) + k8("in_b.gate", w, 2572, 3596) + k8("in_b.q", w, 0, MAIN)
        + k8("in_b.k", w, MAIN, 2 * MAIN), 13)
    add(k8("out_b", a["w_out"][1], 0, D), 3)
    w = a["even_w_in_2"][0]
    for name, lo in (("qa", 0), ("fa", 512), ("ia", 1024), ("ga", 1536), ("qb", 2048), ("kb", 2560), ("vb", 3072)):
        add(k8("even." + name, w, lo, lo + 512), 2)
    add(k8("even_out", a["even_w_out_2"][0], 0, D))

    def ffn(l):
        w = a["ffn_w_in_2"][l]
        v = a["ffn_w_out_2"][l].rearrange("(t p) n -> p t n", p=P)
        for lo, hi in FFN_PARTS:
            for x, g in zip(k8(f"ffn{l}.a", w, lo * P, hi * P), k8(f"ffn{l}.g", w, FFN + lo * P, FFN + hi * P)):
                add([x, g], min(len(ada), 1))
            half = (hi - lo) // 2
            for c in range(0, D, CHUNK):
                add([(f"ffn{l}.out", v[:, t:t + half, c:c + CHUNK], half, CHUNK) for t in (lo, lo + half)])

    ffn(0)
    assert not ada
    w = a["odd_w_in_2"][0]
    add(k8("odd.gates", w, 3008, 3088) + k8("odd.qk", w, 0, 1024) + k8("odd.v", w, 1024, 2048)
        + k8("odd.og", w, 2048, 3072))
    add(k8("odd_out", a["odd_w_out_2"][0], 0, D))
    ffn(1)
    return plan


class Engine:

    def __init__(self, eng):
        self.eng, self.seen = eng, {}

    def wait_ge(self, sem, value):
        if self.seen.get(sem.name, 0) < value:
            self.eng.wait_ge(sem, value)
            self.seen[sem.name] = value


class Chain:

    def __init__(self, eng, sem):
        self.eng, self.sem, self.n = eng, sem, 0

    def step(self, ins):
        ins.then_inc(self.sem, 1)
        self.n += 1

    def settle(self):
        self.eng.wait_ge(self.sem, self.n)

    def link(self, ins):
        self.step(ins)
        self.settle()


def two_block_kernel(nc, a, out):
    plan = weight_plan(a)
    landing = []
    for n, (_, src, kt, _) in enumerate(plan):
        landing.append((landing[n - RING] if n >= RING else 0) + 16 * (kt if len(src.shape) == 4 else 1))
    with ExitStack() as ctx:
        def sb(name, shape, dt=F32):
            return ctx.enter_context(nc.sbuf_tensor(name, shape, dt))

        def sem(name):
            return ctx.enter_context(nc.semaphore(name))

        banks = [ctx.enter_context(nc.psum_tensor(f"bank{n}", [P, S], F32)) for n in range(8)]
        ssq_bank, mod_bank = banks[ROT], banks[ROT + 1]

        x = sb("x", [P, KT, S])
        ring = sb("ring", [P, RING, KT * CHUNK])
        consts = sb("consts", [P, C_COLS])
        masks = sb("masks", [P, (len(HG_LEVELS) + 1) * P], U8)
        identb = sb("identb", [P, P], BF16)
        causal = sb("causal", [P, P], BF16)
        not_before = sb("not_before", [P, P], BF16)
        vecs = sb("vecs", [P, VEC_TILES * P])
        cs = sb("cs", [P, KT])
        acc = sb("acc", [P, ACC, CHUNK])
        mod = sb("mod", [P, 6 * KT * DEPTH])
        gmod = sb("gmod", [P, 4, KT])
        sq = sb("sq", [P, 2, S])
        var = sb("var", [P, S])
        rstd = var
        mx = sb("mx", [P, 2, NB])
        nmx = sb("nmx", [P, 2, NB])
        rsum = sb("rsum", [P, 2, NB])
        rinv = sb("rinv", [P, 2, NB])
        bf = sb("bf", [16, 2])
        lbt = sb("lbt", [P, 4, HG_HEADS])
        wh = sb("wh", [P, SPLIT, KT * CHUNK], F32R)
        wl = sb("wl", [P, SPLIT, KT * CHUNK], F32R)

        slab = sb("slab", [P, 120 * 256])
        base = nc.sbuf_base - 120 * 1024

        def at(name, kb, *shape, dt=F32):
            return nc.alloc_sbuf_tensor_at(name, [P, *shape], dt, offset=base + int(kb * 1024))

        def pair(name, kh, kl, *shape):
            return at(name + "h", kh, *shape, dt=F32R), at(name + "l", kl, *shape, dt=F32R)

        ident = consts[:, C_ID:C_ID + P]
        ones = consts[:, C_ONE:C_ONE + P]
        nincl = consts[:, C_NINCL:C_NINCL + P]
        nones = consts[:, C_NONE:C_NONE + P]
        ropes = slice(NOPE, NOPE + ROPE)
        rot = consts[ropes, C_ROT:C_ROT + ROPE]
        freq = consts[ropes, C_FREQ:C_FREQ + 1]

        km = at("km", 112, DEPTH, 2, M)
        vm = at("vm", 116, DEPTH, 2, M)
        x_tok, m_tok, vec_tok = at("x_tok", 32, NB, D), at("m_tok", 48, 2, D), at("vec_tok", 56, VEC_TILES, P)
        masks_f = at("masks_f", 58, (len(HG_LEVELS) + 2) * P)
        mem_n = at("mem_n", 64, KT, M)
        mh, ml = pair("mem", 80, 88, KT, M)
        xa = pair("xa", 0, 16, KT, S)
        tmp_a = at("tmp_a", 106, 2, S)
        pos_i, posf, turn = at("pos_i", 96, S, dt=I32), at("posf", 98, S), at("turn", 100, S)
        cos, sin = at("cos", 102, S), at("sin", 104, S)
        cq, ckv = at("cq", 48, 3, S), at("ckv", 54, 2, S)
        cqs, ckvs, kr = pair("cqs", 80, 86, 3, S), pair("ckvs", 92, 96, 2, S), at("kr", 100, S)
        rt = at("rt", 48, 4, S)
        qf, kf = at("qf", 0, HEADS, S), at("kf", 24, HEADS, S)
        v1 = at("v1", 48, NB, MAIN)
        gate = at("gate", 60, KT, S)
        qm = at("qm", 76, 2, S)
        probs = at("probs", 80, 2, PACK)
        probsT = at("probsT", 90, 2, 4, S)
        o1 = at("o1", 0, KT, S)
        ys = pair("ys", 16, 32, KT, S)
        xb = pair("xb", 80, 96, KT, S)
        tmp_b = at("tmp_b", 76, 2, S)
        frow = at("frow", 24, 6, S)
        hq, hk, pf, va = (at(n, 8 * i, 4, S) for i, n in enumerate(("hq", "hk", "pf", "va")))
        y2 = at("y2", 32, KT, S)
        qb, kb, vb = (at(n, 48 + 8 * i, 4, S) for i, n in enumerate(("qb", "kb", "vb")))
        xe = pair("xe", 72, 88, KT, S)
        tmp_e = at("tmp_e", 104, 2, S)
        pb = at("pb", 72, HG_HEADS, S)
        hx = [at("hx0", 88, HG_HEADS, S), at("hx1", 80, HG_HEADS, S)]
        at_d, at_1, at_2 = at("at_d", 96, HG_HEADS, S), at("at_1", 104, HG_HEADS, 256), at("at_2", 16, HG_HEADS, S)
        soft = [at("soft0", 72, PACK), at("soft1", 77, PACK)]
        lnb = at("lnb", 82, PACK)
        stick = [at("stick0", 96, PACK), at("stick1", 101, PACK)]
        ye = pair("ye", 0, 16, KT, S)
        xf = pair("xf", 0, 16, KT, S)
        tmp_f = at("tmp_f", 32, 2, S)
        hsp = pair("hsp", 36, 60, 12, S)
        a_raw = [at("a_raw0", 84, S + 2), at("a_raw1", 86.5, S + 2)]
        conv = [at("conv0", 89, S), at("conv1", 91, S)]
        gel = [at("gel0", 93, S), at("gel1", 95, S)]
        prod = at("prod", 97, 2, S)
        xo = pair("xo", 0, 16, KT, S)
        tmp_o = at("tmp_o", 32, 2, S)
        yo = pair("yo", 0, 16, KT, S)
        qk_raw = at("qk_raw", 36, KT, S + 3)
        qkc = at("qkc", 53, KT, S)
        vo = at("vo", 69, NB, D)
        og = at("og", 85, KT, S)
        grow = [at(f"grow{n}", 112 + 2 * n if n < 4 else 101 + 2 * (n - 4), S) for n in range(8)]
        dec = [at("dec0", 0, PACK), at("dec1", 5, PACK)]
        floor_b = [at("floor0", 10, S), at("floor1", 12, S)]
        den, deni = at("den", 14, S), at("deni", 16, S)
        hsq = at("hsq", 18, 4, S)
        hrs = [v[:, n, :] for v in (at("hrs0", 27, 4, S), at("hrs1", 112, 4, S)) for n in range(4)]
        ngcol = at("ngcol", 26, NB, ML_HEADS)
        ho = at("ho", 36, KT, S)
        out_n, out_tok = at("out_n", 0, KT, S), at("out_tok", 16, NB, D)

        def vec(name, n=0):
            tile, row, _ = VEC_ROWS[name]
            return vecs[:, tile * P + row + n:tile * P + row + n + 1]

        loaded_x, loaded_m, loaded_masks = sem("loaded_x"), sem("loaded_m"), sem("loaded_masks")
        loaded_c, loaded_p = sem("loaded_constants"), sem("loaded_positions")
        loaded_v = [sem("vectors_by_act"), sem("vectors_by_pool")]
        landed = [sem(f"chunk_landed{n}") for n in range(RING)]
        filled = sem("banks_filled")
        emptied = {"act": sem("emptied_by_act"), "dve": sem("emptied_by_dve")}
        sq_ready, sq_used = sem("square_ready"), sem("square_summed")
        ssq_taken, var_ready, rstd_ready = sem("ssq_taken"), sem("inverse_ready"), sem("rstd_ready")
        wh_ready, wl_ready, w_part = sem("weights_high_part"), sem("weights_low_part"), sem("chunk_part_used")
        xh_ready, xl_ready, scaled = sem("high_part"), sem("low_part"), sem("normed")
        x_ready = sem("x_tile_ready")
        ada_done, ada_summed = sem("ada_partial"), sem("ada_summed")
        cs_ready, mod_ready, const_ready = sem("silu_c_ready"), sem("mod_ready"), sem("bf16_constants")
        nmx_ready, rinv_ready, probs_ready = sem("neg_max_ready"), sem("inverse_sum_ready"), sem("probs_ready")
        last_ready = sem("last_block_ready")
        angle_ready, sin_ready = sem("angle_ready"), sem("sin_ready")
        kr_ready, rope_done, kf_ready = sem("rotary_key_ready"), sem("rope_done"), sem("keys_ready")
        f_log, frows_ready, frows_moved = sem("forget_log"), sem("forget_rows"), sem("forget_rows_moved")
        frows_set = sem("unit_rows_set")
        dve_step, act_step, pool_step = sem("dve_step"), sem("act_step"), sem("pool_step")
        hx_ready, levels_up, hg_ready = sem("level_ready"), sem("level_updated"), sem("decay_ready")
        lb_diff, lb_exp, lb_ready, hg_set = (sem("lb_difference"), sem("lb_exp"), sem("lb_ready"), sem("hgrn_set"))
        soft_log, soft_ready, soft_masked = sem("softplus_log"), sem("softplus_ready"), sem("softplus_masked")
        stick_sums = sem("stick_sums")
        sq_heads, head_inv, rstd_heads, y_heads = (sem("head_squares"), sem("head_inverse"), sem("head_rstd"),
                                                   sem("head_output_ready"))
        gates_moved, g_log = sem("gates_moved"), sem("gate_log")
        grows_ready, m_ready = sem("gate_rows_ready"), sem("gate_maxima_ready")
        floor_rows = sem("floor_rows")
        dec_exp, dec_masked = sem("decay_exp"), sem("decay_masked")
        qk_conv, qk_silu, qk_pads, pads = sem("qk_conv"), sem("qk_ready"), sem("qk_pads"), sem("conv_pads")
        post_scaled, mem_normed, cq_normed = sem("post_scaled"), sem("mem_normed"), sem("cq_normed")
        conv_ready, gelu_ready = sem("conv_ready"), sem("gelu_ready")
        stored, out_normed = sem("stored"), sem("out_normed")

        tiles, index, chunks = [], {}, []
        released, tile_chunk, mark = [], [], {}

        def wait_emptied(eng, key):
            owner, nth = tiles[index[key]][1:]
            eng.wait_ge(emptied[owner], nth + 1)

        def load_vectors(eng, queue):
            for name, (tile, row, k) in list(VEC_ROWS.items())[queue::2]:
                base, _, l = name.partition("/")
                src = a[base][int(l)] if l else a[base]
                if len(src.shape) > 1:
                    dims = " ".join("abc"[:len(src.shape)])
                    src = src.rearrange(f"{dims} -> ({dims})")
                eng.dma_start(vec_tok[row:row + k, tile, :], src.rearrange("(r p) -> r p", p=P)).then_inc(
                    loaded_v[queue], 16)

        block = ctx.enter_context(nc.Block())

        @block.tensor
        def _(eng):
            pe = Engine(eng)
            owned = {"act": 0, "dve": 0}
            counts = {"sq": 0, "ada": 0, "sum": 0, "hn": 0, "part": 0}

            def bank(key, owner):
                n = len(tiles)
                if n >= ROT:
                    _, who, nth = tiles[n - ROT]
                    pe.wait_ge(emptied[who], nth + 1)
                tiles.append((key, owner, owned[owner]))
                tile_chunk.append(len(released) - 1)
                index[key] = n
                owned[owner] += 1
                return banks[n % ROT]

            def done(ins):
                ins.then_inc(filled, 1)

            def chunk(stage):
                n = len(chunks)
                name, _, kt, cols = plan[n]
                assert name == stage, (name, stage)
                chunks.append("pe")
                while len(chunks) < len(plan) and plan[len(chunks)][0] == "ada":
                    chunks.append("ada")
                    counts["ada"] += 1
                m = len(released)
                released.append(None)
                pe.wait_ge(wl_ready, m + 1)
                return m, [v[:, m % SPLIT, 0:kt * cols].rearrange("p (t n) -> p t n", t=kt) for v in (wh, wl)]

            def chunk_done(m, part=None):
                released[m] = (filled, len(tiles)) if part is None else (w_part, part)

            def ada_sums(lag):
                while counts["sum"] < counts["ada"] - lag:
                    j = counts["sum"]
                    pe.wait_ge(ada_done, j + 1)
                    for half in range(2):
                        mm = eng.matmul(mod_bank[:, 2 * j + half:2 * j + half + 1],
                                        acc[:, j % ACC, half * P:(half + 1) * P], ones[:, 0:1], start=True, stop=True)
                    mm.then_inc(ada_summed, 1)
                    counts["sum"] += 1

            def three(o, ws, cols, xs, k, toks, first, last, swap=False):
                for i, (a_, b_) in enumerate(((0, 0), (0, 1), (1, 0))):
                    w, xx = ws[a_][:, k, cols], xs[b_][:, k, toks]
                    l_, r_ = (xx, w) if swap else (w, xx)
                    mm = eng.matmul(o, l_, r_, start=(first and i == 0), stop=(last and i == 2))
                return mm

            def features(key, owner, ws, cols, xs, kts, ready, n=S):
                b = bank(key, owner)
                for k in range(kts):
                    pe.wait_ge(xl_ready, SPLIT_AT[ready] + k + 1)
                    mm = three(b[0:cols.stop - cols.start, 0:n], ws, cols, xs, k, slice(0, n), k == 0, k == kts - 1)
                done(mm)

            def tokens(key, owner, ws, cols, xs, kts, blk, ready):
                b = bank(key, owner)
                pe.wait_ge(xl_ready, SPLIT_AT[ready] + kts)
                for k in range(kts):
                    mm = three(b[:, 0:cols.stop - cols.start], ws, cols, xs, k, slice(blk * P, (blk + 1) * P),
                               k == 0, k == kts - 1, swap=True)
                done(mm)

            def ssq(t, total):
                i = counts["sq"]
                pe.wait_ge(sq_ready, i + 1)
                if t == 0:
                    pe.wait_ge(ssq_taken, counts["hn"])
                    counts["hn"] += 1
                eng.matmul(ssq_bank[:, :], ones, sq[:, i % 2, :], start=(t == 0), stop=(t == total - 1)
                           ).then_inc(sq_used, 1)
                counts["sq"] += 1

            def wide(keys, owner, ws, xs, kts, ready, n=S):
                bs = [bank(key, owner) for key in keys]
                for k in range(kts):
                    pe.wait_ge(xl_ready, SPLIT_AT[ready] + k + 1)
                    for t, b in enumerate(bs):
                        mm = three(b[:, 0:n], ws, slice(t * P, (t + 1) * P), xs, k, slice(0, n), k == 0, k == kts - 1)
                        if k == kts - 1:
                            done(mm)

            def project(stage, nchunks, owner, ready, xs, tok=False, lag=None):
                t = 0
                for _ in range(nchunks):
                    m, ws = chunk(stage)
                    cols = ws[0].shape[2]
                    if tok:
                        for b in range(NB):
                            tokens((stage, t, b), owner, ws, slice(0, cols), xs, KT, b, ready)
                        t += 1
                    elif cols == CHUNK:
                        wide([(stage, t), (stage, t + 1)], owner, ws, xs, KT, ready)
                        t += 2
                    else:
                        features((stage, t), owner, ws, slice(0, cols), xs, KT, ready)
                    chunk_done(m)
                    if lag is not None:
                        ada_sums(lag)

            pe.wait_ge(loaded_c, 16)
            pe.wait_ge(loaded_m, 16)
            for k in range(0, KT, 2):
                b = bank(("mT", k), "dve")
                for j in range(4):
                    t = eng.transpose(b[:, j * P:(j + 1) * P],
                                      m_tok[:, j % 2, (k + j // 2) * P:(k + j // 2 + 1) * P], ident)
                done(t)
            pe.wait_ge(loaded_x, 16)
            for k in range(KT):
                b = bank(("xT", k), "dve")
                for j in range(NB):
                    t = eng.transpose(b[:, j * P:(j + 1) * P], x_tok[:, j, k * P:(k + 1) * P], ident)
                done(t)
            for queue in range(2):
                pe.wait_ge(loaded_v[queue], 16 * len(list(VEC_ROWS)[queue::2]))
            for n in range(VEC_TILES):
                rows = max(r + k for t, r, k in VEC_ROWS.values() if t == n)
                b = bank(("vec", n), "dve")
                done(eng.transpose(b[:, 0:rows], vec_tok[0:rows, n, :], ident[0:rows, 0:rows]))
            for k in range(4):
                i = counts["sq"]
                pe.wait_ge(sq_ready, i + 1)
                eng.matmul(ssq_bank[:, 0:M], ones, sq[:, i % 2, 0:M], start=(k == 0), stop=False)
                eng.matmul(ssq_bank[:, 0:M], ones, sq[:, i % 2, M:2 * M], start=False, stop=(k == 3)
                           ).then_inc(sq_used, 1)
                counts["sq"] += 1
            counts["hn"] += 1
            for k in range(KT):
                ssq(k, KT)
            for l in range(DEPTH):
                m, ws = chunk(f"mem{l}")
                wide([("km", l, c) for c in range(2)], "act", ws, (mh, ml), KT, "mem", n=M)
                chunk_done(m)
                m, ws = chunk(f"mem{l}")
                for b in range(2):
                    tokens(("vm", l, b), "act", ws, slice(0, M), (mh, ml), KT, b, "mem")
                chunk_done(m)
                ada_sums(1)
            for c in range(2):
                m, ws = chunk("in_a.cq")
                wide([("cq", 2 * c + t) for t in range(2)], "act", ws, xa, KT, "x_a")
                chunk_done(m)
                ada_sums(1)
            m, ws = chunk("in_a.kr")
            features(("cq", 4), "act", ws, slice(0, P), xa, KT, "x_a")
            features(("kr",), "act", ws, slice(P - NOPE, P + ROPE), xa, KT, "x_a")
            chunk_done(m)
            ada_sums(1)
            project("in_a.qm", 1, "act", "x_a", xa, lag=1)
            for t in range(3):
                ssq(t, 3)
            for t in range(2):
                ssq(t, 2)
            b = bank(("krot",), "dve")
            wait_emptied(pe, ("kr",))
            done(eng.matmul(b[ropes, :], rot, kr[ropes, :], start=True, stop=True))
            project("in_a.gate", 4, "act", "x_a", xa, lag=1)
            h = 0
            for _ in range(2):
                m, ws = chunk("q_up")
                for j in range(6):
                    features(("q", h), "act", ws, slice(96 * j, 96 * (j + 1)), cqs, 3, "cq")
                    if h >= 1:
                        rotate = h - 1
                        b = bank(("qrot", rotate), "dve")
                        wait_emptied(pe, ("q", rotate))
                        done(eng.matmul(b[ropes, :], rot, qf[ropes, rotate, :], start=True, stop=True))
                    h += 1
                chunk_done(m)
            b = bank(("qrot", HEADS - 1), "dve")
            wait_emptied(pe, ("q", HEADS - 1))
            done(eng.matmul(b[ropes, :], rot, qf[ropes, HEADS - 1, :], start=True, stop=True))
            m, ws = chunk("kv_up")
            for t in range(6):
                features(("k", 2 * t), "act", ws, slice(t * P, (t + 1) * P), ckvs, 2, "ckv")
            chunk_done(m)
            m, ws = chunk("kv_up")
            for c in range(2):
                for blk in range(NB):
                    tokens(("v", c, blk), "act", ws, slice(384 * c, 384 * (c + 1)), ckvs, 2, blk, "ckv")
            chunk_done(m)
            mark["att0"] = len(released)

            def attention(l):
                def scores(h):
                    if h == HEADS:
                        wait_emptied(pe, (("in_a.qm", "in_b.qm")[l], 1))
                        wait_emptied(pe, ("km", l, 1))
                    for i in range(NB):
                        b = bank(("s", l, h, i), "act")
                        if h < HEADS:
                            kd, n = (NOPE + ROPE, HD + 2)[l], (i + 1) * P
                            eng.matmul(b[:, 0:n], qf[0:kd, h, i * P:n], kf[0:kd, h, 0:n], start=True, stop=False)
                            done(eng.matmul(b[:, i * P:n], identb[:, :], causal[:, :], start=False, stop=True))
                        else:
                            g = h - HEADS
                            rows = slice(HD * (g % 2), HD * (g % 2) + HD)
                            done(eng.matmul(b[:, 0:M], qm[rows, g // 2, i * P:(i + 1) * P], km[rows, l, g // 2, :],
                                            start=True, stop=True))

                def transposes(h):
                    par = h % 2
                    for i in range(NB):
                        nk = i + 1 if h < HEADS else 2
                        po = 128 * (i * (i + 1) // 2) if h < HEADS else i * M
                        b = bank(("t", l, h, i), "dve" if i % 2 else "act")
                        if i < NB - 1:
                            pe.wait_ge(probs_ready, (l * 16 + h) * (NB - 1) + i + 1)
                        else:
                            pe.wait_ge(last_ready, l * 16 + h + 1)
                        for j in range(nk):
                            t = eng.transpose(b[:, j * P:(j + 1) * P], probs[:, par, po + j * P:po + (j + 1) * P], ident)
                        done(t)

                def apply(h):
                    par = h % 2
                    b = bank(("o", l, h), "dve")
                    o = b[HD * par:HD * par + HD, :]
                    for i in range(NB):
                        wait_emptied(pe, ("t", l, h, i))
                    nk = NB if h < HEADS else 2
                    for j in range(nk):
                        first = j * P if h < HEADS else 0
                        v = v1[:, j, h * HD:(h + 1) * HD] if h < HEADS else vm[:, l, j, (h - HEADS) * HD:(h - HEADS + 1) * HD]
                        mm = eng.matmul(o[:, first:S], v, probsT[:, par, j, first:S], start=(j == 0), stop=(j == nk - 1))
                    done(mm)

                for h in range(16 + 2):
                    if h < 16:
                        scores(h)
                    if 1 <= h <= 16:
                        transposes(h - 1)
                    if h >= 2:
                        apply(h - 2)

            pe.wait_ge(const_ready, 4)
            pe.wait_ge(kf_ready, 16)
            pe.wait_ge(rope_done, HEADS)
            for c in range(2):
                wait_emptied(pe, ("v", c, NB - 1))
            attention(0)

            def out_first(l):
                stage, ready = ("out_a", "out_b")[l], ("y_a", "y_b")[l]
                for c in range(4):
                    m, ws = chunk(stage)
                    wide([(stage, 2 * c + t) for t in range(2)], "act", ws, ys, KT, ready)
                    if c >= 1:
                        for t in range(2):
                            ssq(2 * c - 2 + t, KT)
                    chunk_done(m)
                    ada_sums(1)
                ssq(KT - 2, KT)
                ssq(KT - 1, KT)
                for t in range(KT):
                    ssq(t, KT)

            out_first(0)
            m, ws = chunk("in_b.f")
            features(("f",), "act", ws, slice(0, P), xb, KT, "x_b")
            chunk_done(m)
            ada_sums(1)
            project("in_b.v", 3, "act", "x_b", xb, tok=True, lag=1)
            project("in_b.qm", 1, "act", "x_b", xb, lag=1)
            project("in_b.gate", 4, "act", "x_b", xb, lag=1)
            project("in_b.q", 3, "act", "x_b", xb, lag=1)
            project("in_b.k", 3, "act", "x_b", xb, lag=1)
            mark["att1"] = len(released)
            for s in range(3):
                wait_emptied(pe, ("in_b.v", s, NB - 1))
            pe.wait_ge(frows_moved, 16 * 2 * HEADS)
            attention(1)
            out_first(1)
            ada_sums(0)

            for name in ("qa", "fa"):
                project("even." + name, 2, "act", "x_even", xe, lag=1)
            project("even.ia", 2, "act", "x_even", xe, tok=True, lag=1)
            for name in ("ga", "qb", "kb"):
                project("even." + name, 2, "act", "x_even", xe, lag=1)
            project("even.vb", 2, "act", "x_even", xe, tok=True, lag=1)
            mark["hgrn"] = len(released)
            def level(name, lhs, rhs):
                for h in range(HG_HEADS):
                    b = bank(name + (h,), "dve")
                    for j in range(NB):
                        c = slice(j * P, (j + 1) * P)
                        mm = eng.matmul(b[:, c], lhs[:, h, c], rhs[:, h, c], start=(j == 0), stop=(j == NB - 1),
                                        skip_group_check=True)
                    done(mm)

            wait_emptied(pe, ("even.vb", 1, NB - 1))
            pe.wait_ge(hg_ready, HG_HEADS)
            level(("diag",), hk, hq)
            for n in range(len(HG_LEVELS)):
                pe.wait_ge(hx_ready, n + 1)
                level(("lv", n), hx[n % 2], hx[n % 2])
            n = len(HG_LEVELS)
            pe.wait_ge(hx_ready, n + 1)
            for h in range(HG_HEADS):
                b = bank(("lv", n, h), "dve")
                X = hx[n % 2]
                eng.matmul(b[:, 0:P], X[:, h, 0:P], X[:, h, P:2 * P], start=True, stop=False, skip_group_check=True)
                done(eng.matmul(b[:, P:2 * P], X[:, h, 2 * P:3 * P], X[:, h, 3 * P:4 * P], start=False, stop=True,
                                skip_group_check=True))
            pe.wait_ge(hx_ready, n + 2)
            for h in range(HG_HEADS):
                b = bank(("lv", n + 1, h), "dve")
                X = hx[(n + 1) % 2]
                eng.matmul(b[:, 0:M], X[:, h, 0:P], X[:, h, M:S], start=True, stop=False, skip_group_check=True)
                done(eng.matmul(b[:, M:S], X[:, h, P:2 * P], X[:, h, M:S], start=False, stop=True,
                                skip_group_check=True))
            for h in range(HG_HEADS):
                b = bank(("ho", h), "act")
                wait_emptied(pe, ("lv", n + 1, h))
                hs = slice(h * P, (h + 1) * P)
                for j in range(NB):
                    c = slice(j * P, (j + 1) * P)
                    eng.matmul(b[:, c], va[:, j, hs], at_d[:, h, c], start=(j == 0), stop=False, skip_group_check=True)
                eng.matmul(b[:, P:2 * P], va[:, 0, hs], at_1[:, h, 0:P], start=False, stop=False, skip_group_check=True)
                eng.matmul(b[:, 3 * P:S], va[:, 2, hs], at_1[:, h, P:2 * P], start=False, stop=False,
                           skip_group_check=True)
                eng.matmul(b[:, M:S], va[:, 0, hs], at_2[:, h, 0:M], start=False, stop=False, skip_group_check=True)
                done(eng.matmul(b[:, M:S], va[:, 1, hs], at_2[:, h, M:S], start=False, stop=True,
                                skip_group_check=True))
            for h in range(HG_HEADS):
                b = bank(("hs", h), "dve")
                pe.wait_ge(sq_heads, h + 1)
                done(eng.matmul(b[:, :], ones, hq[:, h, :], start=True, stop=True))

            def stick_scores(h):
                for j in range(3):
                    zs[h % 2][j] = bank(("z", h, j), "act")
                    for i in range(j, NB):
                        nb, c0 = TRI_BANK[i]
                        if nb == j:
                            mm = eng.matmul(zs[h % 2][j][:, c0:c0 + WIDE[i]], kb[:, h, i * P:(i + 1) * P],
                                            qb[:, h, i * P:S], start=(c0 == 0), stop=(i == NB - 1 or j < 2),
                                            skip_group_check=True)
                    done(mm)

            def stick_later_keys(h):
                pe.wait_ge(soft_masked, h + 1)
                sp = soft[h % 2]
                for j in range(NB):
                    src = sp[:, OFF[j]:OFF[j] + WIDE[j]]
                    nb, c0 = TRI_BANK[j]
                    eng.matmul(zs[h % 2][nb][:, c0:c0 + P], identb[:, :], not_before[:, :], start=False,
                               stop=False, skip_group_check=True)
                    mm = eng.matmul(zs[h % 2][nb][:, c0:c0 + WIDE[j]], nincl, src, start=False, stop=(j == NB - 1),
                                    skip_group_check=True)
                    for i in range(j):
                        nb, c0 = TRI_BANK[i]
                        lo = c0 + (j - i) * P
                        mm = eng.matmul(zs[h % 2][nb][:, lo:lo + WIDE[j]], nones, src, start=False,
                                        stop=(j == NB - 1), skip_group_check=True)
                mm.then_inc(stick_sums, 1)

            def stick_apply(h):
                b = bank(("so", h), "act")
                wait_emptied(pe, ("z", h, 2))
                for j in range(NB):
                    mm = eng.matmul(b[:, j * P:S], vb[:, j, h * P:(h + 1) * P],
                                    stick[h % 2][:, OFF[j]:OFF[j] + WIDE[j]], start=(j == 0), stop=(j == NB - 1))
                done(mm)

            zs = [[None] * 3 for _ in range(2)]
            for h in range(5):
                if h < 4:
                    stick_scores(h)
                if h >= 1:
                    stick_apply(h - 1)
                if h < 4:
                    stick_later_keys(h)

            def out_second(stage, parts, xs, ready, last=True):
                for c in range(4):
                    bs = [bank(stage + (2 * c + t,), "dve") for t in range(2)]
                    k0 = 0
                    for i in range(parts):
                        m, ws = chunk(stage[0])
                        tile_chunk[-1] = tile_chunk[-2] = m
                        kt = ws[0].shape[1]
                        for k in range(kt):
                            pe.wait_ge(xl_ready, SPLIT_AT[ready] + k0 + k + 1)
                            for t, b in enumerate(bs):
                                first, end = k0 + k == 0, (i == parts - 1 and k == kt - 1)
                                for j, (a_, b_) in enumerate(((0, 0), (0, 1), (1, 0))):
                                    mm = eng.matmul(b[:, :], ws[a_][:, k, t * P:(t + 1) * P], xs[b_][:, k0 + k, :],
                                                    start=(first and j == 0), stop=(end and j == 2))
                                if end:
                                    done(mm)
                        k0 += kt
                        if i < parts - 1:
                            mm.then_inc(w_part, 1)
                            counts["part"] += 1
                            chunk_done(m, counts["part"])
                        else:
                            chunk_done(m)
                    if last and c >= 1:
                        for t in range(2):
                            ssq(2 * c - 2 + t, KT)
                if last:
                    ssq(KT - 2, KT)
                    ssq(KT - 1, KT)

            out_second(("even_out",), 1, ye, "y_even")

            def ffn(l):
                for part, (lo, hi) in enumerate(FFN_PARTS):
                    for t in range(lo, hi, 2):
                        for g, owner in (("a", "act"), ("g", "dve")):
                            m, ws = chunk(f"ffn{l}.{g}")
                            wide([("f" + g, l, t + i) for i in range(2)], owner, ws, xf, KT, f"x_ffn{l}")
                            chunk_done(m)
                        if l == 0:
                            ada_sums(1)
                    if l == 0 and part == 1:
                        ada_sums(0)
                    out_second((f"ffn{l}.out", part), 2, hsp, f"ffn{l}/{part}", last=(part == 1))

            ffn(0)
            m, ws = chunk("odd.gates")
            features(("og_rows",), "act", ws, slice(0, 80), xo, KT, "x_odd")
            chunk_done(m)
            project("odd.qk", 4, "act", "x_odd", xo)
            project("odd.v", 4, "act", "x_odd", xo, tok=True)
            project("odd.og", 4, "act", "x_odd", xo)
            mark["mlstm"] = len(released)
            pe.wait_ge(grows_ready, 1)
            b = bank(("gcol",), "dve")
            for j in range(NB):
                t = eng.transpose(b[:, j * ML_HEADS:(j + 1) * ML_HEADS], grow[4][0:8, j * P:(j + 1) * P],
                                  ident[0:8, 0:8])
            done(t)

            def ml_weights(h):
                pick = ident[0:8, h:h + 1].to_broadcast([8, P])
                b = bank(("mb", h), "act")
                done(eng.matmul(b[:, :], pick, grow[5][0:8, :], start=True, stop=True))
                b = bank(("eb", h), "act")
                pe.wait_ge(floor_rows, 1)
                done(eng.matmul(b[:, :], pick, grow[7][0:8, :], start=True, stop=True))
                rows = slice(64 * (h % 2), 64 * (h % 2) + 64)
                for j in range(3):
                    b = bank(("qk", h, j), "dve")
                    for i in range(j, NB):
                        nb, c0 = TRI_BANK[i]
                        if nb == j:
                            mm = eng.matmul(b[:, c0:c0 + WIDE[i]], qkc[rows, 4 + h // 2, i * P:(i + 1) * P],
                                            qkc[rows, h // 2, i * P:S], start=(c0 == 0), stop=(i == NB - 1 or j < 2),
                                            skip_group_check=True)
                    done(mm)

            def ml_apply(h):
                W = dec[h % 2]
                bd = bank(("den", h), "dve")
                wait_emptied(pe, ("qk", h, 2))
                for j in range(NB):
                    mm = eng.matmul(bd[:, j * P:S], ones, W[:, OFF[j]:OFF[j] + WIDE[j]], start=(j == 0),
                                    stop=(j == NB - 1))
                done(mm)
                bn = bank(("num", h), "dve")
                for j in range(NB):
                    mm = eng.matmul(bn[:, j * P:S], vo[:, j, h * P:(h + 1) * P], W[:, OFF[j]:OFF[j] + WIDE[j]],
                                    start=(j == 0), stop=(j == NB - 1))
                done(mm)

            def ml_squares(h):
                b = bank(("ms", h), "dve")
                pe.wait_ge(sq_heads, HG_HEADS + h + 1)
                done(eng.matmul(b[:, :], ones, hsq[:, h % 4, :], start=True, stop=True))

            pe.wait_ge(qk_silu, KT)
            wait_emptied(pe, ("odd.og", KT - 1))
            for h in range(ML_HEADS + 1):
                if h < ML_HEADS:
                    ml_weights(h)
                if h >= 1:
                    ml_apply(h - 1)
                if h >= 2:
                    ml_squares(h - 2)
            ml_squares(ML_HEADS - 1)
            out_second(("odd_out",), 1, yo, "y_odd")
            ffn(1)
            for j in range(NB):
                for half in range(2):
                    b = bank(("out", j, half), "dve")
                    pe.wait_ge(out_normed, KT)
                    for k in range(4):
                        t = eng.transpose(b[:, k * P:(k + 1) * P], out_n[:, 4 * half + k, j * P:(j + 1) * P], ident)
                    done(t)
            assert len(chunks) == len(plan)

        def take(eng, key, owner):
            n = index[key]
            assert tiles[n][1] == owner
            eng.wait_ge(filled, n + 1)
            return banks[n % ROT]

        def peek(eng, key):
            n = index[key]
            eng.wait_ge(filled, n + 1)
            return banks[n % ROT]

        def transposed(eng, who, l, h, odd, owner):
            par = h % 2
            for i in range(odd, NB, 2):
                nk = i + 1 if h < HEADS else 2
                b = take(who, ("t", l, h, i), owner)
                if h >= 2:
                    peek(who, ("o", l, h - 2))
                src = b[:, 0:nk * P].rearrange("p (j q) -> p j q", q=P)
                dst = probsT[:, par, 0:nk, i * P:(i + 1) * P]
                if owner == "act":
                    eng.activation(dst, src, ACT.Copy).then_inc(emptied[owner], 1)
                else:
                    eng.tensor_copy(dst, src).then_inc(emptied[owner], 1)

        @block.sync
        def _(eng):
            sp = Engine(eng)
            eng.dma_start(consts[:, :], a["const_f32"][:, 0:C_COLS]).then_inc(loaded_c, 16)
            eng.dma_start(m_tok[:], a["mem"][0].rearrange("(b p) d -> p b d", p=P)).then_inc(loaded_m, 16)
            eng.dma_start(x_tok[:], a["x"][0].rearrange("(b p) d -> p b d", p=P)).then_inc(loaded_x, 16)
            eng.dma_start(masks_f[:], a["const_f32"][:, C_COLS:]).then_inc(loaded_masks, 16)
            for n, (name, src, kt, cols) in enumerate(plan):
                if n >= RING:
                    user = chunks[n - RING]
                    sp.wait_ge({"pe": wl_ready, "ada": ada_done}[user], chunks[:n - RING + 1].count(user))
                dst = ring[:, n % RING, 0:kt * cols].rearrange("p (t n) -> p t n", t=kt)
                if len(src.shape) == 4:
                    for t in range(kt):
                        eng.dma_start(dst[:, t, :].rearrange("p (h n) -> p h n", h=HEADS), src[:, t]
                                      ).then_inc(landed[n % RING], 16)
                    continue
                eng.dma_start(dst, src).then_inc(landed[n % RING], 16)
            for j in range(NB):
                wait_emptied(sp, ("out", j, 1))
                eng.dma_start(out[0, j * P:(j + 1) * P, :], out_tok[:, j, :]).then_inc(stored, 16)
            eng.wait_ge(stored, 16 * NB)

        @block.scalar
        def _(eng):
            act = Engine(eng)
            chain = Chain(eng, act_step)
            used = {"sq": 0, "norm": 0, "w": 0, "n": 0}
            pe_at = [n for n, c in enumerate(plan) if c[0] != "ada"]

            load_vectors(eng, 0)
            eng.dma_start(bf[0:HEADS, 0:1], a["b_f"].rearrange("a h -> h a")).then_inc(loaded_p, 16)
            eng.dma_start(bf[0:16, 1:2], a["odd_gate_b_2"].rearrange("a h -> h a")).then_inc(loaded_p, 16)
            eng.dma_start(pos_i[ropes, :], a["positions"][0].partition_broadcast(ROPE)).then_inc(loaded_p, 16)

            def split_weights(upto):
                while used["w"] < min(upto, len(released)):
                    m = used["w"]
                    n = pe_at[m]
                    if m >= SPLIT:
                        act.wait_ge(*released[m - SPLIT])
                    act.wait_ge(landed[n % RING], landing[n])
                    w = plan[n][2] * plan[n][3]
                    eng.activation(wh[:, m % SPLIT, 0:w], ring[:, n % RING, 0:w], ACT.Copy).then_inc(wh_ready, 1)
                    used["w"] += 1

            def empty(key, out, func=ACT.Copy, part=None, **kw):
                split_weights(tile_chunk[index[key]] + 2)
                b = take(act, key, "act")
                eng.activation(out, b[:, :] if part is None else b[part], func, **kw).then_inc(emptied["act"], 1)

            def high(src, dst, sem_in=None, value=0):
                if sem_in is not None:
                    act.wait_ge(sem_in, value)
                eng.activation(dst, src, ACT.Copy).then_inc(xh_ready, 1)

            def high_normed(tmp, dst, ts=range(KT)):
                for t in ts:
                    used["n"] += 1
                    high(tmp[:, t % 2, :], dst[0][:, t, :], scaled, used["n"])

            def square(src):
                i = used["sq"]
                if i >= 2:
                    act.wait_ge(sq_used, i - 1)
                eng.activation(sq[:, i % 2, :], src, ACT.Square).then_inc(sq_ready, 1)
                used["sq"] += 1

            def root(n=S):
                k = used["norm"]
                act.wait_ge(var_ready, k + 1)
                eng.activation(rstd[:, 0:n], var[:, 0:n], ACT.Sqrt).then_inc(rstd_ready, 1)
                used["norm"] += 1

            for k in range(4):
                wait_emptied(act, ("mT", 2 * k))
                square(mem_n[:, 2 * k:2 * k + 2, :])
            split_weights(2)
            for k in range(KT):
                wait_emptied(act, ("xT", k))
                square(x[:, k, :])
                if k == 1:
                    root(M)
            for t in range(KT):
                high(mem_n[:, t, :], mh[:, t, :], mem_normed, t + 1)
            root()
            high_normed(tmp_a, xa, range(2))
            for c in range(2):
                empty(("km", 0, c), km[:, 0, c, :], part=(slice(0, P), slice(0, M)))
            high_normed(tmp_a, xa, range(2, KT))
            for b in range(2):
                empty(("vm", 0, b), vm[:, 0, b, :], part=(slice(0, P), slice(0, M)))
            act.wait_ge(angle_ready, 1)
            eng.activation(sin[ropes, :], sin[ropes, :], ACT.Sin).then_inc(sin_ready, 1)
            eng.activation(cos[ropes, :], cos[ropes, :], ACT.Sin).then_inc(sin_ready, 1)
            for c in range(2):
                empty(("km", 1, c), km[:, 1, c, :], part=(slice(0, P), slice(0, M)))
            for b in range(2):
                empty(("vm", 1, b), vm[:, 1, b, :], part=(slice(0, P), slice(0, M)))
            for t in range(5):
                dst = cq[:, t, :] if t < 3 else ckv[:, t - 3, :]
                empty(("cq", t), dst)
            empty(("kr",), kr[ropes, :], part=(ropes, slice(0, S)))
            for t in range(2):
                empty(("in_a.qm", t), qm[:, t, :])
            for t in range(5):
                wait_emptied(act, ("cq", t))
                square(cq[:, t, :] if t < 3 else ckv[:, t - 3, :])
                if t == 2:
                    root()
            for t in range(3):
                high(cq[:, t, :], cqs[0][:, t, :], cq_normed, t + 1)
            root()
            for t in range(2):
                high(ckv[:, t, :], ckvs[0][:, t, :], cq_normed, 3 + t + 1)
            eng.activation(cs[:, :], vecs[:, 0:KT], ACT.Silu).then_inc(cs_ready, 1)
            act.wait_ge(const_ready, 2)
            for t in range(KT):
                empty(("in_a.gate", t), gate[:, t, :], ACT.Silu)
            for h in range(HEADS):
                empty(("q", h), qf[0:96, h, :], part=(slice(0, 96), slice(0, S)))
            for h in range(0, HEADS, 2):
                split_weights(tile_chunk[index[("k", h)]] + 2)
                b = take(act, ("k", h), "act")
                eng.activation(kf[0:NOPE, h, :], b[0:NOPE, :], ACT.Copy)
                eng.activation(kf[0:NOPE, h + 1, :], b[NOPE:P, :], ACT.Copy).then_inc(emptied["act"], 1)
            act.wait_ge(rope_done, HEADS)
            for c in range(2):
                for blk in range(NB):
                    empty(("v", c, blk), v1[:, blk, 384 * c:384 * (c + 1)], part=(slice(0, P), slice(0, 384)))

            def attention(l):
                split_weights(mark[f"att{l}"] + 2)
                for h in range(16 + 1):
                    if h < 16:
                        par = h % 2
                        for i in range(NB):
                            n = (i + 1) * P if h < HEADS else M
                            po = P * (i * (i + 1) // 2) if h < HEADS else i * M
                            scale = (MLA_SCALE, 1.0)[l] if h < HEADS else HD ** -0.5
                            b = take(act, ("s", l, h, i), "act")
                            act.wait_ge(nmx_ready, (l * 16 + h) * NB + i + 1)
                            if h >= 2:
                                peek(act, ("t", l, h - 2, NB - 1))
                            eng.activation(probs[:, par, po:po + n], b[:, 0:n], ACT.Exp, bias=nmx[:, par, i:i + 1],
                                           scale=scale, accum_out=rsum[:, par, i:i + 1]).then_inc(emptied["act"], 1)
                    if h >= 1:
                        transposed(eng, act, l, h - 1, 0, "act")

            attention(0)

            def out_first(l):
                stage = ("out_a", "out_b")[l]
                for t in range(KT):
                    wait_emptied(act, ("o", l, 2 * t + 1))
                    high(gate[:, t, :], ys[0][:, t, :])
                for t in range(KT):
                    split_weights(tile_chunk[index[(stage, t)]] + 2)
                    b = take(act, (stage, t), "act")
                    square(b[:, :])
                    eng.activation(o1[:, t, :], b[:, :], ACT.Copy).then_inc(emptied["act"], 1)
                root()
                for t in range(KT):
                    act.wait_ge(x_ready, l * KT + t + 1)
                    square(x[:, t, :])
                root()

            out_first(0)
            high_normed(tmp_b, xb)

            def log_of(z, rows, sem_out):
                chain.link(eng.activation(rows, z, ACT.Abs))
                chain.link(eng.activation(rows, rows, ACT.Exp, scale=-1.0))
                eng.activation(rows, rows, ACT.Ln, bias=1.0).then_inc(sem_out, 1)

            act.wait_ge(loaded_p, 48)
            empty(("f",), frow[0:HEADS, 0, :], ACT.Identity, part=(slice(0, HEADS), slice(0, S)), bias=bf[0:HEADS, 0:1])
            wait_emptied(act, ("f",))
            log_of(frow[0:HEADS, 0, :], frow[0:HEADS, 1, :], f_log)
            half_bank = (slice(0, P), slice(0, CHUNK))
            for s in range(3):
                for b in range(NB):
                    empty(("in_b.v", s, b), v1[:, b, CHUNK * s:CHUNK * (s + 1)], part=half_bank)
            for t in range(2):
                empty(("in_b.qm", t), qm[:, t, :])
            for t in range(KT):
                empty(("in_b.gate", t), gate[:, t, :], ACT.Silu)
            for name, dst, scale in (("in_b.q", qf, HD ** -0.5), ("in_b.k", kf, 1.0)):
                if dst is kf:
                    act.wait_ge(frows_moved, 16 * 2 * HEADS)
                for t in range(6):
                    split_weights(tile_chunk[index[(name, t)]] + 2)
                    b = take(act, (name, t), "act")
                    eng.activation(dst[0:HD, 2 * t, :], b[0:HD, :], ACT.Copy, scale=scale)
                    eng.activation(dst[0:HD, 2 * t + 1, :], b[HD:P, :], ACT.Copy, scale=scale
                                   ).then_inc(emptied["act"], 1)
            attention(1)
            out_first(1)
            act.wait_ge(mod_ready, 2)

            def shift(l, part, tmp, dst):
                for t in range(KT):
                    used["n"] += 1
                    act.wait_ge(scaled, used["n"])
                    col = 48 * l + 8 * part + t
                    eng.activation(dst[0][:, t, :], tmp[:, t % 2, :], ACT.Identity, bias=mod[:, col:col + 1]
                                   ).then_inc(xh_ready, 1)

            shift(0, 0, tmp_e, xe)
            act.wait_ge(lb_diff, 1)
            eng.activation(lbt[:, 1, :], lbt[:, 0, :], ACT.Exp).then_inc(lb_exp, 1)
            for t in range(4):
                empty(("even.qa", t), hq[:, t, :])
            for t in range(4):
                split_weights(tile_chunk[index[("even.fa", t)]] + 2)
                b = take(act, ("even.fa", t), "act")
                eng.activation(pf[:, t, :], b[:, :], ACT.Sigmoid)
                eng.activation(hk[:, t, :], b[:, :], ACT.Sigmoid, scale=-1.0).then_inc(emptied["act"], 1)
            for s in range(2):
                for b in range(NB):
                    empty(("even.ia", s, b), va[:, b, CHUNK * s:CHUNK * (s + 1)], part=half_bank)
            for t in range(4):
                empty(("even.ga", t), y2[:, t, :], ACT.Silu)
            for t in range(4):
                empty(("even.qb", t), qb[:, t, :], scale=float(P) ** -0.5)
            for t in range(4):
                empty(("even.kb", t), kb[:, t, :])
            for s in range(2):
                for b in range(NB):
                    empty(("even.vb", s, b), vb[:, b, CHUNK * s:CHUNK * (s + 1)], part=half_bank)
            split_weights(mark["hgrn"] + 2)
            for h in range(HG_HEADS):
                b = take(act, ("ho", h), "act")
                eng.activation(hq[:, h, :], b[:, :], ACT.Square).then_inc(sq_heads, 1)
                eng.activation(hk[:, h, :], b[:, :], ACT.Copy).then_inc(emptied["act"], 1)
            for h in range(HG_HEADS):
                act.wait_ge(head_inv, h + 1)
                eng.activation(hx[0][:, h, :], hx[0][:, h, :], ACT.Sqrt).then_inc(rstd_heads, 1)
            for h in range(5):
                if h < 4:
                    if h >= 1:
                        act.wait_ge(soft_ready, h)
                    for j in range(3):
                        b = peek(act, ("z", h, j))
                        n = S if j == 0 else 384
                        chain.step(eng.activation(lnb[:, OFF[j]:OFF[j] + n], b[:, 0:n], ACT.Abs))
                    chain.settle()
                    chain.link(eng.activation(lnb[:], lnb[:], ACT.Exp, scale=-1.0))
                    eng.activation(lnb[:], lnb[:], ACT.Ln, bias=1.0).then_inc(soft_log, 1)
                    act.wait_ge(stick_sums, h + 1)
                    if h >= 2:
                        peek(act, ("so", h - 2))
                    for j in range(3):
                        n = S if j == 0 else 384
                        empty(("z", h, j), stick[h % 2][:, OFF[j]:OFF[j] + n], ACT.Exp,
                              part=(slice(0, P), slice(0, n)))
                if h >= 1:
                    empty(("so", h - 1), y2[:, 4 + h - 1, :])

            def out_second(*stage):
                for t in range(KT):
                    split_weights(tile_chunk[index[stage + (t,)]] + 2)
                    wait_emptied(act, stage + (t,))
                    square(x[:, t, :])
                root()

            for t in range(KT):
                if t < 4:
                    act.wait_ge(y_heads, t + 1)
                else:
                    wait_emptied(act, ("so", t - 4))
                high(y2[:, t, :], ye[0][:, t, :])
            out_second("even_out")
            shift(0, 3, tmp_f, xf)

            def ffn(l):
                for part, (lo, hi) in enumerate(FFN_PARTS):
                    for t0 in range(lo, hi + 1, 2):
                        if t0 < hi:
                            for t in (t0, t0 + 1):
                                i = l * FT + t
                                if i >= 2:
                                    act.wait_ge(conv_ready, i - 1)
                                empty(("fa", l, t), a_raw[t % 2][:, 2:2 + S])
                        if t0 > lo:
                            for t in (t0 - 2, t0 - 1):
                                split_weights(tile_chunk[index[("fg", l, t)]] + 2)
                                wait_emptied(act, ("fg", l, t))
                                high(prod[:, t % 2, :], hsp[0][:, t - lo, :])
                        if t0 < hi:
                            split_weights(tile_chunk[index[("fa", l, t0)]] + 2)
                            for t in (t0, t0 + 1):
                                act.wait_ge(conv_ready, l * FT + t + 1)
                                eng.activation(gel[t % 2][:], conv[t % 2][:], ACT.Gelu_apprx_tanh
                                               ).then_inc(gelu_ready, 1)
                    if part == 0:
                        for t in range(KT):
                            split_weights(tile_chunk[index[(f"ffn{l}.out", part, t)]] + 2)
                out_second(f"ffn{l}.out", 1)

            ffn(0)
            act.wait_ge(mod_ready, 4)
            shift(1, 0, tmp_o, xo)
            empty(("og_rows",), grow[0][0:16, :], ACT.Identity, part=(slice(64, 80), slice(0, S)), bias=bf[0:16, 1:2])
            act.wait_ge(gates_moved, 16)
            log_of(grow[1][0:8, :], grow[2][0:8, :], g_log)
            for t in range(KT):
                empty(("odd.qk", t), qk_raw[:, t, 3:3 + S])
            act.wait_ge(m_ready, 1)
            eng.activation(grow[7][0:8, :], grow[6][0:8, :], ACT.Exp, scale=-1.0).then_inc(floor_rows, 1)
            for s in range(4):
                for b in range(NB):
                    empty(("odd.v", s, b), vo[:, b, CHUNK * s:CHUNK * (s + 1)], part=half_bank)
            for t in range(KT):
                act.wait_ge(qk_conv, t + 1)
                eng.activation(qkc[:, t, :], qkc[:, t, :], ACT.Silu).then_inc(qk_silu, 1)
            for t in range(KT):
                empty(("odd.og", t), og[:, t, :], ACT.Sigmoid)
            split_weights(mark["mlstm"] + 2)
            wait_emptied(act, ("gcol",))
            def head_square(h):
                wait_emptied(act, ("num", h))
                if h >= 4:
                    peek(act, ("ms", h - 4))
                eng.activation(hsq[:, h % 4, :], ho[:, h, :], ACT.Square).then_inc(sq_heads, 1)

            for h in range(ML_HEADS):
                b = take(act, ("mb", h), "act")
                if h >= 2:
                    peek(act, ("num", h - 2))
                for j in range(NB):
                    ins = eng.activation(dec[h % 2][:, OFF[j]:OFF[j] + WIDE[j]], b[:, j * P:S], ACT.Relu,
                                         bias=ngcol[:, j, h:h + 1])
                ins.then_inc(emptied["act"], 1)
                wait_emptied(act, ("mb", h))
                eng.activation(dec[h % 2][:], dec[h % 2][:], ACT.Exp, scale=-1.0).then_inc(dec_exp, 1)
                if h >= 2:
                    wait_emptied(act, ("den", h - 2))
                empty(("eb", h), floor_b[h % 2][:])
                if h >= 1:
                    head_square(h - 1)
            head_square(ML_HEADS - 1)
            for h in range(ML_HEADS):
                act.wait_ge(head_inv, HG_HEADS + h + 1)
                eng.activation(hrs[h], hrs[h], ACT.Sqrt).then_inc(rstd_heads, 1)
            for t in range(KT):
                act.wait_ge(y_heads, HG_HEADS + t + 1)
                high(og[:, t, :], yo[0][:, t, :])
            out_second("odd_out")
            shift(1, 3, tmp_f, xf)
            ffn(1)

        @block.vector
        def _(eng):
            dve = Engine(eng)
            chain = Chain(eng, dve_step)
            used = {"sq": 0, "norm": 0, "ada": 0, "x": 0}
            ada_at = [n for n, c in enumerate(plan) if c[0] == "ada"]

            def ada_steps(count):
                for _ in range(count):
                    j = used["ada"]
                    n = ada_at[j]
                    w = ring[:, n % RING, :].rearrange("p (t n) -> p t n", t=KT)
                    dve.wait_ge(cs_ready, 1)
                    dve.wait_ge(landed[n % RING], landing[n])
                    if j >= ACC:
                        dve.wait_ge(ada_summed, j - ACC + 1)
                    s = acc[:, j % ACC, :]
                    chain.link(eng.tensor_scalar(s, w[:, 0, :], cs[:, 0:1], None, ALU.mult))
                    for k in range(1, KT):
                        ins = eng.scalar_tensor_tensor(out=s, in0=w[:, k, :], scalar=cs[:, k:k + 1], in1=s,
                                                       op0=ALU.mult, op1=ALU.add)
                        if k < KT - 1:
                            chain.link(ins)
                        else:
                            ins.then_inc(ada_done, 1)
                    used["ada"] += 1

            def inverse(count, width, n=S):
                k = used["norm"]
                used["sq"] += count
                dve.wait_ge(sq_used, used["sq"])
                dve.wait_ge(rstd_ready, k)
                eng.tensor_scalar(var[:, 0:n], ssq_bank[:, 0:n], 1.0 / width, EPS, ALU.mult, ALU.add
                                  ).then_inc(ssq_taken, 1)
                dve.wait_ge(ssq_taken, k + 1)
                eng.reciprocal(var[:, 0:n], var[:, 0:n]).then_inc(var_ready, 1)
                used["norm"] += 1

            def normed(count, width, src, dst, gains, ready, n=S):
                inverse(count, width, n)
                dve.wait_ge(rstd_ready, used["norm"])
                for t, g in enumerate(gains):
                    eng.scalar_tensor_tensor(out=dst[:, t, 0:n], in0=src[:, t, 0:n], scalar=g, in1=rstd[:, 0:n],
                                             op0=ALU.mult, op1=ALU.mult).then_inc(ready, 1)

            def low(src, dst, shift=None):
                used["x"] += 1
                dve.wait_ge(xh_ready, used["x"])
                hi, lo = dst
                hi = hi.bitcast(F32)
                if shift is None:
                    eng.tensor_tensor(lo, src, hi, ALU.subtract).then_inc(xl_ready, 1)
                else:
                    eng.scalar_tensor_tensor(out=lo, in0=src, scalar=shift, in1=hi, op0=ALU.add, op1=ALU.subtract
                                             ).then_inc(xl_ready, 1)

            def lows(src, dst, kts):
                for t in range(kts):
                    low(src[:, t, :], (dst[0][:, t, :], dst[1][:, t, :]))

            def normed_split(gains, tmp, dst, shifts=None):
                inverse(KT, D)
                dve.wait_ge(rstd_ready, used["norm"])

                def tail(t):
                    low(tmp[:, t % 2, :], (dst[0][:, t, :], dst[1][:, t, :]), None if shifts is None else shifts[t])

                for t, g in enumerate(gains):
                    if t >= 2:
                        dve.wait_ge(xl_ready, used["x"])
                    eng.scalar_tensor_tensor(out=tmp[:, t % 2, :], in0=x[:, t, :], scalar=g, in1=rstd[:, :],
                                             op0=ALU.mult, op1=ALU.mult).then_inc(scaled, 1)
                    if t >= 1:
                        tail(t - 1)
                tail(KT - 1)

            def empty(key, out, part=None):
                b = take(dve, key, "dve")
                eng.tensor_copy(out, b[:, :] if part is None else b[part]).then_inc(emptied["dve"], 1)

            for k in range(0, KT, 2):
                empty(("mT", k), mem_n[:, k:k + 2, :].rearrange("p k m -> p (k m)"))
            for k in range(KT):
                empty(("xT", k), x[:, k, :])
            for n in range(VEC_TILES):
                rows = max(r + k for t, r, k in VEC_ROWS.values() if t == n)
                empty(("vec", n), vecs[:, n * P:n * P + rows], (slice(0, P), slice(0, rows)))
            wait_emptied(dve, ("vec", VEC_TILES - 1))
            normed(4, D, mem_n, mem_n, [vec("mem_norm", t) for t in range(KT)], mem_normed, M)
            lows(mem_n, (mh, ml), KT)
            normed_split([vec("norm_pre", t) for t in range(KT)], tmp_a, xa)
            dve.wait_ge(loaded_p, 48)
            pr = posf[ropes, :]
            tr = turn[ropes, :]
            sr, cr = sin[ropes, :], cos[ropes, :]
            chain.link(eng.tensor_copy(pr, pos_i[ropes, :]))
            chain.link(eng.tensor_scalar(pr, pr, freq, None, ALU.mult))
            magic = 12582912.0
            chain.link(eng.tensor_scalar(tr, pr, float(1 / (2 * np.pi)), magic, ALU.mult, ALU.add))
            chain.link(eng.tensor_scalar(tr, tr, magic, None, ALU.subtract))
            rest = 2 * np.pi - 6.28125
            mid = float(np.float32(np.round(rest * 2 ** 20) / 2 ** 20))
            chain.link(eng.scalar_tensor_tensor(out=sr, in0=tr, scalar=-6.28125, in1=pr, op0=ALU.mult, op1=ALU.add))
            chain.link(eng.scalar_tensor_tensor(out=sr, in0=tr, scalar=-mid, in1=sr, op0=ALU.mult, op1=ALU.add))
            chain.link(eng.scalar_tensor_tensor(out=sr, in0=tr, scalar=-float(rest - mid), in1=sr, op0=ALU.mult,
                                                op1=ALU.add))
            lim = 3.1415925
            chain.link(eng.tensor_scalar(cr, sr, float(np.pi / 2), None, ALU.add))
            chain.link(eng.tensor_scalar(tr, cr, float(np.pi), 2 * float(np.pi), ALU.is_gt, ALU.mult))
            chain.link(eng.tensor_tensor(cr, cr, tr, ALU.subtract))
            eng.tensor_scalar(cr, cr, lim, -lim, ALU.min, ALU.max)
            eng.tensor_scalar(sr, sr, lim, -lim, ALU.min, ALU.max).then_inc(angle_ready, 1)
            dve.wait_ge(loaded_masks, 16)
            eng.tensor_copy(masks[:, :], masks_f[:, 0:(len(HG_LEVELS) + 1) * P]).then_inc(const_ready, 1)
            eng.tensor_copy(not_before[:, :], masks_f[:, (len(HG_LEVELS) + 1) * P:]).then_inc(const_ready, 1)
            eng.tensor_copy(identb[:, :], ident).then_inc(const_ready, 1)
            eng.tensor_copy(causal[:, :], consts[:, C_CAUSAL:C_CAUSAL + P]).then_inc(const_ready, 1)
            normed(3, Q_LORA, cq, cq, [vec("q_norm_a", t) for t in range(3)], cq_normed)
            lows(cq, cqs, 3)
            normed(2, KV_LORA, ckv, ckv, [vec("kv_norm_a", t) for t in range(2)], cq_normed)
            lows(ckv, ckvs, 2)

            def rotate(key, dst, par):
                b = take(dve, key, "dve")
                dve.wait_ge(sin_ready, 2)
                eng.tensor_tensor(rt[ropes, par, :], b[ropes, :], sr, ALU.mult).then_inc(emptied["dve"], 1)
                chain.link(eng.tensor_tensor(rt[ropes, 2 + par, :], dst, cr, ALU.mult))
                wait_emptied(dve, key)
                return eng.tensor_tensor(dst, rt[ropes, par, :], rt[ropes, 2 + par, :], ALU.add)

            dve.wait_ge(xl_ready, used["x"])
            rotate(("krot",), kr[ropes, :], 1).then_inc(kr_ready, 1)
            ada_steps(5)
            for h in range(HEADS):
                if h == 1:
                    dve.wait_ge(kr_ready, 1)
                if h >= 2:
                    dve.wait_ge(rope_done, h - 1)
                rotate(("qrot", h), qf[ropes, h, :], h % 2).then_inc(rope_done, 1)

            def attention(l):
                for h in range(16 + 2):
                    par = h % 2
                    if h < 16:
                        for i in range(NB):
                            n = (i + 1) * P if h < HEADS else M
                            scale = (MLA_SCALE, 1.0)[l] if h < HEADS else HD ** -0.5
                            b = peek(dve, ("s", l, h, i))
                            chain.link(eng.reduce_max(mx[:, par, i:i + 1], b[:, 0:n], AX_X))
                            eng.tensor_scalar(nmx[:, par, i:i + 1], mx[:, par, i:i + 1], -scale, None, ALU.mult
                                              ).then_inc(nmx_ready, 1)
                        wait_emptied(dve, ("s", l, h, NB - 1))
                        eng.reciprocal(rinv[:, par, :], rsum[:, par, :]).then_inc(rinv_ready, 1)
                        dve.wait_ge(rinv_ready, l * 16 + h + 1)
                        po, n = (6 * P, S) if h < HEADS else (3 * M, M)
                        w = probs[:, par, po:po + n]
                        eng.tensor_scalar(w, w, rinv[:, par, NB - 1:NB], None, ALU.mult).then_inc(last_ready, 1)
                    if 1 <= h <= 16:
                        transposed(eng, dve, l, h - 1, 1, "dve")
                    if h >= 2:
                        g = h - 2
                        b = take(dve, ("o", l, g), "dve")
                        rows = slice(HD * (g % 2), HD * (g % 2) + HD)
                        wait_emptied(dve, (("in_a.gate", "in_b.gate")[l], KT - 1))
                        ins = eng.tensor_tensor(gate[rows, g // 2, :], b[rows, :], gate[rows, g // 2, :], ALU.mult)
                        ins.then_inc(emptied["dve"], 1)

            attention(0)

            def out_first(l):
                lows(gate, ys, KT)
                ada_steps(3)
                inverse(KT, D)
                dve.wait_ge(rstd_ready, used["norm"])
                for t in range(KT):
                    eng.scalar_tensor_tensor(out=o1[:, t, :], in0=o1[:, t, :], scalar=vec("norm_post", KT * l + t),
                                             in1=rstd[:, :], op0=ALU.mult, op1=ALU.mult).then_inc(post_scaled, 1)

            out_first(0)
            normed_split([vec("norm_pre", KT + t) for t in range(KT)], tmp_b, xb)

            def log_sigmoid(z, t, lf, s_log):
                dve.wait_ge(s_log, 1)
                chain.link(eng.scalar_tensor_tensor(out=lf, in0=z, scalar=0.0, in1=t, op0=ALU.min, op1=ALU.subtract))

            wait_emptied(dve, ("f",))
            fr = [frow[0:HEADS, n, :] for n in range(6)]
            log_sigmoid(fr[0], fr[1], fr[2], f_log)
            chain.link(eng.memset(fr[5], 1.0))
            chain.link(eng.tensor_tensor_scan(fr[3], fr[5], fr[2], 0.0, ALU.mult, ALU.add))
            eng.tensor_scalar(fr[4], fr[3], -1.0, None, ALU.mult).then_inc(frows_ready, 1)
            ada_steps(13)
            attention(1)
            out_first(1)
            def modulation(l):
                half = slice(48 * l, 48 * l + 48)
                dve.wait_ge(ada_summed, 24 * (l + 1))
                chain.link(eng.tensor_tensor(mod[:, half], mod_bank[:, half], vecs[:, P + 48 * l:P + 48 * l + 48],
                                             ALU.add))
                for n, (part, name) in enumerate([(1, "norm_mix_g_2"), (4, "norm_ffn_g_2")]):
                    tile, row, _ = VEC_ROWS[name]
                    g = vecs[:, tile * P + row + 8 * l:tile * P + row + 8 * l + 8]
                    c = 48 * l + 8 * part
                    eng.scalar_tensor_tensor(out=gmod[:, 2 * l + n, :], in0=mod[:, c:c + 8], scalar=1.0, in1=g,
                                             op0=ALU.add, op1=ALU.mult).then_inc(mod_ready, 1)
                dve.wait_ge(mod_ready, 2 * (l + 1))

            modulation(0)

            def modulated(j, l, part, tmp, dst):
                c = 48 * l + 8 * part
                normed_split([gmod[:, j, t:t + 1] for t in range(KT)], tmp, dst,
                             [mod[:, c + t:c + t + 1] for t in range(KT)])

            modulated(0, 0, 0, tmp_e, xe)
            tile, row, _ = VEC_ROWS["hgrn_lb_2"]
            lb_in = vecs[:, tile * P + row:tile * P + row + 4]
            eng.tensor_tensor(lbt[:, 0, :], lb_in, lb_in, ALU.subtract).then_inc(lb_diff, 1)
            dve.wait_ge(lb_exp, 1)
            chain.link(eng.reciprocal(lbt[:, 2, :], lbt[:, 1, :]))
            chain.link(eng.tensor_tensor(lbt[:, 2, :], lbt[:, 1, :], lbt[:, 2, :], ALU.mult))
            chain.link(eng.tensor_tensor(lbt[:, 2, :], lbt[:, 2, :], lbt[:, 2, :], ALU.subtract))
            eng.tensor_scalar(lbt[:, 3, :], lbt[:, 2, :], -1.0, 1.0, ALU.mult, ALU.add).then_inc(lb_ready, 1)

            ada_steps(14)
            def masked(key, n, last=None):
                for h in range(HG_HEADS):
                    if last is not None:
                        wait_emptied(dve, last + (h,))
                    b = take(dve, key + (h,), "dve")
                    mk = masks[:, n * P:(n + 1) * P].unsqueeze(1).to_broadcast([P, NB, P])
                    eng.copy_predicated(at_d[:, h, :].rearrange("p (b t) -> p b t", b=NB), mk,
                                        b[:, :].rearrange("p (b t) -> p b t", b=NB)).then_inc(emptied["dve"], 1)

            def halves(v, half):
                u = v[:].rearrange("p h (n two m) -> p (h n) two m", two=2, m=half)
                return u[:, :, 0, :], u[:, :, 1, :]

            def level(n):
                half = 1 << n
                X = hx[n % 2]
                xl, xr = halves(X, half)
                kl, _ = halves(hk, half)
                _, qr = halves(hq, half)
                pbl, _ = halves(pb, half)
                _, pfr = halves(pf, half)
                dve.wait_ge(levels_up, n)
                if n >= 2:
                    peek(dve, ("lv", n - 2, HG_HEADS - 1))
                chain.step(eng.tensor_tensor(xl, kl, pbl, ALU.mult))
                eng.tensor_tensor(xr, qr, pfr, ALU.mult).then_inc(hx_ready, 1)

            dve.wait_ge(hg_ready, HG_HEADS)
            dve.wait_ge(hg_set, 2)
            wait_emptied(dve, ("even.qa", 3))
            level(0)
            masked(("diag",), 0)
            for n in range(len(HG_LEVELS)):
                level(n + 1)
                masked(("lv", n), n + 1, ("lv", n - 1) if n else ("diag",))
            n = len(HG_LEVELS)
            level(n + 1)
            for h in range(HG_HEADS):
                empty(("lv", n, h), at_1[:, h, :], (slice(0, P), slice(0, 256)))
            for h in range(HG_HEADS):
                empty(("lv", n + 1, h), at_2[:, h, :])

            def head_inverse(key, h, rs):
                b = take(dve, (key, h), "dve")
                eng.tensor_scalar(rs, b[:, :], 1.0 / P, EPS, ALU.mult, ALU.add).then_inc(emptied["dve"], 1)
                wait_emptied(dve, (key, h))
                eng.reciprocal(rs, rs).then_inc(head_inv, 1)

            def head_norms(base, count, src, rs, name, gated):
                for h in range(count):
                    dve.wait_ge(rstd_heads, base + h + 1)
                    chain.link(eng.scalar_tensor_tensor(out=src[:, h, :], in0=src[:, h, :], scalar=vec(name, h),
                                                        in1=rs[h], op0=ALU.mult, op1=ALU.mult))
                    eng.tensor_tensor(gated[:, h, :], gated[:, h, :], src[:, h, :], ALU.mult).then_inc(y_heads, 1)

            for h in range(HG_HEADS):
                wait_emptied(dve, ("ho", h))
            for h in range(HG_HEADS):
                head_inverse("hs", h, hx[0][:, h, :])
            head_norms(0, HG_HEADS, hk, [hx[0][:, h, :] for h in range(HG_HEADS)], "hgrn_norm_g_2", y2)
            for h in range(4):
                dve.wait_ge(soft_log, h + 1)
                if h >= 2:
                    dve.wait_ge(stick_sums, h - 1)
                for j in range(3):
                    b = peek(dve, ("z", h, j))
                    n = S if j == 0 else 384
                    c = slice(OFF[j], OFF[j] + n)
                    ins = eng.scalar_tensor_tensor(out=soft[h % 2][:, c], in0=b[:, 0:n], scalar=0.0, in1=lnb[:, c],
                                                   op0=ALU.max, op1=ALU.add)
                ins.then_inc(soft_ready, 1)

            def out_second(stage, l, part):
                for t in range(KT):
                    b = take(dve, stage + (t,), "dve")
                    col = 48 * l + 8 * part + t
                    eng.scalar_tensor_tensor(out=x[:, t, :], in0=b[:, :], scalar=mod[:, col:col + 1],
                                             in1=x[:, t, :], op0=ALU.mult, op1=ALU.add).then_inc(emptied["dve"], 1)

            lows(y2, ye, KT)
            out_second(("even_out",), 0, 2)
            modulated(1, 0, 3, tmp_f, xf)

            def ffn(l):
                name = f"ffn_conv_w_2/{l}"
                dve.wait_ge(pads, l + 1)

                def convolve(t):
                    i = l * FT + t
                    wait_emptied(dve, ("fa", l, t))
                    if i >= 2:
                        dve.wait_ge(gelu_ready, i - 1)
                    r, u = a_raw[t % 2], conv[t % 2][:]
                    chain.link(eng.tensor_scalar(u, r[:, 0:S], vec(name, t), vec("ffn_conv_b_2", FT * l + t),
                                                 ALU.mult, ALU.add))
                    chain.link(eng.scalar_tensor_tensor(out=u, in0=r[:, 1:1 + S], scalar=vec(name, FT + t),
                                                        in1=u, op0=ALU.mult, op1=ALU.add))
                    eng.scalar_tensor_tensor(out=u, in0=r[:, 2:2 + S], scalar=vec(name, 2 * FT + t), in1=u,
                                             op0=ALU.mult, op1=ALU.add).then_inc(conv_ready, 1)

                for part, (lo, hi) in enumerate(FFN_PARTS):
                    for t0 in range(lo, hi + 1, 2):
                        if t0 < hi:
                            convolve(t0)
                            convolve(t0 + 1)
                            if l == 0 and used["ada"] < 48:
                                ada_steps(1)
                        if t0 > lo:
                            for t in (t0 - 2, t0 - 1):
                                low(prod[:, t % 2, :], (hsp[0][:, t - lo, :], hsp[1][:, t - lo, :]))
                        if t0 < hi:
                            for t in (t0, t0 + 1):
                                b = take(dve, ("fg", l, t), "dve")
                                dve.wait_ge(gelu_ready, l * FT + t + 1)
                                dve.wait_ge(xl_ready, used["x"])
                                eng.tensor_tensor(prod[:, t % 2, :], b[:, :], gel[t % 2][:], ALU.mult
                                                  ).then_inc(emptied["dve"], 1)
                    if l == 0 and part == 1:
                        modulation(1)
                    out_second((f"ffn{l}.out", part), l, 5)

            ffn(0)
            modulated(2, 1, 0, tmp_o, xo)
            gr = [g[0:8, :] for g in grow]
            dve.wait_ge(gates_moved, 16)
            log_sigmoid(gr[1], gr[2], gr[3], g_log)
            chain.link(eng.memset(gr[2], 1.0))
            chain.link(eng.tensor_tensor_scan(gr[6], gr[2], gr[3], 0.0, ALU.mult, ALU.add))
            eng.tensor_tensor(gr[4], gr[0], gr[6], ALU.subtract).then_inc(grows_ready, 1)
            dve.wait_ge(grows_ready, 1)
            chain.link(eng.tensor_tensor_scan(gr[5], gr[2], gr[4], 0.0, ALU.mult, ALU.max))
            eng.tensor_tensor(gr[6], gr[6], gr[5], ALU.add).then_inc(m_ready, 1)
            def wcol(k, t):
                return vec("odd_conv_w_2", KT * k + t)

            dve.wait_ge(qk_pads, 1)
            for t in range(KT):
                wait_emptied(dve, ("odd.qk", t))
                u = qkc[:, t, :]
                chain.link(eng.tensor_scalar(u, qk_raw[:, t, 0:S], wcol(0, t), vec("odd_conv_b_2", t),
                                             ALU.mult, ALU.add))
                for k in range(1, 4):
                    ins = eng.scalar_tensor_tensor(out=u, in0=qk_raw[:, t, k:k + S], scalar=wcol(k, t), in1=u,
                                                   op0=ALU.mult, op1=ALU.add)
                    if k < 3:
                        chain.link(ins)
                    else:
                        ins.then_inc(qk_conv, 1)
            b = take(dve, ("gcol",), "dve")
            eng.tensor_scalar(ngcol.rearrange("p a b -> p (a b)"), b[:, 0:NB * ML_HEADS], -1.0, None, ALU.mult
                              ).then_inc(emptied["dve"], 1)
            for h in range(ML_HEADS + 1):
                if h < ML_HEADS:
                    dve.wait_ge(dec_masked, h + 1)
                    W = dec[h % 2]
                    for j in range(3):
                        b = take(dve, ("qk", h, j), "dve")
                        n = S if j == 0 else 384
                        c = slice(OFF[j], OFF[j] + n)
                        eng.scalar_tensor_tensor(out=W[:, c], in0=b[:, 0:n], scalar=64.0 ** -0.5, in1=W[:, c],
                                                 op0=ALU.mult, op1=ALU.mult).then_inc(emptied["dve"], 1)
                if h >= 1:
                    g = h - 1
                    b = take(dve, ("den", g), "dve")
                    wait_emptied(dve, ("eb", g))
                    chain.link(eng.tensor_tensor(den[:], b[:, :], floor_b[g % 2][:], ALU.max))
                    eng.scalar_tensor_tensor(out=den[:], in0=b[:, :], scalar=-1.0, in1=den[:], op0=ALU.mult, op1=ALU.max
                                             ).then_inc(emptied["dve"], 1)
                    wait_emptied(dve, ("den", g))
                    if g >= 1:
                        wait_emptied(dve, ("num", g - 1))
                    chain.link(eng.reciprocal(deni[:], den[:]))
                    b = take(dve, ("num", g), "dve")
                    eng.tensor_tensor(ho[:, g, :], b[:, :], deni[:], ALU.mult).then_inc(emptied["dve"], 1)
                if h >= 2:
                    head_inverse("ms", h - 2, hrs[h - 2])
            head_inverse("ms", ML_HEADS - 1, hrs[ML_HEADS - 1])
            head_norms(HG_HEADS, ML_HEADS, ho, hrs, "odd_norm_g_2", og)
            lows(og, yo, KT)
            out_second(("odd_out",), 1, 2)
            modulated(3, 1, 3, tmp_f, xf)
            ffn(1)
            normed(KT, D, x, out_n, [vec("final_g_2", t) for t in range(KT)], out_normed)
            for j in range(NB):
                for half in range(2):
                    empty(("out", j, half), out_tok[:, j, half * S:(half + 1) * S])

        @block.gpsimd
        def _(eng):
            pool = Engine(eng)
            low_done = [0]
            pe_at = [n for n, c in enumerate(plan) if c[0] != "ada"]

            def low_weights(upto):
                while low_done[0] < min(upto, len(released)):
                    m = low_done[0]
                    n = pe_at[m]
                    w = plan[n][2] * plan[n][3]
                    pool.wait_ge(wh_ready, m + 1)
                    eng.tensor_tensor(wl[:, m % SPLIT, 0:w], ring[:, n % RING, 0:w],
                                      wh[:, m % SPLIT, 0:w].bitcast(F32), ALU.subtract).then_inc(wl_ready, 1)
                    low_done[0] += 1

            load_vectors(eng, 1)
            low_weights(tile_chunk[index[("in_a.gate", KT - 1)]] + 2)
            peek(pool, ("in_a.gate", KT - 1))
            pool.wait_ge(kr_ready, 1)
            eng.dma_start(kf[ropes, :, :], kr[ropes, :].unsqueeze(1).to_broadcast([ROPE, HEADS, S])
                          ).then_inc(kf_ready, 16)

            def attention(l):
                low_weights(mark[f"att{l}"] + 2)
                for h in range(16):
                    par = h % 2
                    pool.wait_ge(rinv_ready, l * 16 + h + 1)
                    for i in range(NB - 1):
                        n = (i + 1) * P if h < HEADS else M
                        po = P * (i * (i + 1) // 2) if h < HEADS else i * M
                        w = probs[:, par, po:po + n]
                        eng.tensor_scalar(w, w, rinv[:, par, i:i + 1], None, ALU.mult).then_inc(probs_ready, 1)

            def add_x(l):
                low_weights(tile_chunk[index[(("out_a", "out_b")[l], KT - 1)]] + 2)
                for t in range(KT):
                    pool.wait_ge(post_scaled, l * KT + t + 1)
                    eng.tensor_tensor(x[:, t, :], x[:, t, :], o1[:, t, :], ALU.add).then_inc(x_ready, 1)

            attention(0)
            add_x(0)
            pool.wait_ge(xl_ready, SPLIT_AT["x_b"] + KT)
            eng.memset(qf[HD:HD + 2, :, :], 1.0).then_inc(frows_set, 1)
            eng.memset(kf[HD:HD + 2, :, :], 1.0).then_inc(frows_set, 1)
            pool.wait_ge(frows_set, 2)
            low_weights(tile_chunk[index[("in_b.qm", 0)]] + 2)
            pool.wait_ge(frows_ready, 1)
            for h in range(HEADS):
                eng.dma_start(qf[HD:HD + 1, h, :], frow[h:h + 1, 3, :]).then_inc(frows_moved, 16)
                eng.dma_start(kf[HD + 1:HD + 2, h, :], frow[h:h + 1, 4, :]).then_inc(frows_moved, 16)
            attention(1)
            add_x(1)
            pool.wait_ge(lb_ready, 1)
            for h in range(HG_HEADS):
                low_weights(tile_chunk[index[("even.fa", h)]] + 2)
                wait_emptied(pool, ("even.fa", h))
                eng.tensor_scalar(pf[:, h, :], pf[:, h, :], lbt[:, 3, h:h + 1], lbt[:, 2, h:h + 1], ALU.mult, ALU.add)
                eng.tensor_scalar(hk[:, h, :], hk[:, h, :], lbt[:, 3, h:h + 1], None, ALU.mult).then_inc(hg_ready, 1)
            low_weights(mark["hgrn"] + 2)
            peek(pool, ("even.vb", 1, NB - 1))
            eng.memset(pb[:, :, :], 1.0).then_inc(hg_set, 1)
            eng.memset(at_d[:, :, :], 0.0).then_inc(hg_set, 1)
            pool.wait_ge(hg_ready, HG_HEADS)
            pool.wait_ge(hg_set, 2)
            for n in range(8):
                half = 1 << n
                u = pf[:].rearrange("p h (n two m) -> p (h n) two m", two=2, m=half)
                v = pb[:].rearrange("p h (n two m) -> p (h n) two m", two=2, m=half)
                pool.wait_ge(hx_ready, n + 1)
                shape = [P, HG_HEADS * S // (2 * half), half]
                eng.tensor_tensor(v[:, :, 0, :], v[:, :, 0, :], u[:, :, 1, half - 1:half].to_broadcast(shape),
                                  ALU.mult).then_inc(pool_step, 1)
                pool.wait_ge(pool_step, n + 1)
                eng.tensor_tensor(u[:, :, 1, :], u[:, :, 1, :], u[:, :, 0, half - 1:half].to_broadcast(shape),
                                  ALU.mult).then_inc(levels_up, 1)
                pool.wait_ge(levels_up, n + 1)

            def triangle(v, op, last):
                for j in range(NB):
                    d = v[:, OFF[j]:OFF[j] + P]
                    ins = eng.affine_select(out=d, in_=d, compare_op=op, fill=0.0, base=0, pattern=[[1, P]],
                                            channel_multiplier=-1)
                ins.then_inc(last, 1)

            for h in range(4):
                pool.wait_ge(soft_ready, h + 1)
                triangle(soft[h % 2], ALU.is_gt, soft_masked)
            def zero_pads(first):
                pool.wait_ge(scaled, first)
                for n in range(2):
                    ins = eng.memset(a_raw[n][:, 0:2], 0.0)
                ins.then_inc(pads, 1)

            low_weights(tile_chunk[index[("even_out", KT - 1)]] + 2)
            zero_pads(3 * KT + 1)
            low_weights(tile_chunk[index[("ffn0.out", 1, KT - 1)]] + 2)
            pool.wait_ge(scaled, 4 * KT + 1)
            eng.memset(qk_raw[:, :, 0:3], 0.0).then_inc(qk_pads, 1)
            low_weights(tile_chunk[index[("og_rows",)]] + 2)
            wait_emptied(pool, ("og_rows",))
            eng.dma_start(grow[1][0:8, :], grow[0][8:16, :]).then_inc(gates_moved, 16)
            low_weights(mark["mlstm"] + 2)
            for h in range(ML_HEADS):
                pool.wait_ge(dec_exp, h + 1)
                triangle(dec[h % 2], ALU.is_ge, dec_masked)
            low_weights(tile_chunk[index[("odd_out", KT - 1)]] + 2)
            zero_pads(5 * KT + 1)
            low_weights(len(released))


def kernel(**inputs):
    import concourse.bacc as bacc
    from concourse.bass_utils import run_bass_kernel_spmd as run

    arrays = {name: np.ascontiguousarray(v) for name, v in inputs.items()}
    arrays["const_f32"] = constants()
    nc = bacc.Bacc("TRN2", target_bir_lowering=False, num_devices=1)
    aps = {name: nc.dram_tensor(f"in_{name}", v.shape, mybir.dt.from_np(v.dtype), kind="ExternalInput").ap()
           for name, v in arrays.items()}
    out = nc.dram_tensor("out", (1, S, D), F32, kind="ExternalOutput").ap()
    two_block_kernel(nc, aps, out)
    r = run(nc, [{f"in_{name}": v for name, v in arrays.items()}], core_ids=[0])
    return r.results[0]["out"]
```

```python
from contextlib import ExitStack

import numpy as np

import concourse.bass as bass
from concourse import mybir

P = 128
S = 512
NB = S // P
D = 1024
KT = D // P
M = 256
DEPTH = 2
EPS = 1e-6
HEADS = 12
MEM_HEADS = 4
Q_LORA, KV_LORA, ROPE, NOPE = 384, 256, 32, 64
MLA_SCALE = float(NOPE + ROPE) ** -0.5
HD = 64
MAIN = HEADS * HD
FFN = 2816
FT = FFN // P
FFN_PARTS = [(0, 12), (12, 22)]
HG_HEADS = 4
ML_HEADS = 8
RING = 3
SPLIT = 2
CHUNK = 256
ROT = 6
POOL_ADDS = 5
ADA_FIRST = 26
ACC = 2

ALU = mybir.AluOpType
ACT = mybir.ActivationFunctionType
AX_X = mybir.AxisListType.X
F32 = mybir.dt.float32
BF16 = mybir.dt.bfloat16
F32R = mybir.dt.float32r
I32 = mybir.dt.int32
U8 = mybir.dt.uint8

WIDE = [S - P * j for j in range(NB)]
OFF = [0, 512, 896, 1152]
PACK = sum(WIDE)
TRI_BANK = [(0, 0), (1, 0), (2, 0), (2, 256)]

VEC_ROWS = {}
for _tile, _names in enumerate([
        [("c_2", 8), ("norm_pre", 16), ("norm_post", 16), ("mem_norm", 8), ("q_norm_a", 3), ("kv_norm_a", 2),
         ("norm_mix_g_2", 16), ("norm_ffn_g_2", 16), ("hgrn_norm_g_2", 4), ("odd_norm_g_2", 8), ("final_g_2", 8),
         ("odd_conv_b_2", 8), ("hgrn_lb_2", 4)],
        [("ada_b_2", 96), ("odd_conv_w_2", 32)],
        [("ffn_conv_b_2", 44), ("ffn_conv_w_2/0", 66)],
        [("ffn_conv_w_2/1", 66)]]):
    _at = 0
    for _n, _k in _names:
        VEC_ROWS[_n] = (_tile, _at, _k)
        _at += _k
VEC_TILES = 4

SPLIT_AT, _at = {}, 0
for _n, _k in [("mem", 8), ("x_a", 8), ("cq", 3), ("ckv", 2), ("y_a", 8), ("x_b", 8), ("y_b", 8), ("x_even", 8),
               ("y_even", 8), ("x_ffn0", 8), ("ffn0/0", 12), ("ffn0/1", 10), ("x_odd", 8), ("y_odd", 8),
               ("x_ffn1", 8), ("ffn1/0", 12), ("ffn1/1", 10)]:
    SPLIT_AT[_n] = _at
    _at += _k

C_ID, C_ONE, C_NINCL, C_NONE, C_CAUSAL, C_ROT, C_FREQ = 0, 128, 256, 384, 512, 640, 672
C_COLS = 673
HG_LEVELS = [1, 2, 4, 8, 16, 32, 64]


def constants():
    c = np.zeros((P, C_COLS), np.float32)
    i = np.arange(P)
    c[:, C_ID:C_ID + P] = np.eye(P)
    c[:, C_ONE:C_ONE + P] = 1.0
    c[:, C_NINCL:C_NINCL + P] = -(i[None, :] <= i[:, None]).astype(np.float32)
    c[:, C_NONE:C_NONE + P] = -1.0
    c[:, C_CAUSAL:C_CAUSAL + P] = np.where(i[None, :] <= i[:, None], 0.0, -1e30)
    half = ROPE // 2
    for r in range(half):
        c[NOPE + r + half, C_ROT + r] = -1.0
        c[NOPE + r, C_ROT + r + half] = 1.0
    freq = np.float32(10000.0) ** (-np.arange(half, dtype=np.float32) / np.float32(half))
    c[NOPE:NOPE + ROPE, C_FREQ] = np.concatenate([freq, freq])
    m = np.zeros((P, len(HG_LEVELS) + 1, P), np.float32)
    s, t = i[:, None], i[None, :]
    m[:, 0] = s == t
    for n, h in enumerate(HG_LEVELS):
        m[:, n + 1] = (s // (2 * h) == t // (2 * h)) & (s // h % 2 == 0) & (t // h % 2 == 1)
    before = np.where(t <= s, -1e30, 0.0).astype(np.float32)
    return np.concatenate([c, m.reshape(P, -1), before], axis=1)


def weight_plan(a):
    def k8(name, w, lo, hi):
        v = w.rearrange("(t p) n -> p t n", p=P)
        return [(name, v[:, :, c:min(c + CHUNK, hi)], KT, min(CHUNK, hi - c)) for c in range(lo, hi, CHUNK)]

    plan = []
    ada = [("ada", c[1], KT, CHUNK) for l in range(DEPTH) for c in k8("ada", a["ada_w_2"][l], 0, 6 * D)]

    def add(chunks, per=0):
        for n, c in enumerate(chunks):
            plan.append(c)
            for _ in range((n + 1) * per // len(chunks) - n * per // len(chunks)):
                plan.append(ada.pop(0))

    for l in range(DEPTH):
        add(k8(f"mem{l}", a["w_mem_kv"][l], 0, 512))
    w = a["w_in_a"][0]
    add(k8("in_a.cq", w, 0, 256) + k8("in_a.cq", w, 256, 512) + k8("in_a.kr", w, 512, 672)
        + k8("in_a.qm", w, 672, 928))
    add(k8("in_a.gate", w, 928, 1952), 6)
    q = a["w_q_up_a"][0].rearrange("(t p) n -> p t n", p=P)
    add([("q_up", q[:, :, n * 576:(n + 1) * 576], 3, 576) for n in range(2)])
    kv = a["w_kv_up_a"][0].rearrange("(t p) (h n) -> p t h n", p=P, n=NOPE + HD)
    add([("kv_up", kv[:, :, :, 0:NOPE], 2, MAIN), ("kv_up", kv[:, :, :, NOPE:NOPE + HD], 2, MAIN)])
    add(k8("out_a", a["w_out"][0], 0, D), 3)
    w = a["w_in_b"][0]
    add(k8("in_b.f", w, 3 * MAIN, 3 * MAIN + P))
    add(k8("in_b.v", w, 2 * MAIN, 3 * MAIN) + k8("in_b.qm", w, 2316, 2572) + k8("in_b.gate", w, 2572, 3596) + k8("in_b.q", w, 0, MAIN)
        + k8("in_b.k", w, MAIN, 2 * MAIN), 15)
    add(k8("out_b", a["w_out"][1], 0, D), 3)
    w = a["even_w_in_2"][0]
    for name, lo, per in (("qa", 0, 2), ("fa", 512, 2), ("ia", 1024, 2), ("ga", 1536, 0), ("qb", 2048, 0),
                          ("kb", 2560, 0), ("vb", 3072, 0)):
        add(k8("even." + name, w, lo, lo + 512), per)
    add(k8("even_out", a["even_w_out_2"][0], 0, D))

    def ffn(l):
        w = a["ffn_w_in_2"][l]
        v = a["ffn_w_out_2"][l].rearrange("(t p) n -> p t n", p=P)
        for lo, hi in FFN_PARTS:
            for x, g in zip(k8(f"ffn{l}.a", w, lo * P, hi * P), k8(f"ffn{l}.g", w, FFN + lo * P, FFN + hi * P)):
                add([x, g], min(len(ada), 1))
            half = (hi - lo) // 2
            for c in range(0, D, CHUNK):
                add([(f"ffn{l}.out", v[:, t:t + half, c:c + CHUNK], half, CHUNK) for t in (lo, lo + half)],
                    int(l == 0 and lo == 0))

    ffn(0)
    assert not ada
    w = a["odd_w_in_2"][0]
    add(k8("odd.gates", w, 3008, 3088) + k8("odd.qk", w, 0, 1024) + k8("odd.v", w, 1024, 2048)
        + k8("odd.og", w, 2048, 3072))
    add(k8("odd_out", a["odd_w_out_2"][0], 0, D))
    ffn(1)
    return plan


BLOCKS = [(0, 1), (2,), (3,)]


def keys(h, i):
    return (i + 1) * P if h < HEADS else M


def column(h, i):
    return keys(h, 0) if i == 1 else 0


def packed(h, i):
    return P * (i * (i + 1) // 2) if h < HEADS else i * M


class Engine:

    def __init__(self, eng):
        self.eng, self.seen = eng, {}

    def wait_ge(self, sem, value):
        if self.seen.get(sem.name, 0) < value:
            self.eng.wait_ge(sem, value)
            self.seen[sem.name] = value


class Chain:

    def __init__(self, eng, sem):
        self.eng, self.sem, self.n = eng, sem, 0

    def step(self, ins):
        ins.then_inc(self.sem, 1)
        self.n += 1

    def settle(self):
        self.eng.wait_ge(self.sem, self.n)

    def link(self, ins):
        self.step(ins)
        self.settle()


def two_block_kernel(nc, a, out):
    plan = weight_plan(a)
    landing = []
    for n, (_, src, kt, _) in enumerate(plan):
        landing.append((landing[n - RING] if n >= RING else 0) + 16 * (kt if len(src.shape) == 4 else 1))
    with ExitStack() as ctx:
        def sb(name, shape, dt=F32):
            return ctx.enter_context(nc.sbuf_tensor(name, shape, dt))

        def sem(name):
            return ctx.enter_context(nc.semaphore(name))

        banks = [ctx.enter_context(nc.psum_tensor(f"bank{n}", [P, S], F32)) for n in range(8)]
        ssq_bank, mod_bank = banks[ROT], banks[ROT + 1]

        x = sb("x", [P, KT, S])
        ring = sb("ring", [P, RING, KT * CHUNK])
        consts = sb("consts", [P, C_COLS])
        masks = sb("masks", [P, (len(HG_LEVELS) + 1) * P], U8)
        identb = sb("identb", [P, P], BF16)
        causal = sb("causal", [P, P], BF16)
        not_before = sb("not_before", [P, P], BF16)
        vecs = sb("vecs", [P, VEC_TILES * P])
        cs = sb("cs", [P, KT])
        acc = sb("acc", [P, ACC, CHUNK])
        mod = sb("mod", [P, 6 * KT * DEPTH])
        gmod = sb("gmod", [P, 4, KT])
        sq = sb("sq", [P, 2, S])
        var = sb("var", [P, S])
        rstd = var
        mx = sb("mx", [P, 2, NB])
        nmx = sb("nmx", [P, 2, NB])
        rsum = sb("rsum", [P, 2, NB])
        rinv = sb("rinv", [P, 2, NB])
        bf = sb("bf", [16, 2])
        lbt = sb("lbt", [P, 4, HG_HEADS])
        wh = sb("wh", [P, SPLIT, KT * CHUNK], F32R)
        wl = sb("wl", [P, SPLIT, KT * CHUNK], F32R)

        slab = sb("slab", [P, 120 * 256])
        base = nc.sbuf_base - 120 * 1024

        def at(name, kb, *shape, dt=F32):
            return nc.alloc_sbuf_tensor_at(name, [P, *shape], dt, offset=base + int(kb * 1024))

        def pair(name, kh, kl, *shape):
            return at(name + "h", kh, *shape, dt=F32R), at(name + "l", kl, *shape, dt=F32R)

        ident = consts[:, C_ID:C_ID + P]
        ones = consts[:, C_ONE:C_ONE + P]
        nincl = consts[:, C_NINCL:C_NINCL + P]
        nones = consts[:, C_NONE:C_NONE + P]
        ropes = slice(NOPE, NOPE + ROPE)
        rot = consts[ropes, C_ROT:C_ROT + ROPE]
        freq = consts[ropes, C_FREQ:C_FREQ + 1]

        sq_sum = at("sq_sum", 110, S)
        km = at("km", 112, DEPTH, 2, M)
        vm = at("vm", 116, DEPTH, 2, M)
        x_tok, m_tok, vec_tok = at("x_tok", 32, NB, D), at("m_tok", 48, 2, D), at("vec_tok", 56, VEC_TILES, P)
        masks_f = at("masks_f", 58, (len(HG_LEVELS) + 2) * P)
        mem_n = at("mem_n", 64, KT, M)
        mh, ml = pair("mem", 80, 88, KT, M)
        xa = pair("xa", 0, 16, KT, S)
        tmp_a = at("tmp_a", 106, 2, S)
        pos_i, posf, turn = at("pos_i", 96, S, dt=I32), at("posf", 98, S), at("turn", 100, S)
        cos, sin = at("cos", 102, S), at("sin", 104, S)
        cq, ckv = at("cq", 48, 3, S), at("ckv", 54, 2, S)
        cqs, ckvs, kr = pair("cqs", 80, 86, 3, S), pair("ckvs", 92, 96, 2, S), at("kr", 100, S)
        rt = at("rt", 48, 4, S)
        qf, kf = at("qf", 0, HEADS, S), at("kf", 24, HEADS, S)
        v1 = at("v1", 48, NB, MAIN)
        gate = at("gate", 60, KT, S)
        qm = at("qm", 76, 2, S)
        probs = at("probs", 80, 2, PACK)
        probsT = at("probsT", 90, 2, 4, S)
        o1 = at("o1", 0, KT, S)
        ys = pair("ys", 16, 32, KT, S)
        xb = pair("xb", 80, 96, KT, S)
        tmp_b = at("tmp_b", 76, 2, S)
        frow = at("frow", 24, 6, S)
        hq, hk, pf, va = (at(n, 8 * i, 4, S) for i, n in enumerate(("hq", "hk", "pf", "va")))
        y2 = at("y2", 32, KT, S)
        qb, kb, vb = (at(n, 48 + 8 * i, 4, S) for i, n in enumerate(("qb", "kb", "vb")))
        xe = pair("xe", 72, 88, KT, S)
        tmp_e = at("tmp_e", 104, 2, S)
        pb = at("pb", 104, HG_HEADS, S)
        hx = [at("hx0", 112, HG_HEADS, S), at("hx1", 64, HG_HEADS, S)]
        at_d, at_1, at_2 = at("at_d", 40, HG_HEADS, S), at("at_1", 104, HG_HEADS, 256), at("at_2", 16, HG_HEADS, S)
        soft = [at("soft0", 16, PACK), at("soft1", 72, PACK)]
        lnb = at("lnb", 24, PACK)
        stick = [at("stick0", 104, PACK), at("stick1", 77, PACK)]
        ye = pair("ye", 0, 16, KT, S)
        xf = pair("xf", 0, 16, KT, S)
        tmp_f = at("tmp_f", 32, 2, S)
        hsp = pair("hsp", 36, 60, 12, S)
        a_raw = [at("a_raw0", 84, S + 2), at("a_raw1", 86.5, S + 2)]
        conv = [at("conv0", 89, S), at("conv1", 91, S)]
        gel = [at("gel0", 93, S), at("gel1", 95, S)]
        prod = at("prod", 97, 2, S)
        xo = pair("xo", 0, 16, KT, S)
        tmp_o = at("tmp_o", 32, 2, S)
        yo = pair("yo", 0, 16, KT, S)
        qk_raw = at("qk_raw", 36, KT, S + 3)
        qkc = at("qkc", 53, KT, S)
        vo = at("vo", 69, NB, D)
        og = at("og", 85, KT, S)
        grow = [at(f"grow{n}", 112 + 2 * n if n < 4 else 101 + 2 * (n - 4), S) for n in range(8)]
        dec = [at("dec0", 0, PACK), at("dec1", 5, PACK)]
        floor_b = [at("floor0", 10, S), at("floor1", 12, S)]
        den, deni = at("den", 14, S), at("deni", 16, S)
        hsq = at("hsq", 18, 4, S)
        hrs = [v[:, n, :] for v in (at("hrs0", 27, 4, S), at("hrs1", 112, 4, S)) for n in range(4)]
        ngcol = at("ngcol", 26, NB, ML_HEADS)
        ho = at("ho", 36, KT, S)
        out_n, out_tok = at("out_n", 0, KT, S), at("out_tok", 16, NB, D)

        def vec(name, n=0):
            tile, row, _ = VEC_ROWS[name]
            return vecs[:, tile * P + row + n:tile * P + row + n + 1]

        loaded_x, loaded_m, loaded_masks = sem("loaded_x"), sem("loaded_m"), sem("loaded_masks")
        loaded_c, loaded_p = sem("loaded_constants"), sem("loaded_positions")
        loaded_v = [sem("vectors_by_act"), sem("vectors_by_pool"), sem("vectors_by_sync")]
        landed = [sem(f"chunk_landed{n}") for n in range(RING)]
        filled = sem("banks_filled")
        emptied = {"act": sem("emptied_by_act"), "dve": sem("emptied_by_dve"),
                   "scores": sem("scores_emptied_by_act")}
        sq_ready, sq_used, sq_added = sem("square_ready"), sem("square_summed"), sem("square_pair_added")
        ssq_taken, var_ready, rstd_ready = sem("ssq_taken"), sem("inverse_ready"), sem("rstd_ready")
        wh_ready, wl_ready, w_part = sem("weights_high_part"), sem("weights_low_part"), sem("chunk_part_used")
        xh_ready, xl_ready, scaled = sem("high_part"), sem("low_part"), sem("normed")
        x_ready, x_added = sem("x_tile_ready"), sem("x_added_by_dve")
        ada_done, ada_summed = sem("ada_partial"), sem("ada_summed")
        cs_ready, mod_ready, const_ready = sem("silu_c_ready"), sem("mod_ready"), sem("bf16_constants")
        nmx_ready, rinv_ready, probs_ready = sem("neg_max_ready"), sem("inverse_sum_ready"), sem("probs_ready")
        last_ready = sem("last_block_ready")
        angle_ready, sin_ready = sem("angle_ready"), sem("sin_ready")
        kr_ready, rope_done, kf_ready = sem("rotary_key_ready"), sem("rope_done"), sem("keys_ready")
        f_log, frows_ready, frows_moved = sem("forget_log"), sem("forget_rows"), sem("forget_rows_moved")
        frows_set = sem("unit_rows_set")
        dve_step, act_step = sem("dve_step"), sem("act_step")
        hx_ready, hg_ready = sem("level_ready"), sem("decay_ready")
        lb_diff, lb_exp, lb_ready, hg_set = (sem("lb_difference"), sem("lb_exp"), sem("lb_ready"), sem("hgrn_set"))
        soft_log, soft_ready, soft_masked = sem("softplus_log"), sem("softplus_ready"), sem("softplus_masked")
        stick_sums = sem("stick_sums")
        sq_heads, head_inv, rstd_heads, y_heads = (sem("head_squares"), sem("head_inverse"), sem("head_rstd"),
                                                   sem("head_output_ready"))
        gates_moved, g_log = sem("gates_moved"), sem("gate_log")
        grows_ready, m_ready = sem("gate_rows_ready"), sem("gate_maxima_ready")
        floor_rows, gated = sem("floor_rows"), sem("head_output_gated")
        dec_exp, dec_masked = sem("decay_exp"), sem("decay_masked")
        qk_conv, qk_silu, qk_pads, pads = sem("qk_conv"), sem("qk_ready"), sem("qk_pads"), sem("conv_pads")
        post_scaled, mem_normed, cq_normed = sem("post_scaled"), sem("mem_normed"), sem("cq_normed")
        conv_ready, gelu_ready = sem("conv_ready"), sem("gelu_ready")
        stored, out_normed = sem("stored"), sem("out_normed")

        tiles, index, chunks, rotation = [], {}, [], []
        released, tile_chunk, mark = [], [], {}

        def wait_emptied(eng, key):
            _, owner, nth, _ = tiles[index[key]]
            eng.wait_ge(emptied[owner], nth + 1)

        def load_vectors(eng, queue):
            for name, (tile, row, k) in list(VEC_ROWS.items())[queue::3]:
                base, _, l = name.partition("/")
                src = a[base][int(l)] if l else a[base]
                if len(src.shape) > 1:
                    dims = " ".join("abc"[:len(src.shape)])
                    src = src.rearrange(f"{dims} -> ({dims})")
                eng.dma_start(vec_tok[row:row + k, tile, :], src.rearrange("(r p) -> r p", p=P)).then_inc(
                    loaded_v[queue], 16)

        block = ctx.enter_context(nc.Block())

        @block.tensor
        def _(eng):
            pe = Engine(eng)
            owned = {"act": 0, "dve": 0, "scores": 0}
            counts = {"sq": 0, "sq_sum": 0, "ada": 0, "sum": 0, "hn": 0, "part": 0}

            def bank(key, owner):
                if len(rotation) >= ROT:
                    _, who, nth, _ = tiles[rotation[-ROT]]
                    pe.wait_ge(emptied[who], nth + 1)
                rotation.append(len(tiles))
                return opened(key, owner, banks[(len(rotation) - 1) % ROT])

            def side(key, owner, last):
                if last is None:
                    pe.wait_ge(ssq_taken, counts["hn"])
                else:
                    wait_emptied(pe, last)
                return opened(key, owner, ssq_bank)

            def opened(key, owner, b):
                index[key] = len(tiles)
                tiles.append((key, owner, owned[owner], b))
                tile_chunk.append(len(released) - 1)
                owned[owner] += 1
                return b

            def done(ins):
                ins.then_inc(filled, 1)

            def chunk(stage):
                n = len(chunks)
                name, _, kt, cols = plan[n]
                assert name == stage, (name, stage)
                chunks.append("pe")
                while len(chunks) < len(plan) and plan[len(chunks)][0] == "ada":
                    chunks.append("ada")
                    counts["ada"] += 1
                m = len(released)
                released.append(None)
                pe.wait_ge(wl_ready, m + 1)
                return m, [v[:, m % SPLIT, 0:kt * cols].rearrange("p (t n) -> p t n", t=kt) for v in (wh, wl)]

            def chunk_done(m, part=None):
                released[m] = (filled, len(tiles)) if part is None else (w_part, part)

            def ada_sums(lag):
                while counts["sum"] < counts["ada"] - lag:
                    j = counts["sum"]
                    pe.wait_ge(ada_done, j + 1)
                    if j >= ADA_FIRST:
                        pe.wait_ge(mod_ready, 2)
                    for half in range(2):
                        mm = eng.matmul(mod_bank[:, 2 * j + half:2 * j + half + 1],
                                        acc[:, j % ACC, half * P:(half + 1) * P], ones[:, 0:1], start=True, stop=True)
                    mm.then_inc(ada_summed, 1)
                    counts["sum"] += 1

            def three(o, ws, cols, xs, k, toks, first, last, swap=False):
                for i, (a_, b_) in enumerate(((0, 0), (0, 1), (1, 0))):
                    w, xx = ws[a_][:, k, cols], xs[b_][:, k, toks]
                    l_, r_ = (xx, w) if swap else (w, xx)
                    mm = eng.matmul(o, l_, r_, start=(first and i == 0), stop=(last and i == 2))
                return mm

            def features(key, owner, ws, cols, xs, kts, ready, n=S):
                b = bank(key, owner)
                for k in range(kts):
                    pe.wait_ge(xl_ready, SPLIT_AT[ready] + k + 1)
                    mm = three(b[0:cols.stop - cols.start, 0:n], ws, cols, xs, k, slice(0, n), k == 0, k == kts - 1)
                done(mm)

            def tokens(key, owner, ws, cols, xs, kts, blk, ready):
                b = bank(key, owner)
                pe.wait_ge(xl_ready, SPLIT_AT[ready] + kts)
                for k in range(kts):
                    mm = three(b[:, 0:cols.stop - cols.start], ws, cols, xs, k, slice(blk * P, (blk + 1) * P),
                               k == 0, k == kts - 1, swap=True)
                done(mm)

            def ssq(t, total):
                i = counts["sq"]
                pe.wait_ge(sq_ready, i + 1)
                if t == 0:
                    pe.wait_ge(ssq_taken, counts["hn"])
                    counts["hn"] += 1
                eng.matmul(ssq_bank[:, :], ones, sq[:, i % 2, :], start=(t == 0), stop=(t == total - 1)
                           ).then_inc(sq_used, 1)
                counts["sq"] += 1

            def ssq_summed():
                pe.wait_ge(ssq_taken, counts["hn"])
                counts["hn"] += 1
                counts["sq"] += KT - 2
                counts["sq_sum"] += 3
                pe.wait_ge(sq_added, counts["sq_sum"])
                eng.matmul(ssq_bank[:, :], ones, sq_sum[:, :], start=True, stop=False).then_inc(sq_used, 1)
                for t in (KT - 2, KT - 1):
                    ssq(t, KT)

            def wide(keys, owner, ws, xs, kts, ready, n=S):
                bs = [bank(key, owner) for key in keys]
                for k in range(kts):
                    pe.wait_ge(xl_ready, SPLIT_AT[ready] + k + 1)
                    for t, b in enumerate(bs):
                        mm = three(b[:, 0:n], ws, slice(t * P, (t + 1) * P), xs, k, slice(0, n), k == 0, k == kts - 1)
                        if k == kts - 1:
                            done(mm)

            def project(stage, nchunks, owner, ready, xs, tok=False, lag=None):
                t = 0
                for _ in range(nchunks):
                    m, ws = chunk(stage)
                    cols = ws[0].shape[2]
                    if tok:
                        for b in range(NB):
                            tokens((stage, t, b), owner, ws, slice(0, cols), xs, KT, b, ready)
                        t += 1
                    elif cols == CHUNK:
                        wide([(stage, t), (stage, t + 1)], owner, ws, xs, KT, ready)
                        t += 2
                    else:
                        features((stage, t), owner, ws, slice(0, cols), xs, KT, ready)
                    chunk_done(m)
                    if lag is not None:
                        ada_sums(lag)

            pe.wait_ge(loaded_c, 16)
            pe.wait_ge(loaded_m, 16)
            for k in range(0, KT, 2):
                b = bank(("mT", k), "dve")
                for j in range(4):
                    t = eng.transpose(b[:, j * P:(j + 1) * P],
                                      m_tok[:, j % 2, (k + j // 2) * P:(k + j // 2 + 1) * P], ident)
                done(t)
            pe.wait_ge(loaded_x, 16)
            for k in range(KT):
                b = bank(("xT", k), "dve")
                for j in range(NB):
                    t = eng.transpose(b[:, j * P:(j + 1) * P], x_tok[:, j, k * P:(k + 1) * P], ident)
                done(t)
            for queue in range(3):
                pe.wait_ge(loaded_v[queue], 16 * len(list(VEC_ROWS)[queue::3]))
            for n in range(VEC_TILES):
                rows = max(r + k for t, r, k in VEC_ROWS.values() if t == n)
                b = bank(("vec", n), "dve")
                done(eng.transpose(b[:, 0:rows], vec_tok[0:rows, n, :], ident[0:rows, 0:rows]))
            for k in range(4):
                i = counts["sq"]
                pe.wait_ge(sq_ready, i + 1)
                eng.matmul(ssq_bank[:, 0:M], ones, sq[:, i % 2, 0:M], start=(k == 0), stop=False)
                eng.matmul(ssq_bank[:, 0:M], ones, sq[:, i % 2, M:2 * M], start=False, stop=(k == 3)
                           ).then_inc(sq_used, 1)
                counts["sq"] += 1
            counts["hn"] += 1
            for k in range(KT):
                ssq(k, KT)
            for l in range(DEPTH):
                m, ws = chunk(f"mem{l}")
                wide([("km", l, c) for c in range(2)], "act", ws, (mh, ml), KT, "mem", n=M)
                chunk_done(m)
                m, ws = chunk(f"mem{l}")
                for b in range(2):
                    tokens(("vm", l, b), "act", ws, slice(0, M), (mh, ml), KT, b, "mem")
                chunk_done(m)
                ada_sums(1)
            for c in range(2):
                m, ws = chunk("in_a.cq")
                wide([("cq", 2 * c + t) for t in range(2)], "act", ws, xa, KT, "x_a")
                chunk_done(m)
                ada_sums(1)
            m, ws = chunk("in_a.kr")
            features(("cq", 4), "act", ws, slice(0, P), xa, KT, "x_a")
            features(("kr",), "act", ws, slice(P - NOPE, P + ROPE), xa, KT, "x_a")
            chunk_done(m)
            ada_sums(1)
            project("in_a.qm", 1, "act", "x_a", xa, lag=1)
            for t in range(3):
                ssq(t, 3)
            for t in range(2):
                ssq(t, 2)
            b = bank(("krot",), "dve")
            wait_emptied(pe, ("kr",))
            done(eng.matmul(b[ropes, :], rot, kr[ropes, :], start=True, stop=True))
            project("in_a.gate", 4, "act", "x_a", xa, lag=1)
            h = 0
            for _ in range(2):
                m, ws = chunk("q_up")
                for j in range(6):
                    features(("q", h), "act", ws, slice(96 * j, 96 * (j + 1)), cqs, 3, "cq")
                    if h >= 1:
                        rotate = h - 1
                        b = bank(("qrot", rotate), "dve")
                        wait_emptied(pe, ("q", rotate))
                        done(eng.matmul(b[ropes, :], rot, qf[ropes, rotate, :], start=True, stop=True))
                    h += 1
                chunk_done(m)
            b = bank(("qrot", HEADS - 1), "dve")
            wait_emptied(pe, ("q", HEADS - 1))
            done(eng.matmul(b[ropes, :], rot, qf[ropes, HEADS - 1, :], start=True, stop=True))
            m, ws = chunk("kv_up")
            for t in range(6):
                features(("k", 2 * t), "act", ws, slice(t * P, (t + 1) * P), ckvs, 2, "ckv")
            chunk_done(m)
            m, ws = chunk("kv_up")
            for c in range(2):
                for blk in range(NB):
                    tokens(("v", c, blk), "act", ws, slice(384 * c, 384 * (c + 1)), ckvs, 2, blk, "ckv")
            chunk_done(m)
            mark["att0"] = len(released)

            def attention(l):
                def scores(h):
                    if h == HEADS:
                        wait_emptied(pe, (("in_a.qm", "in_b.qm")[l], 1))
                        wait_emptied(pe, ("km", l, 1))
                    for g, blocks in enumerate(BLOCKS):
                        b = bank(("s", l, h, g), "act")
                        for i in blocks:
                            kd, n, at_col = (NOPE + ROPE, HD + 2)[l], keys(h, i), column(h, i)
                            first, last = i == blocks[0], i == blocks[-1]
                            if h < HEADS:
                                eng.matmul(b[:, at_col:at_col + n], qf[0:kd, h, i * P:n], kf[0:kd, h, 0:n],
                                           start=first, stop=False, skip_group_check=True)
                                mm = eng.matmul(b[:, at_col + i * P:at_col + n], identb[:, :], causal[:, :],
                                                start=False, stop=last, skip_group_check=True)
                            else:
                                g_ = h - HEADS
                                rows = slice(HD * (g_ % 2), HD * (g_ % 2) + HD)
                                mm = eng.matmul(b[:, at_col:at_col + n], qm[rows, g_ // 2, i * P:(i + 1) * P],
                                                km[rows, l, g_ // 2, :], start=first, stop=last,
                                                skip_group_check=True)
                        done(mm)

                def transposes(h):
                    par = h % 2
                    for g, blocks in enumerate(BLOCKS):
                        b = bank(("t", l, h, g), "dve" if g == 2 else "act")
                        if g < 2:
                            pe.wait_ge(probs_ready, (l * 16 + h) * (NB - 1) + blocks[-1] + 1)
                        else:
                            pe.wait_ge(last_ready, l * 16 + h + 1)
                        for i in blocks:
                            for j in range(keys(h, i) // P):
                                src = packed(h, i) + j * P
                                to = column(h, i) + j * P
                                t = eng.transpose(b[:, to:to + P], probs[:, par, src:src + P], ident)
                        done(t)

                def apply(h):
                    par = h % 2
                    b = side(("o", l, h), "dve", ("o", l, h - 1) if h else None)
                    o = b[HD * par:HD * par + HD, :]
                    for g in range(3):
                        wait_emptied(pe, ("t", l, h, g))
                    nk = NB if h < HEADS else 2
                    for j in range(nk):
                        first = j * P if h < HEADS else 0
                        v = v1[:, j, h * HD:(h + 1) * HD] if h < HEADS else vm[:, l, j, (h - HEADS) * HD:(h - HEADS + 1) * HD]
                        mm = eng.matmul(o[:, first:S], v, probsT[:, par, j, first:S], start=(j == 0), stop=(j == nk - 1))
                    done(mm)

                for h in range(16 + 2):
                    if h < 16:
                        scores(h)
                    if 1 <= h <= 16:
                        transposes(h - 1)
                    if h >= 2:
                        apply(h - 2)

            pe.wait_ge(const_ready, 4)
            pe.wait_ge(kf_ready, 16)
            pe.wait_ge(rope_done, HEADS)
            for c in range(2):
                wait_emptied(pe, ("v", c, NB - 1))
            attention(0)

            def out_first(l):
                stage, ready = ("out_a", "out_b")[l], ("y_a", "y_b")[l]
                for c in range(4):
                    m, ws = chunk(stage)
                    if c < 3:
                        wide([(stage, 2 * c + t) for t in range(2)], "act", ws, ys, KT, ready)
                    else:
                        for t in range(2):
                            features((stage, 2 * c + t), "act", ws, slice(t * P, (t + 1) * P), ys, KT, ready)
                    chunk_done(m)
                    ada_sums(1)
                ssq_summed()
                for t in range(KT):
                    ssq(t, KT)

            out_first(0)
            m, ws = chunk("in_b.f")
            features(("f",), "act", ws, slice(0, P), xb, KT, "x_b")
            chunk_done(m)
            ada_sums(1)
            project("in_b.v", 3, "act", "x_b", xb, tok=True, lag=1)
            project("in_b.qm", 1, "act", "x_b", xb, lag=1)
            project("in_b.gate", 4, "act", "x_b", xb, lag=1)
            project("in_b.q", 3, "act", "x_b", xb, lag=1)
            project("in_b.k", 3, "act", "x_b", xb, lag=1)
            mark["att1"] = len(released)
            for s in range(3):
                wait_emptied(pe, ("in_b.v", s, NB - 1))
            pe.wait_ge(frows_moved, 16 * 2 * HEADS)
            attention(1)
            out_first(1)
            ada_sums(0)

            for name in ("qa", "fa"):
                project("even." + name, 2, "act", "x_even", xe, lag=1)
            project("even.ia", 2, "act", "x_even", xe, tok=True, lag=1)
            def level(name, lhs, rhs):
                for h in range(HG_HEADS):
                    b = bank(name + (h,), "dve")
                    for j in range(NB):
                        c = slice(j * P, (j + 1) * P)
                        mm = eng.matmul(b[:, c], lhs[:, h, c], rhs[:, h, c], start=(j == 0), stop=(j == NB - 1),
                                        skip_group_check=True)
                    done(mm)

            def diagonal():
                pe.wait_ge(hg_ready, HG_HEADS)
                level(("diag",), hk, hq)

            def inner(n):
                pe.wait_ge(hx_ready, n + 1)
                level(("lv", n), hx[n % 2], hx[n % 2])

            def outer(n):
                pe.wait_ge(hx_ready, n + 1)
                for h in range(HG_HEADS):
                    b = bank(("lv", n, h), "dve")
                    X = hx[n % 2]
                    if n == len(HG_LEVELS):
                        pairs = [(slice(0, P), 0, slice(P, 2 * P)), (slice(2 * P, 3 * P), P, slice(3 * P, S))]
                    else:
                        pairs = [(slice(0, P), 0, slice(M, S)), (slice(P, 2 * P), M, slice(M, S))]
                    for i, (keys, at_col, toks) in enumerate(pairs):
                        mm = eng.matmul(b[:, at_col:at_col + toks.stop - toks.start], X[:, h, keys], X[:, h, toks],
                                        start=(i == 0), stop=(i == 1), skip_group_check=True)
                    done(mm)

            steps = [(diagonal,)] + [(inner, n) for n in range(len(HG_LEVELS))]
            steps += [(outer, len(HG_LEVELS)), (outer, len(HG_LEVELS) + 1)]
            for name in ("ga", "qb", "kb"):
                for c in range(2):
                    m, ws = chunk("even." + name)
                    for t in range(2):
                        features(("even." + name, 2 * c + t), "act", ws, slice(t * P, (t + 1) * P), xe, KT, "x_even")
                        if t == 1:
                            chunk_done(m)
                        if steps and (name, c, t) != ("ga", 0, 0):
                            step = steps.pop(0)
                            step[0](*step[1:])
            assert not steps
            m, ws = chunk("even.vb")
            for blk in range(NB):
                tokens(("even.vb", 0, blk), "act", ws, slice(0, CHUNK), xe, KT, blk, "x_even")
            chunk_done(m)
            for h in range(HG_HEADS):
                b = bank(("ho", h), "act")
                wait_emptied(pe, ("lv", len(HG_LEVELS) + 1, h))
                hs = slice(h * P, (h + 1) * P)
                for j in range(NB):
                    c = slice(j * P, (j + 1) * P)
                    eng.matmul(b[:, c], va[:, j, hs], at_d[:, h, c], start=(j == 0), stop=False, skip_group_check=True)
                eng.matmul(b[:, P:2 * P], va[:, 0, hs], at_1[:, h, 0:P], start=False, stop=False, skip_group_check=True)
                eng.matmul(b[:, 3 * P:S], va[:, 2, hs], at_1[:, h, P:2 * P], start=False, stop=False,
                           skip_group_check=True)
                eng.matmul(b[:, M:S], va[:, 0, hs], at_2[:, h, 0:M], start=False, stop=False, skip_group_check=True)
                done(eng.matmul(b[:, M:S], va[:, 1, hs], at_2[:, h, M:S], start=False, stop=True,
                                skip_group_check=True))

            def stick_scores(h):
                wait_emptied(pe, ("even.kb", 3))
                for j in range(3):
                    zs[h % 2][j] = bank(("z", h, j), "scores")
                    for i in range(j, NB):
                        nb, c0 = TRI_BANK[i]
                        if nb == j:
                            mm = eng.matmul(zs[h % 2][j][:, c0:c0 + WIDE[i]], kb[:, h, i * P:(i + 1) * P],
                                            qb[:, h, i * P:S], start=(c0 == 0), stop=(i == NB - 1 or j < 2),
                                            skip_group_check=True)
                    done(mm)

            def stick_later_keys(h):
                pe.wait_ge(soft_masked, h + 1)
                sp = soft[h % 2]
                for j in range(NB):
                    src = sp[:, OFF[j]:OFF[j] + WIDE[j]]
                    nb, c0 = TRI_BANK[j]
                    eng.matmul(zs[h % 2][nb][:, c0:c0 + P], identb[:, :], not_before[:, :], start=False,
                               stop=False, skip_group_check=True)
                    mm = eng.matmul(zs[h % 2][nb][:, c0:c0 + WIDE[j]], nincl, src, start=False, stop=(j == NB - 1),
                                    skip_group_check=True)
                    for i in range(j):
                        nb, c0 = TRI_BANK[i]
                        lo = c0 + (j - i) * P
                        mm = eng.matmul(zs[h % 2][nb][:, lo:lo + WIDE[j]], nones, src, start=False,
                                        stop=(j == NB - 1), skip_group_check=True)
                mm.then_inc(stick_sums, 1)

            def stick_apply(h):
                b = side(("so", h), "act", ("so", h - 1) if h else ("hs", HG_HEADS - 1))
                wait_emptied(pe, ("z", h, 2))
                for j in range(NB):
                    mm = eng.matmul(b[:, j * P:S], vb[:, j, h * P:(h + 1) * P],
                                    stick[h % 2][:, OFF[j]:OFF[j] + WIDE[j]], start=(j == 0), stop=(j == NB - 1))
                done(mm)

            def head_squares(h):
                b = side(("hs", h), "dve", ("hs", h - 1) if h else None)
                pe.wait_ge(sq_heads, h + 1)
                done(eng.matmul(b[:, :], ones, hq[:, h, :], start=True, stop=True))

            zs = [[None] * 3 for _ in range(2)]
            stick_scores(0)
            m, ws = chunk("even.vb")
            for blk in range(NB):
                if blk == NB - 1:
                    stick_later_keys(0)
                    head_squares(0)
                tokens(("even.vb", 1, blk), "act", ws, slice(0, CHUNK), xe, KT, blk, "x_even")
            chunk_done(m)
            mark["hgrn"] = len(released)
            for h in range(1, HG_HEADS):
                head_squares(h)
            stick_scores(1)
            wait_emptied(pe, ("even.vb", 1, NB - 1))
            stick_apply(0)
            stick_scores(2)
            stick_later_keys(1)
            stick_scores(3)
            stick_apply(1)
            for h in (2, 3):
                stick_later_keys(h)
                stick_apply(h)

            def out_second(stage, parts, xs, ready, last=True):
                for c in range(4):
                    bs = [bank(stage + (2 * c + t,), "dve") for t in range(2)]
                    k0 = 0
                    for i in range(parts):
                        m, ws = chunk(stage[0])
                        tile_chunk[-1] = tile_chunk[-2] = m
                        kt = ws[0].shape[1]
                        order = [(k, t) for k in range(kt) for t in range(2)]
                        if c == 3 and i == parts - 1:
                            order.sort(key=lambda kt_: (kt_[1], kt_[0]))
                        for k, t in order:
                            pe.wait_ge(xl_ready, SPLIT_AT[ready] + k0 + k + 1)
                            for b in bs[t:t + 1]:
                                first, end = k0 + k == 0, (i == parts - 1 and k == kt - 1)
                                for j, (a_, b_) in enumerate(((0, 0), (0, 1), (1, 0))):
                                    mm = eng.matmul(b[:, :], ws[a_][:, k, t * P:(t + 1) * P], xs[b_][:, k0 + k, :],
                                                    start=(first and j == 0), stop=(end and j == 2))
                                if end:
                                    done(mm)
                        k0 += kt
                        if i < parts - 1:
                            mm.then_inc(w_part, 1)
                            counts["part"] += 1
                            chunk_done(m, counts["part"])
                        else:
                            chunk_done(m)
                    if counts["sum"] < 48:
                        ada_sums(1)
                if last:
                    ssq_summed()

            out_second(("even_out",), 1, ye, "y_even")

            def ffn(l):
                for part, (lo, hi) in enumerate(FFN_PARTS):
                    for t in range(lo, hi, 2):
                        for g, owner in (("a", "act"), ("g", "dve")):
                            m, ws = chunk(f"ffn{l}.{g}")
                            wide([("f" + g, l, t + i) for i in range(2)], owner, ws, xf, KT, f"x_ffn{l}")
                            chunk_done(m)
                            if l == 0:
                                ada_sums(1)
                    if l == 0 and part == 1:
                        ada_sums(0)
                    out_second((f"ffn{l}.out", part), 2, hsp, f"ffn{l}/{part}", last=(part == 1))

            ffn(0)
            m, ws = chunk("odd.gates")
            features(("og_rows",), "act", ws, slice(0, 80), xo, KT, "x_odd")
            chunk_done(m)
            project("odd.qk", 4, "act", "x_odd", xo)
            project("odd.v", 4, "act", "x_odd", xo, tok=True)
            project("odd.og", 4, "act", "x_odd", xo)
            mark["mlstm"] = len(released)
            pe.wait_ge(grows_ready, 1)
            b = bank(("gcol",), "dve")
            for j in range(NB):
                t = eng.transpose(b[:, j * ML_HEADS:(j + 1) * ML_HEADS], grow[4][0:8, j * P:(j + 1) * P],
                                  ident[0:8, 0:8])
            done(t)

            def ml_weights(h):
                pick = ident[0:8, h:h + 1].to_broadcast([8, P])
                b = bank(("mb", h), "act")
                done(eng.matmul(b[:, :], pick, grow[5][0:8, :], start=True, stop=True))
                b = bank(("eb", h), "act")
                pe.wait_ge(floor_rows, 1)
                done(eng.matmul(b[:, :], pick, grow[7][0:8, :], start=True, stop=True))
                rows = slice(64 * (h % 2), 64 * (h % 2) + 64)
                for j in range(3):
                    b = bank(("qk", h, j), "dve")
                    for i in range(j, NB):
                        nb, c0 = TRI_BANK[i]
                        if nb == j:
                            mm = eng.matmul(b[:, c0:c0 + WIDE[i]], qkc[rows, 4 + h // 2, i * P:(i + 1) * P],
                                            qkc[rows, h // 2, i * P:S], start=(c0 == 0), stop=(i == NB - 1 or j < 2),
                                            skip_group_check=True)
                    done(mm)

            def ml_apply(h):
                W = dec[h % 2]
                bd = bank(("den", h), "dve")
                wait_emptied(pe, ("qk", h, 2))
                for j in range(NB):
                    mm = eng.matmul(bd[:, j * P:S], ones, W[:, OFF[j]:OFF[j] + WIDE[j]], start=(j == 0),
                                    stop=(j == NB - 1))
                done(mm)
                bn = bank(("num", h), "dve")
                for j in range(NB):
                    mm = eng.matmul(bn[:, j * P:S], vo[:, j, h * P:(h + 1) * P], W[:, OFF[j]:OFF[j] + WIDE[j]],
                                    start=(j == 0), stop=(j == NB - 1))
                done(mm)

            def ml_squares(h):
                b = bank(("ms", h), "dve")
                pe.wait_ge(sq_heads, HG_HEADS + h + 1)
                done(eng.matmul(b[:, :], ones, hsq[:, h % 4, :], start=True, stop=True))

            pe.wait_ge(qk_silu, KT)
            wait_emptied(pe, ("odd.og", KT - 1))
            for h in range(ML_HEADS + 1):
                if h < ML_HEADS:
                    ml_weights(h)
                if h >= 1:
                    ml_apply(h - 1)
                if h >= 2:
                    ml_squares(h - 2)
            ml_squares(ML_HEADS - 1)
            out_second(("odd_out",), 1, yo, "y_odd")
            ffn(1)
            for half in range(2):
                for j in range(NB):
                    b = bank(("out", j, half), "dve")
                    pe.wait_ge(out_normed, KT // 2 * (half + 1))
                    for k in range(4):
                        t = eng.transpose(b[:, k * P:(k + 1) * P], out_n[:, 4 * half + k, j * P:(j + 1) * P], ident)
                    done(t)
            assert len(chunks) == len(plan)

        def take(eng, key, owner):
            n = index[key]
            assert tiles[n][1] == owner
            eng.wait_ge(filled, n + 1)
            return tiles[n][3]

        def peek(eng, key):
            n = index[key]
            eng.wait_ge(filled, n + 1)
            return tiles[n][3]

        def transposed(eng, who, l, h, owner):
            par = h % 2
            for g in (0, 1) if owner == "act" else (2,):
                b = take(who, ("t", l, h, g), owner)
                if h >= 2:
                    peek(who, ("o", l, h - 2))
                for i in BLOCKS[g]:
                    nk, c = keys(h, i) // P, column(h, i)
                    src = b[:, c:c + nk * P].rearrange("p (j q) -> p j q", q=P)
                    dst = probsT[:, par, 0:nk, i * P:(i + 1) * P]
                    ins = eng.activation(dst, src, ACT.Copy) if owner == "act" else eng.tensor_copy(dst, src)
                ins.then_inc(emptied[owner], 1)

        @block.sync
        def _(eng):
            sp = Engine(eng)
            eng.dma_start(consts[:, :], a["const_f32"][:, 0:C_COLS]).then_inc(loaded_c, 16)
            eng.dma_start(m_tok[:], a["mem"][0].rearrange("(b p) d -> p b d", p=P)).then_inc(loaded_m, 16)
            load_vectors(eng, 2)
            eng.dma_start(x_tok[:], a["x"][0].rearrange("(b p) d -> p b d", p=P)).then_inc(loaded_x, 16)
            eng.dma_start(masks_f[:], a["const_f32"][:, C_COLS:]).then_inc(loaded_masks, 16)
            for n, (name, src, kt, cols) in enumerate(plan):
                if n >= RING:
                    user = chunks[n - RING]
                    sp.wait_ge({"pe": wl_ready, "ada": ada_done}[user], chunks[:n - RING + 1].count(user))
                dst = ring[:, n % RING, 0:kt * cols].rearrange("p (t n) -> p t n", t=kt)
                if len(src.shape) == 4:
                    for t in range(kt):
                        eng.dma_start(dst[:, t, :].rearrange("p (h n) -> p h n", h=HEADS), src[:, t]
                                      ).then_inc(landed[n % RING], 16)
                    continue
                eng.dma_start(dst, src).then_inc(landed[n % RING], 16)
            for half in range(2):
                for j in range(NB):
                    wait_emptied(sp, ("out", j, half))
                    cols = slice(half * S, (half + 1) * S)
                    eng.dma_start(out[0, j * P:(j + 1) * P, cols], out_tok[:, j, cols]).then_inc(stored, 16)
            eng.wait_ge(stored, 16 * 2 * NB)

        @block.scalar
        def _(eng):
            act = Engine(eng)
            chain = Chain(eng, act_step)
            used = {"sq": 0, "norm": 0, "w": 0, "n": 0, "added": 0, "summed": 0}
            sq_free = []
            pe_at = [n for n, c in enumerate(plan) if c[0] != "ada"]

            load_vectors(eng, 0)
            eng.dma_start(bf[0:HEADS, 0:1], a["b_f"].rearrange("a h -> h a")).then_inc(loaded_p, 16)
            eng.dma_start(bf[0:16, 1:2], a["odd_gate_b_2"].rearrange("a h -> h a")).then_inc(loaded_p, 16)
            eng.dma_start(pos_i[ropes, :], a["positions"][0].partition_broadcast(ROPE)).then_inc(loaded_p, 16)

            def split_weights(upto):
                while used["w"] < min(upto, len(released)):
                    m = used["w"]
                    n = pe_at[m]
                    if m >= SPLIT:
                        act.wait_ge(*released[m - SPLIT])
                    act.wait_ge(landed[n % RING], landing[n])
                    w = plan[n][2] * plan[n][3]
                    eng.activation(wh[:, m % SPLIT, 0:w], ring[:, n % RING, 0:w], ACT.Copy).then_inc(wh_ready, 1)
                    used["w"] += 1

            def empty(key, out, func=ACT.Copy, part=None, owner="act", **kw):
                split_weights(tile_chunk[index[key]] + 2)
                b = take(act, key, owner)
                eng.activation(out, b[:, :] if part is None else b[part], func, **kw).then_inc(emptied[owner], 1)

            def high(src, dst, sem_in=None, value=0):
                if sem_in is not None:
                    act.wait_ge(sem_in, value)
                eng.activation(dst, src, ACT.Copy).then_inc(xh_ready, 1)

            def high_normed(tmp, dst, ts=range(KT)):
                for t in ts:
                    used["n"] += 1
                    high(tmp[:, t % 2, :], dst[0][:, t, :], scaled, used["n"])

            def square(src, t=None):
                i = used["sq"]
                if i >= 2:
                    act.wait_ge(*sq_free[i - 2])
                eng.activation(sq[:, i % 2, :], src, ACT.Square).then_inc(sq_ready, 1)
                used["sq"] += 1
                if t is not None and t < KT - 2:
                    used["added"] += (t % 2 == 0)
                    sq_free.append((sq_added, used["added"]))
                else:
                    used["summed"] += 1 + (t == KT - 2)
                    sq_free.append((sq_used, used["summed"]))

            def root(n=S):
                k = used["norm"]
                act.wait_ge(var_ready, k + 1)
                eng.activation(rstd[:, 0:n], var[:, 0:n], ACT.Sqrt).then_inc(rstd_ready, 1)
                used["norm"] += 1

            for k in range(4):
                wait_emptied(act, ("mT", 2 * k))
                square(mem_n[:, 2 * k:2 * k + 2, :])
            split_weights(2)
            for k in range(KT):
                wait_emptied(act, ("xT", k))
                square(x[:, k, :])
                if k == 1:
                    root(M)
            for t in range(KT):
                high(mem_n[:, t, :], mh[:, t, :], mem_normed, t + 1)
            root()
            high_normed(tmp_a, xa, range(2))
            for c in range(2):
                empty(("km", 0, c), km[:, 0, c, :], part=(slice(0, P), slice(0, M)))
            split_weights(3)
            high_normed(tmp_a, xa, range(2, KT))
            for b in range(2):
                empty(("vm", 0, b), vm[:, 0, b, :], part=(slice(0, P), slice(0, M)))
            split_weights(4)
            act.wait_ge(angle_ready, 1)
            eng.activation(sin[ropes, :], sin[ropes, :], ACT.Sin).then_inc(sin_ready, 1)
            eng.activation(cos[ropes, :], cos[ropes, :], ACT.Sin).then_inc(sin_ready, 1)
            for c in range(2):
                empty(("km", 1, c), km[:, 1, c, :], part=(slice(0, P), slice(0, M)))
            for b in range(2):
                empty(("vm", 1, b), vm[:, 1, b, :], part=(slice(0, P), slice(0, M)))
            for t in range(5):
                dst = cq[:, t, :] if t < 3 else ckv[:, t - 3, :]
                empty(("cq", t), dst)
            empty(("kr",), kr[ropes, :], part=(ropes, slice(0, S)))
            for t in range(2):
                empty(("in_a.qm", t), qm[:, t, :])
            for t in range(5):
                wait_emptied(act, ("cq", t))
                square(cq[:, t, :] if t < 3 else ckv[:, t - 3, :])
                if t == 2:
                    root()
            for t in range(3):
                high(cq[:, t, :], cqs[0][:, t, :], cq_normed, t + 1)
            root()
            for t in range(2):
                high(ckv[:, t, :], ckvs[0][:, t, :], cq_normed, 3 + t + 1)
            eng.activation(cs[:, :], vecs[:, 0:KT], ACT.Silu).then_inc(cs_ready, 1)
            act.wait_ge(const_ready, 2)
            for t in range(KT):
                empty(("in_a.gate", t), gate[:, t, :], ACT.Silu)
            for h in range(HEADS):
                empty(("q", h), qf[0:96, h, :], part=(slice(0, 96), slice(0, S)))
            for h in range(0, HEADS, 2):
                split_weights(tile_chunk[index[("k", h)]] + 2)
                b = take(act, ("k", h), "act")
                eng.activation(kf[0:NOPE, h, :], b[0:NOPE, :], ACT.Copy)
                eng.activation(kf[0:NOPE, h + 1, :], b[NOPE:P, :], ACT.Copy).then_inc(emptied["act"], 1)
            act.wait_ge(rope_done, HEADS)
            for c in range(2):
                for blk in range(NB):
                    empty(("v", c, blk), v1[:, blk, 384 * c:384 * (c + 1)], part=(slice(0, P), slice(0, 384)))

            def attention(l):
                split_weights(mark[f"att{l}"] + 2)
                for h in range(16 + 1):
                    if h < 16:
                        par = h % 2
                        scale = (MLA_SCALE, 1.0)[l] if h < HEADS else HD ** -0.5
                        for g, blocks in enumerate(BLOCKS):
                            b = take(act, ("s", l, h, g), "act")
                            act.wait_ge(nmx_ready, (l * 16 + h) * 3 + g + 1)
                            if h >= 2:
                                peek(act, ("t", l, h - 2, 2))
                            for i in blocks:
                                n, c, po = keys(h, i), column(h, i), packed(h, i)
                                ins = eng.activation(probs[:, par, po:po + n], b[:, c:c + n], ACT.Exp,
                                                     bias=nmx[:, par, i:i + 1], scale=scale,
                                                     accum_out=rsum[:, par, i:i + 1])
                            ins.then_inc(emptied["act"], 1)
                    if h >= 1:
                        transposed(eng, act, l, h - 1, "act")

            attention(0)

            def out_first(l):
                stage = ("out_a", "out_b")[l]
                for t in range(KT):
                    wait_emptied(act, ("o", l, 2 * t + 1))
                    high(gate[:, t, :], ys[0][:, t, :])
                for t in range(KT):
                    split_weights(tile_chunk[index[(stage, t)]] + 2)
                    b = take(act, (stage, t), "act")
                    square(b[:, :], t)
                    eng.activation(o1[:, t, :], b[:, :], ACT.Copy).then_inc(emptied["act"], 1)
                split_weights(tile_chunk[index[(stage, KT - 1)]] + 3)
                root()
                for t in range(KT):
                    if t < POOL_ADDS:
                        act.wait_ge(x_ready, l * POOL_ADDS + t + 1)
                    else:
                        act.wait_ge(x_added, l * (KT - POOL_ADDS) + t - POOL_ADDS + 1)
                    square(x[:, t, :])
                root()

            out_first(0)
            high_normed(tmp_b, xb)

            def log_of(z, rows, sem_out):
                chain.link(eng.activation(rows, z, ACT.Abs))
                chain.link(eng.activation(rows, rows, ACT.Exp, scale=-1.0))
                eng.activation(rows, rows, ACT.Ln, bias=1.0).then_inc(sem_out, 1)

            act.wait_ge(loaded_p, 48)
            empty(("f",), frow[0:HEADS, 0, :], ACT.Identity, part=(slice(0, HEADS), slice(0, S)), bias=bf[0:HEADS, 0:1])
            wait_emptied(act, ("f",))
            log_of(frow[0:HEADS, 0, :], frow[0:HEADS, 1, :], f_log)
            half_bank = (slice(0, P), slice(0, CHUNK))
            for s in range(3):
                for b in range(NB):
                    empty(("in_b.v", s, b), v1[:, b, CHUNK * s:CHUNK * (s + 1)], part=half_bank)
            for t in range(2):
                empty(("in_b.qm", t), qm[:, t, :])
            for t in range(KT):
                empty(("in_b.gate", t), gate[:, t, :], ACT.Silu)
                if t >= 2:
                    act.wait_ge(frows_set, 32)
                    act.wait_ge(frows_ready, 1)
                    for h in (2 * t - 4, 2 * t - 3):
                        eng.dma_start(qf[HD:HD + 1, h, :], frow[h:h + 1, 3, :]).then_inc(frows_moved, 16)
                        eng.dma_start(kf[HD + 1:HD + 2, h, :], frow[h:h + 1, 4, :]).then_inc(frows_moved, 16)
            for name, dst, scale in (("in_b.q", qf, HD ** -0.5), ("in_b.k", kf, 1.0)):
                if dst is kf:
                    act.wait_ge(frows_moved, 16 * 2 * HEADS)
                for t in range(6):
                    split_weights(tile_chunk[index[(name, t)]] + 2)
                    b = take(act, (name, t), "act")
                    eng.activation(dst[0:HD, 2 * t, :], b[0:HD, :], ACT.Copy, scale=scale)
                    eng.activation(dst[0:HD, 2 * t + 1, :], b[HD:P, :], ACT.Copy, scale=scale
                                   ).then_inc(emptied["act"], 1)
            attention(1)
            out_first(1)
            act.wait_ge(mod_ready, 2)

            def shift(l, part, tmp, dst):
                for t in range(KT):
                    used["n"] += 1
                    act.wait_ge(scaled, used["n"])
                    col = 48 * l + 8 * part + t
                    eng.activation(dst[0][:, t, :], tmp[:, t % 2, :], ACT.Identity, bias=mod[:, col:col + 1]
                                   ).then_inc(xh_ready, 1)

            shift(0, 0, tmp_e, xe)
            act.wait_ge(lb_diff, 1)
            eng.activation(lbt[:, 1, :], lbt[:, 0, :], ACT.Exp).then_inc(lb_exp, 1)
            for t in range(4):
                empty(("even.qa", t), hq[:, t, :])
            for t in range(4):
                split_weights(tile_chunk[index[("even.fa", t)]] + 2)
                b = take(act, ("even.fa", t), "act")
                eng.activation(pf[:, t, :], b[:, :], ACT.Sigmoid)
                eng.activation(hk[:, t, :], b[:, :], ACT.Sigmoid, scale=-1.0).then_inc(emptied["act"], 1)
            for s in range(2):
                for b in range(NB):
                    empty(("even.ia", s, b), va[:, b, CHUNK * s:CHUNK * (s + 1)], part=half_bank)
            for t in range(4):
                empty(("even.ga", t), y2[:, t, :], ACT.Silu)
            for t in range(4):
                empty(("even.qb", t), qb[:, t, :], scale=float(P) ** -0.5)
            for t in range(4):
                empty(("even.kb", t), kb[:, t, :])
            for b in range(NB):
                empty(("even.vb", 0, b), vb[:, b, 0:CHUNK], part=half_bank)
            for h in range(HG_HEADS):
                b = take(act, ("ho", h), "act")
                eng.activation(hq[:, h, :], b[:, :], ACT.Square).then_inc(sq_heads, 1)
                eng.activation(hk[:, h, :], b[:, :], ACT.Copy).then_inc(emptied["act"], 1)

            def stick_logs(h):
                if h >= 1:
                    act.wait_ge(soft_ready, h)
                for j in range(3):
                    b = peek(act, ("z", h, j))
                    n = S if j == 0 else 384
                    chain.step(eng.activation(lnb[:, OFF[j]:OFF[j] + n], b[:, 0:n], ACT.Abs))
                chain.settle()
                chain.link(eng.activation(lnb[:], lnb[:], ACT.Exp, scale=-1.0))
                eng.activation(lnb[:], lnb[:], ACT.Ln, bias=1.0).then_inc(soft_log, 1)

            def stick_weights(h):
                act.wait_ge(stick_sums, h + 1)
                for j in range(3):
                    n = S if j == 0 else 384
                    empty(("z", h, j), stick[h % 2][:, OFF[j]:OFF[j] + n], ACT.Exp, (slice(0, P), slice(0, n)), "scores")

            def stick_out(h):
                empty(("so", h), y2[:, 4 + h, :])

            stick_logs(0)
            for b in range(NB):
                if b == NB - 1:
                    stick_weights(0)
                empty(("even.vb", 1, b), vb[:, b, CHUNK:2 * CHUNK], part=half_bank)
            split_weights(mark["hgrn"] + 2)
            stick_logs(1)
            stick_out(0)
            stick_logs(2)
            for h in range(HG_HEADS):
                act.wait_ge(head_inv, h + 1)
                eng.activation(hx[0][:, h, :], hx[0][:, h, :], ACT.Sqrt).then_inc(rstd_heads, 1)
            stick_weights(1)
            stick_logs(3)
            stick_out(1)
            for h in (2, 3):
                stick_weights(h)
                stick_out(h)

            def out_second(*stage):
                for t in range(KT):
                    split_weights(tile_chunk[index[stage + (t,)]] + 2)
                    wait_emptied(act, stage + (t,))
                    square(x[:, t, :], t)
                split_weights(tile_chunk[index[stage + (KT - 1,)]] + 3)
                root()

            for t in range(KT):
                if t < 4:
                    act.wait_ge(y_heads, t + 1)
                else:
                    wait_emptied(act, ("so", t - 4))
                high(y2[:, t, :], ye[0][:, t, :])
            out_second("even_out")
            shift(0, 3, tmp_f, xf)

            def ffn(l):
                for part, (lo, hi) in enumerate(FFN_PARTS):
                    for t0 in range(lo, hi + 1, 2):
                        if t0 < hi:
                            for t in (t0, t0 + 1):
                                i = l * FT + t
                                if i >= 2:
                                    act.wait_ge(conv_ready, i - 1)
                                empty(("fa", l, t), a_raw[t % 2][:, 2:2 + S])
                        if t0 > lo:
                            for t in (t0 - 2, t0 - 1):
                                split_weights(tile_chunk[index[("fg", l, t)]] + 2)
                                wait_emptied(act, ("fg", l, t))
                                high(prod[:, t % 2, :], hsp[0][:, t - lo, :])
                        if t0 < hi:
                            split_weights(tile_chunk[index[("fa", l, t0)]] + 2)
                            for t in (t0, t0 + 1):
                                act.wait_ge(conv_ready, l * FT + t + 1)
                                eng.activation(gel[t % 2][:], conv[t % 2][:], ACT.Gelu_apprx_tanh
                                               ).then_inc(gelu_ready, 1)
                    if part == 0:
                        for t in range(KT):
                            split_weights(tile_chunk[index[(f"ffn{l}.out", part, t)]] + 2)
                out_second(f"ffn{l}.out", 1)

            ffn(0)
            act.wait_ge(mod_ready, 4)
            shift(1, 0, tmp_o, xo)
            empty(("og_rows",), grow[0][0:16, :], ACT.Identity, part=(slice(64, 80), slice(0, S)), bias=bf[0:16, 1:2])
            act.wait_ge(gates_moved, 16)
            log_of(grow[1][0:8, :], grow[2][0:8, :], g_log)
            for t in range(KT):
                empty(("odd.qk", t), qk_raw[:, t, 3:3 + S])
            act.wait_ge(m_ready, 1)
            eng.activation(grow[7][0:8, :], grow[6][0:8, :], ACT.Exp, scale=-1.0).then_inc(floor_rows, 1)
            for s in range(4):
                for b in range(NB):
                    empty(("odd.v", s, b), vo[:, b, CHUNK * s:CHUNK * (s + 1)], part=half_bank)
            for t in range(KT):
                act.wait_ge(qk_conv, t + 1)
                eng.activation(qkc[:, t, :], qkc[:, t, :], ACT.Silu).then_inc(qk_silu, 1)
            for t in range(KT):
                empty(("odd.og", t), og[:, t, :], ACT.Sigmoid)
            split_weights(mark["mlstm"] + 2)
            wait_emptied(act, ("gcol",))

            def head_square(h):
                wait_emptied(act, ("num", h))
                if h >= 4:
                    peek(act, ("ms", h - 4))
                eng.activation(hsq[:, h % 4, :], ho[:, h, :], ACT.Square).then_inc(sq_heads, 1)

            for h in range(ML_HEADS):
                b = take(act, ("mb", h), "act")
                if h >= 2:
                    peek(act, ("num", h - 2))
                for j in range(NB):
                    ins = eng.activation(dec[h % 2][:, OFF[j]:OFF[j] + WIDE[j]], b[:, j * P:S], ACT.Relu,
                                         bias=ngcol[:, j, h:h + 1])
                ins.then_inc(emptied["act"], 1)
                wait_emptied(act, ("mb", h))
                eng.activation(dec[h % 2][:], dec[h % 2][:], ACT.Exp, scale=-1.0).then_inc(dec_exp, 1)
                if h >= 2:
                    wait_emptied(act, ("den", h - 2))
                empty(("eb", h), floor_b[h % 2][:])
                if h >= 1:
                    head_square(h - 1)

            def head_root(h):
                act.wait_ge(head_inv, HG_HEADS + h + 1)
                eng.activation(hrs[h], hrs[h], ACT.Sqrt).then_inc(rstd_heads, 1)

            for h in range(ML_HEADS - 2):
                head_root(h)
            head_square(ML_HEADS - 1)
            for t in range(KT):
                if t >= ML_HEADS - 2:
                    head_root(t)
                act.wait_ge(y_heads, HG_HEADS + t + 1)
                high(og[:, t, :], yo[0][:, t, :])
            out_second("odd_out")
            shift(1, 3, tmp_f, xf)
            ffn(1)

        @block.vector
        def _(eng):
            dve = Engine(eng)
            chain = Chain(eng, dve_step)
            used = {"sq": 0, "norm": 0, "ada": 0, "x": 0, "squares": 0, "pairs": 0}
            ada_at = [n for n, c in enumerate(plan) if c[0] == "ada"]

            def ada_steps(count):
                for _ in range(count):
                    j = used["ada"]
                    n = ada_at[j]
                    w = ring[:, n % RING, :].rearrange("p (t n) -> p t n", t=KT)
                    dve.wait_ge(cs_ready, 1)
                    dve.wait_ge(landed[n % RING], landing[n])
                    if j >= ACC:
                        dve.wait_ge(ada_summed, j - ACC + 1)
                    s = acc[:, j % ACC, :]
                    chain.link(eng.tensor_scalar(s, w[:, 0, :], cs[:, 0:1], None, ALU.mult))
                    for k in range(1, KT):
                        ins = eng.scalar_tensor_tensor(out=s, in0=w[:, k, :], scalar=cs[:, k:k + 1], in1=s,
                                                       op0=ALU.mult, op1=ALU.add)
                        if k < KT - 1:
                            chain.link(ins)
                        else:
                            ins.then_inc(ada_done, 1)
                    used["ada"] += 1

            def add_squares(pair):
                i = used["squares"]
                dve.wait_ge(sq_ready, i + 2)
                if pair == 0:
                    ins = eng.tensor_tensor(sq_sum[:, :], sq[:, i % 2, :], sq[:, (i + 1) % 2, :], ALU.add)
                else:
                    dve.wait_ge(sq_added, used["pairs"])
                    chain.link(eng.tensor_tensor(sq_sum[:, :], sq_sum[:, :], sq[:, i % 2, :], ALU.add))
                    ins = eng.tensor_tensor(sq_sum[:, :], sq_sum[:, :], sq[:, (i + 1) % 2, :], ALU.add)
                ins.then_inc(sq_added, 1)
                used["pairs"] += 1
                used["squares"] += 2

            def inverse(count, width, n=S, squares=None):
                k = used["norm"]
                used["sq"] += count
                used["squares"] += count if squares is None else squares
                dve.wait_ge(sq_used, used["sq"])
                dve.wait_ge(rstd_ready, k)
                eng.tensor_scalar(var[:, 0:n], ssq_bank[:, 0:n], 1.0 / width, EPS, ALU.mult, ALU.add
                                  ).then_inc(ssq_taken, 1)
                dve.wait_ge(ssq_taken, k + 1)
                eng.reciprocal(var[:, 0:n], var[:, 0:n]).then_inc(var_ready, 1)
                used["norm"] += 1

            def normed(count, width, src, dst, gains, ready, n=S, squares=None):
                inverse(count, width, n, squares)
                dve.wait_ge(rstd_ready, used["norm"])
                for t, g in enumerate(gains):
                    eng.scalar_tensor_tensor(out=dst[:, t, 0:n], in0=src[:, t, 0:n], scalar=g, in1=rstd[:, 0:n],
                                             op0=ALU.mult, op1=ALU.mult).then_inc(ready, 1)

            def low(src, dst, shift=None):
                used["x"] += 1
                dve.wait_ge(xh_ready, used["x"])
                hi, lo = dst
                hi = hi.bitcast(F32)
                if shift is None:
                    eng.tensor_tensor(lo, src, hi, ALU.subtract).then_inc(xl_ready, 1)
                else:
                    eng.scalar_tensor_tensor(out=lo, in0=src, scalar=shift, in1=hi, op0=ALU.add, op1=ALU.subtract
                                             ).then_inc(xl_ready, 1)

            def lows(src, dst, kts):
                for t in range(kts):
                    low(src[:, t, :], (dst[0][:, t, :], dst[1][:, t, :]))

            def normed_split(gains, tmp, dst, shifts=None, summed=False):
                if summed:
                    inverse(3, D, squares=2)
                else:
                    inverse(KT, D)
                dve.wait_ge(rstd_ready, used["norm"])

                def tail(t):
                    low(tmp[:, t % 2, :], (dst[0][:, t, :], dst[1][:, t, :]), None if shifts is None else shifts[t])

                for t, g in enumerate(gains):
                    if t >= 2:
                        dve.wait_ge(xl_ready, used["x"])
                    eng.scalar_tensor_tensor(out=tmp[:, t % 2, :], in0=x[:, t, :], scalar=g, in1=rstd[:, :],
                                             op0=ALU.mult, op1=ALU.mult).then_inc(scaled, 1)
                    if t >= 1:
                        tail(t - 1)
                tail(KT - 1)

            def empty(key, out, part=None):
                b = take(dve, key, "dve")
                eng.tensor_copy(out, b[:, :] if part is None else b[part]).then_inc(emptied["dve"], 1)

            for k in range(0, KT, 2):
                empty(("mT", k), mem_n[:, k:k + 2, :].rearrange("p k m -> p (k m)"))
            for k in range(KT):
                empty(("xT", k), x[:, k, :])
            for n in range(VEC_TILES):
                rows = max(r + k for t, r, k in VEC_ROWS.values() if t == n)
                empty(("vec", n), vecs[:, n * P:n * P + rows], (slice(0, P), slice(0, rows)))
            wait_emptied(dve, ("vec", VEC_TILES - 1))
            normed(4, D, mem_n, mem_n, [vec("mem_norm", t) for t in range(KT)], mem_normed, M)
            lows(mem_n, (mh, ml), KT)
            normed_split([vec("norm_pre", t) for t in range(KT)], tmp_a, xa)
            dve.wait_ge(loaded_p, 48)
            pr = posf[ropes, :]
            tr = turn[ropes, :]
            sr, cr = sin[ropes, :], cos[ropes, :]
            chain.link(eng.tensor_copy(pr, pos_i[ropes, :]))
            chain.link(eng.tensor_scalar(pr, pr, freq, None, ALU.mult))
            magic = 12582912.0
            chain.link(eng.tensor_scalar(tr, pr, float(1 / (2 * np.pi)), magic, ALU.mult, ALU.add))
            chain.link(eng.tensor_scalar(tr, tr, magic, None, ALU.subtract))
            rest = 2 * np.pi - 6.28125
            mid = float(np.float32(np.round(rest * 2 ** 20) / 2 ** 20))
            chain.link(eng.scalar_tensor_tensor(out=sr, in0=tr, scalar=-6.28125, in1=pr, op0=ALU.mult, op1=ALU.add))
            chain.link(eng.scalar_tensor_tensor(out=sr, in0=tr, scalar=-mid, in1=sr, op0=ALU.mult, op1=ALU.add))
            chain.link(eng.scalar_tensor_tensor(out=sr, in0=tr, scalar=-float(rest - mid), in1=sr, op0=ALU.mult,
                                                op1=ALU.add))
            lim = 3.1415925
            chain.link(eng.tensor_scalar(cr, sr, float(np.pi / 2), None, ALU.add))
            chain.link(eng.tensor_scalar(tr, cr, float(np.pi), 2 * float(np.pi), ALU.is_gt, ALU.mult))
            chain.link(eng.tensor_tensor(cr, cr, tr, ALU.subtract))
            eng.tensor_scalar(cr, cr, lim, -lim, ALU.min, ALU.max)
            eng.tensor_scalar(sr, sr, lim, -lim, ALU.min, ALU.max).then_inc(angle_ready, 1)
            dve.wait_ge(loaded_masks, 16)
            eng.tensor_copy(masks[:, :], masks_f[:, 0:(len(HG_LEVELS) + 1) * P]).then_inc(const_ready, 1)
            eng.tensor_copy(not_before[:, :], masks_f[:, (len(HG_LEVELS) + 1) * P:]).then_inc(const_ready, 1)
            eng.tensor_copy(identb[:, :], ident).then_inc(const_ready, 1)
            eng.tensor_copy(causal[:, :], consts[:, C_CAUSAL:C_CAUSAL + P]).then_inc(const_ready, 1)
            normed(3, Q_LORA, cq, cq, [vec("q_norm_a", t) for t in range(3)], cq_normed)
            lows(cq, cqs, 3)
            normed(2, KV_LORA, ckv, ckv, [vec("kv_norm_a", t) for t in range(2)], cq_normed)
            lows(ckv, ckvs, 2)

            def rotate(key, dst, par):
                b = take(dve, key, "dve")
                dve.wait_ge(sin_ready, 2)
                eng.tensor_tensor(rt[ropes, par, :], b[ropes, :], sr, ALU.mult).then_inc(emptied["dve"], 1)
                chain.link(eng.tensor_tensor(rt[ropes, 2 + par, :], dst, cr, ALU.mult))
                wait_emptied(dve, key)
                return eng.tensor_tensor(dst, rt[ropes, par, :], rt[ropes, 2 + par, :], ALU.add)

            dve.wait_ge(xl_ready, used["x"])
            rotate(("krot",), kr[ropes, :], 1).then_inc(kr_ready, 1)
            ada_steps(6)
            for h in range(HEADS):
                if h == 1:
                    dve.wait_ge(kr_ready, 1)
                if h >= 2:
                    dve.wait_ge(rope_done, h - 1)
                rotate(("qrot", h), qf[ropes, h, :], h % 2).then_inc(rope_done, 1)

            def attention(l):
                for h in range(16 + 2):
                    par = h % 2
                    if h < 16:
                        scale = (MLA_SCALE, 1.0)[l] if h < HEADS else HD ** -0.5
                        for g, blocks in enumerate(BLOCKS):
                            b = peek(dve, ("s", l, h, g))
                            for i in blocks:
                                c = column(h, i)
                                chain.step(eng.reduce_max(mx[:, par, i:i + 1], b[:, c:c + keys(h, i)], AX_X))
                            chain.settle()
                            group = slice(blocks[0], blocks[-1] + 1)
                            eng.tensor_scalar(nmx[:, par, group], mx[:, par, group], -scale, None, ALU.mult
                                              ).then_inc(nmx_ready, 1)
                        wait_emptied(dve, ("s", l, h, 2))
                        eng.reciprocal(rinv[:, par, :], rsum[:, par, :]).then_inc(rinv_ready, 1)
                        dve.wait_ge(rinv_ready, l * 16 + h + 1)
                        po, n = packed(h, NB - 1), keys(h, NB - 1)
                        w = probs[:, par, po:po + n]
                        eng.tensor_scalar(w, w, rinv[:, par, NB - 1:NB], None, ALU.mult).then_inc(last_ready, 1)
                    if 1 <= h <= 16:
                        transposed(eng, dve, l, h - 1, "dve")
                    if h >= 2:
                        g = h - 2
                        b = take(dve, ("o", l, g), "dve")
                        rows = slice(HD * (g % 2), HD * (g % 2) + HD)
                        wait_emptied(dve, (("in_a.gate", "in_b.gate")[l], KT - 1))
                        ins = eng.tensor_tensor(gate[rows, g // 2, :], b[rows, :], gate[rows, g // 2, :], ALU.mult)
                        ins.then_inc(emptied["dve"], 1)

            attention(0)

            def out_first(l):
                lows(gate, ys, KT)
                for pair in range(3):
                    ada_steps(1)
                    add_squares(pair)
                inverse(3, D, squares=2)
                dve.wait_ge(rstd_ready, used["norm"])
                for t in range(KT):
                    eng.scalar_tensor_tensor(out=o1[:, t, :], in0=o1[:, t, :], scalar=vec("norm_post", KT * l + t),
                                             in1=rstd[:, :], op0=ALU.mult, op1=ALU.mult).then_inc(post_scaled, 1)
                for t in range(POOL_ADDS, KT):
                    dve.wait_ge(post_scaled, l * KT + t + 1)
                    eng.tensor_tensor(x[:, t, :], x[:, t, :], o1[:, t, :], ALU.add).then_inc(x_added, 1)

            out_first(0)
            normed_split([vec("norm_pre", KT + t) for t in range(KT)], tmp_b, xb)

            def log_sigmoid(z, t, lf, s_log):
                dve.wait_ge(s_log, 1)
                chain.link(eng.scalar_tensor_tensor(out=lf, in0=z, scalar=0.0, in1=t, op0=ALU.min, op1=ALU.subtract))

            wait_emptied(dve, ("f",))
            fr = [frow[0:HEADS, n, :] for n in range(6)]
            log_sigmoid(fr[0], fr[1], fr[2], f_log)
            chain.link(eng.memset(fr[5], 1.0))
            chain.link(eng.tensor_tensor_scan(fr[3], fr[5], fr[2], 0.0, ALU.mult, ALU.add))
            eng.tensor_scalar(fr[4], fr[3], -1.0, None, ALU.mult).then_inc(frows_ready, 1)
            ada_steps(15)
            attention(1)
            out_first(1)
            def modulation(l):
                half = slice(48 * l, 48 * l + 48)
                dve.wait_ge(ada_summed, (ADA_FIRST, 48)[l])
                chain.link(eng.tensor_tensor(mod[:, half], mod_bank[:, half], vecs[:, P + 48 * l:P + 48 * l + 48],
                                             ALU.add))
                for n, (part, name) in enumerate([(1, "norm_mix_g_2"), (4, "norm_ffn_g_2")]):
                    tile, row, _ = VEC_ROWS[name]
                    g = vecs[:, tile * P + row + 8 * l:tile * P + row + 8 * l + 8]
                    c = 48 * l + 8 * part
                    eng.scalar_tensor_tensor(out=gmod[:, 2 * l + n, :], in0=mod[:, c:c + 8], scalar=1.0, in1=g,
                                             op0=ALU.add, op1=ALU.mult).then_inc(mod_ready, 1)
                dve.wait_ge(mod_ready, 2 * (l + 1))

            modulation(0)

            def modulated(j, l, part, tmp, dst):
                c = 48 * l + 8 * part
                normed_split([gmod[:, j, t:t + 1] for t in range(KT)], tmp, dst,
                             [mod[:, c + t:c + t + 1] for t in range(KT)], summed=(j > 0))

            modulated(0, 0, 0, tmp_e, xe)
            tile, row, _ = VEC_ROWS["hgrn_lb_2"]
            lb_in = vecs[:, tile * P + row:tile * P + row + 4]
            eng.tensor_tensor(lbt[:, 0, :], lb_in, lb_in, ALU.subtract).then_inc(lb_diff, 1)
            dve.wait_ge(lb_exp, 1)
            chain.link(eng.reciprocal(lbt[:, 2, :], lbt[:, 1, :]))
            chain.link(eng.tensor_tensor(lbt[:, 2, :], lbt[:, 1, :], lbt[:, 2, :], ALU.mult))
            chain.link(eng.tensor_tensor(lbt[:, 2, :], lbt[:, 2, :], lbt[:, 2, :], ALU.subtract))
            eng.tensor_scalar(lbt[:, 3, :], lbt[:, 2, :], -1.0, 1.0, ALU.mult, ALU.add).then_inc(lb_ready, 1)

            ada_steps(6)
            def masked(key, n, last=None):
                for h in range(HG_HEADS):
                    if last is not None:
                        wait_emptied(dve, last + (h,))
                    b = take(dve, key + (h,), "dve")
                    mk = masks[:, n * P:(n + 1) * P].unsqueeze(1).to_broadcast([P, NB, P])
                    eng.copy_predicated(at_d[:, h, :].rearrange("p (b t) -> p b t", b=NB), mk,
                                        b[:, :].rearrange("p (b t) -> p b t", b=NB)).then_inc(emptied["dve"], 1)

            def halves(v, half):
                u = v[:].rearrange("p h (n two m) -> p (h n) two m", two=2, m=half)
                return u[:, :, 0, :], u[:, :, 1, :]

            def level(n):
                half = 1 << n
                X = hx[n % 2]
                xl, xr = halves(X, half)
                kl, _ = halves(hk, half)
                _, qr = halves(hq, half)
                pbl, _ = halves(pb, half)
                _, pfr = halves(pf, half)
                if n >= 2:
                    peek(dve, ("lv", n - 2, HG_HEADS - 1))
                chain.step(eng.tensor_tensor(xl, kl, pbl, ALU.mult))
                eng.tensor_tensor(xr, qr, pfr, ALU.mult).then_inc(hx_ready, 1)

            def double(n):
                half = 1 << n
                u = pf[:].rearrange("p h (n two m) -> p (h n) two m", two=2, m=half)
                v = pb[:].rearrange("p h (n two m) -> p (h n) two m", two=2, m=half)
                shape = [P, HG_HEADS * S // (2 * half), half]
                chain.settle()
                dve.wait_ge(hx_ready, n + 1)
                chain.link(eng.tensor_tensor(v[:, :, 0, :], v[:, :, 0, :], u[:, :, 1, half - 1:half].to_broadcast(shape),
                                             ALU.mult))
                chain.link(eng.tensor_tensor(u[:, :, 1, :], u[:, :, 1, :], u[:, :, 0, half - 1:half].to_broadcast(shape),
                                             ALU.mult))

            dve.wait_ge(hg_ready, HG_HEADS)
            dve.wait_ge(hg_set, 2)
            wait_emptied(dve, ("even.qa", 3))
            level(0)
            masked(("diag",), 0)
            for n in range(len(HG_LEVELS)):
                double(n)
                level(n + 1)
                masked(("lv", n), n + 1, ("lv", n - 1) if n else ("diag",))
            n = len(HG_LEVELS)
            double(n)
            level(n + 1)
            dve.wait_ge(hx_ready, n + 2)
            for h in range(HG_HEADS):
                empty(("lv", n, h), at_1[:, h, :], (slice(0, P), slice(0, 256)))
            for h in range(HG_HEADS):
                empty(("lv", n + 1, h), at_2[:, h, :])

            def head_inverse(key, h, rs):
                b = take(dve, (key, h), "dve")
                eng.tensor_scalar(rs, b[:, :], 1.0 / P, EPS, ALU.mult, ALU.add).then_inc(emptied["dve"], 1)
                wait_emptied(dve, (key, h))
                eng.reciprocal(rs, rs).then_inc(head_inv, 1)

            def head_norms():
                for h in range(HG_HEADS):
                    dve.wait_ge(rstd_heads, h + 1)
                    chain.link(eng.scalar_tensor_tensor(out=hk[:, h, :], in0=hk[:, h, :],
                                                        scalar=vec("hgrn_norm_g_2", h), in1=hx[0][:, h, :],
                                                        op0=ALU.mult, op1=ALU.mult))
                    eng.tensor_tensor(y2[:, h, :], y2[:, h, :], hk[:, h, :], ALU.mult).then_inc(y_heads, 1)

            def softplus(h):
                dve.wait_ge(soft_log, h + 1)
                if h >= 2:
                    dve.wait_ge(stick_sums, h - 1)
                for j in range(3):
                    b = peek(dve, ("z", h, j))
                    n = S if j == 0 else 384
                    c = slice(OFF[j], OFF[j] + n)
                    ins = eng.scalar_tensor_tensor(out=soft[h % 2][:, c], in0=b[:, 0:n], scalar=0.0, in1=lnb[:, c],
                                                   op0=ALU.max, op1=ALU.add)
                ins.then_inc(soft_ready, 1)

            softplus(0)
            for h in range(HG_HEADS):
                head_inverse("hs", h, hx[0][:, h, :])
            softplus(1)
            softplus(2)
            head_norms()
            softplus(3)

            def out_second(stage, l, part, summed=True):
                for t in range(KT):
                    b = take(dve, stage + (t,), "dve")
                    col = 48 * l + 8 * part + t
                    eng.scalar_tensor_tensor(out=x[:, t, :], in0=b[:, :], scalar=mod[:, col:col + 1],
                                             in1=x[:, t, :], op0=ALU.mult, op1=ALU.add).then_inc(emptied["dve"], 1)
                    if summed and t % 2 and t < KT - 2:
                        add_squares(t // 2)
                    if l == 0 and t % 2 and not summed:
                        ada_steps(1)

            lows(y2, ye, KT)
            out_second(("even_out",), 0, 2)
            modulated(1, 0, 3, tmp_f, xf)

            def ffn(l):
                name = f"ffn_conv_w_2/{l}"
                dve.wait_ge(pads, l + 1)

                def convolve(t):
                    i = l * FT + t
                    wait_emptied(dve, ("fa", l, t))
                    if i >= 2:
                        dve.wait_ge(gelu_ready, i - 1)
                    r, u = a_raw[t % 2], conv[t % 2][:]
                    chain.link(eng.tensor_scalar(u, r[:, 0:S], vec(name, t), vec("ffn_conv_b_2", FT * l + t),
                                                 ALU.mult, ALU.add))
                    chain.link(eng.scalar_tensor_tensor(out=u, in0=r[:, 1:1 + S], scalar=vec(name, FT + t),
                                                        in1=u, op0=ALU.mult, op1=ALU.add))
                    eng.scalar_tensor_tensor(out=u, in0=r[:, 2:2 + S], scalar=vec(name, 2 * FT + t), in1=u,
                                             op0=ALU.mult, op1=ALU.add).then_inc(conv_ready, 1)

                for part, (lo, hi) in enumerate(FFN_PARTS):
                    for t0 in range(lo, hi + 1, 2):
                        if t0 < hi:
                            convolve(t0)
                            convolve(t0 + 1)
                            if l == 0:
                                ada_steps(1)
                        if t0 > lo:
                            for t in (t0 - 2, t0 - 1):
                                low(prod[:, t % 2, :], (hsp[0][:, t - lo, :], hsp[1][:, t - lo, :]))
                        if t0 < hi:
                            for t in (t0, t0 + 1):
                                b = take(dve, ("fg", l, t), "dve")
                                dve.wait_ge(gelu_ready, l * FT + t + 1)
                                dve.wait_ge(xl_ready, used["x"])
                                eng.tensor_tensor(prod[:, t % 2, :], b[:, :], gel[t % 2][:], ALU.mult
                                                  ).then_inc(emptied["dve"], 1)
                    if l == 0 and part == 1:
                        modulation(1)
                    out_second((f"ffn{l}.out", part), l, 5, part == 1)

            ffn(0)
            modulated(2, 1, 0, tmp_o, xo)
            gr = [g[0:8, :] for g in grow]
            dve.wait_ge(gates_moved, 16)
            log_sigmoid(gr[1], gr[2], gr[3], g_log)
            chain.link(eng.memset(gr[2], 1.0))
            chain.link(eng.tensor_tensor_scan(gr[6], gr[2], gr[3], 0.0, ALU.mult, ALU.add))
            eng.tensor_tensor(gr[4], gr[0], gr[6], ALU.subtract).then_inc(grows_ready, 1)
            dve.wait_ge(grows_ready, 1)
            chain.link(eng.tensor_tensor_scan(gr[5], gr[2], gr[4], 0.0, ALU.mult, ALU.max))
            eng.tensor_tensor(gr[6], gr[6], gr[5], ALU.add).then_inc(m_ready, 1)
            def wcol(k, t):
                return vec("odd_conv_w_2", KT * k + t)

            dve.wait_ge(qk_pads, 1)
            for t in range(KT):
                wait_emptied(dve, ("odd.qk", t))
                u = qkc[:, t, :]
                chain.link(eng.tensor_scalar(u, qk_raw[:, t, 0:S], wcol(0, t), vec("odd_conv_b_2", t),
                                             ALU.mult, ALU.add))
                for k in range(1, 4):
                    ins = eng.scalar_tensor_tensor(out=u, in0=qk_raw[:, t, k:k + S], scalar=wcol(k, t), in1=u,
                                                   op0=ALU.mult, op1=ALU.add)
                    if k < 3:
                        chain.link(ins)
                    else:
                        ins.then_inc(qk_conv, 1)
            b = take(dve, ("gcol",), "dve")
            eng.tensor_scalar(ngcol.rearrange("p a b -> p (a b)"), b[:, 0:NB * ML_HEADS], -1.0, None, ALU.mult
                              ).then_inc(emptied["dve"], 1)
            for h in range(ML_HEADS + 1):
                if h < ML_HEADS:
                    dve.wait_ge(dec_masked, h + 1)
                    W = dec[h % 2]
                    for j in range(3):
                        b = take(dve, ("qk", h, j), "dve")
                        n = S if j == 0 else 384
                        c = slice(OFF[j], OFF[j] + n)
                        eng.scalar_tensor_tensor(out=W[:, c], in0=b[:, 0:n], scalar=64.0 ** -0.5, in1=W[:, c],
                                                 op0=ALU.mult, op1=ALU.mult).then_inc(emptied["dve"], 1)
                if h >= 1:
                    g = h - 1
                    b = take(dve, ("den", g), "dve")
                    wait_emptied(dve, ("eb", g))
                    chain.link(eng.tensor_tensor(den[:], b[:, :], floor_b[g % 2][:], ALU.max))
                    eng.scalar_tensor_tensor(out=den[:], in0=b[:, :], scalar=-1.0, in1=den[:], op0=ALU.mult, op1=ALU.max
                                             ).then_inc(emptied["dve"], 1)
                    wait_emptied(dve, ("den", g))
                    if g >= 1:
                        wait_emptied(dve, ("num", g - 1))
                    chain.link(eng.reciprocal(deni[:], den[:]))
                    b = take(dve, ("num", g), "dve")
                    eng.tensor_tensor(ho[:, g, :], b[:, :], deni[:], ALU.mult).then_inc(emptied["dve"], 1)
                if h >= 2:
                    head_inverse("ms", h - 2, hrs[h - 2])

            def head_output(h):
                dve.wait_ge(rstd_heads, HG_HEADS + h + 1)
                dve.wait_ge(gated, h + 1)
                eng.scalar_tensor_tensor(out=og[:, h, :], in0=og[:, h, :], scalar=vec("odd_norm_g_2", h),
                                         in1=hrs[h], op0=ALU.mult, op1=ALU.mult).then_inc(y_heads, 1)

            for h in range(2):
                head_output(h)
            head_inverse("ms", ML_HEADS - 1, hrs[ML_HEADS - 1])
            for h in range(KT):
                if h >= 2:
                    head_output(h)
                low(og[:, h, :], (yo[0][:, h, :], yo[1][:, h, :]))
            out_second(("odd_out",), 1, 2)
            modulated(3, 1, 3, tmp_f, xf)
            ffn(1)
            normed(3, D, x, out_n, [vec("final_g_2", t) for t in range(KT)], out_normed, squares=2)
            for half in range(2):
                for j in range(NB):
                    empty(("out", j, half), out_tok[:, j, half * S:(half + 1) * S])

        @block.gpsimd
        def _(eng):
            pool = Engine(eng)
            low_done = [0]
            pe_at = [n for n, c in enumerate(plan) if c[0] != "ada"]

            def low_weights(upto):
                while low_done[0] < min(upto, len(released)):
                    m = low_done[0]
                    n = pe_at[m]
                    w = plan[n][2] * plan[n][3]
                    pool.wait_ge(wh_ready, m + 1)
                    eng.tensor_tensor(wl[:, m % SPLIT, 0:w], ring[:, n % RING, 0:w],
                                      wh[:, m % SPLIT, 0:w].bitcast(F32), ALU.subtract).then_inc(wl_ready, 1)
                    low_done[0] += 1

            load_vectors(eng, 1)
            low_weights(tile_chunk[index[("in_a.gate", KT - 1)]] + 2)
            peek(pool, ("in_a.gate", KT - 1))
            pool.wait_ge(kr_ready, 1)
            eng.dma_start(kf[ropes, :, :], kr[ropes, :].unsqueeze(1).to_broadcast([ROPE, HEADS, S])
                          ).then_inc(kf_ready, 16)

            def attention(l):
                low_weights(mark[f"att{l}"] + 2)
                for h in range(16):
                    par = h % 2
                    pool.wait_ge(rinv_ready, l * 16 + h + 1)
                    for i in range(NB - 1):
                        w = probs[:, par, packed(h, i):packed(h, i) + keys(h, i)]
                        eng.tensor_scalar(w, w, rinv[:, par, i:i + 1], None, ALU.mult).then_inc(probs_ready, 1)

            def add_x(l):
                low_weights(tile_chunk[index[(("out_a", "out_b")[l], KT - 1)]] + 2)
                for t in range(POOL_ADDS):
                    pool.wait_ge(post_scaled, l * KT + t + 1)
                    eng.tensor_tensor(x[:, t, :], x[:, t, :], o1[:, t, :], ALU.add).then_inc(x_ready, 1)
                low_weights(tile_chunk[index[(("out_a", "out_b")[l], KT - 1)]] + 3)

            attention(0)
            add_x(0)
            pool.wait_ge(xl_ready, SPLIT_AT["x_b"] + KT)
            for t in (qf, kf):
                eng.dma_start(t[HD:HD + 2, :, :].rearrange("p h s -> p (h s)").rearrange("p (r c) -> p r c", c=P),
                              a["const_f32"][0:2 * HEADS * NB, C_ONE:C_ONE + P].rearrange("(p r) c -> p r c", p=2)
                              ).then_inc(frows_set, 16)
            attention(1)
            add_x(1)
            low_weights(mark["att1"] + 6)
            pool.wait_ge(xl_ready, SPLIT_AT["x_even"] + KT)
            eng.memset(pb[:, :, :], 1.0).then_inc(hg_set, 1)
            eng.memset(at_d[:, :, :], 0.0).then_inc(hg_set, 1)
            pool.wait_ge(lb_ready, 1)
            for h in range(HG_HEADS):
                low_weights(tile_chunk[index[("even.fa", h)]] + 2)
                wait_emptied(pool, ("even.fa", h))
                eng.tensor_scalar(pf[:, h, :], pf[:, h, :], lbt[:, 3, h:h + 1], lbt[:, 2, h:h + 1], ALU.mult, ALU.add)
                eng.tensor_scalar(hk[:, h, :], hk[:, h, :], lbt[:, 3, h:h + 1], None, ALU.mult).then_inc(hg_ready, 1)
            def triangle(v, op, last):
                for j in range(NB):
                    d = v[:, OFF[j]:OFF[j] + P]
                    ins = eng.affine_select(out=d, in_=d, compare_op=op, fill=0.0, base=0, pattern=[[1, P]],
                                            channel_multiplier=-1)
                ins.then_inc(last, 1)

            low_weights(mark["hgrn"] + 1)
            for h in range(4):
                pool.wait_ge(soft_ready, h + 1)
                triangle(soft[h % 2], ALU.is_gt, soft_masked)
                low_weights(mark["hgrn"] + 2)

            def zero_pads(first):
                pool.wait_ge(scaled, first)
                for n in range(2):
                    ins = eng.memset(a_raw[n][:, 0:2], 0.0)
                ins.then_inc(pads, 1)

            low_weights(tile_chunk[index[("even_out", KT - 1)]] + 3)
            zero_pads(3 * KT + 1)
            low_weights(tile_chunk[index[("ffn0.out", 1, KT - 1)]] + 3)
            pool.wait_ge(scaled, 4 * KT + 1)
            eng.memset(qk_raw[:, :, 0:3], 0.0).then_inc(qk_pads, 1)
            low_weights(tile_chunk[index[("og_rows",)]] + 2)
            wait_emptied(pool, ("og_rows",))
            eng.dma_start(grow[1][0:8, :], grow[0][8:16, :]).then_inc(gates_moved, 16)
            low_weights(mark["mlstm"] + 2)

            def gate_head(h):
                wait_emptied(pool, ("num", h))
                wait_emptied(pool, ("odd.og", KT - 1))
                eng.tensor_tensor(og[:, h, :], og[:, h, :], ho[:, h, :], ALU.mult).then_inc(gated, 1)

            for h in range(ML_HEADS):
                pool.wait_ge(dec_exp, h + 1)
                triangle(dec[h % 2], ALU.is_ge, dec_masked)
                if h >= 2:
                    gate_head(h - 2)
            gate_head(ML_HEADS - 2)
            gate_head(ML_HEADS - 1)
            low_weights(tile_chunk[index[("odd_out", KT - 1)]] + 3)
            zero_pads(5 * KT + 1)
            low_weights(len(released))


def kernel(**inputs):
    import concourse.bacc as bacc
    from concourse.bass_utils import run_bass_kernel_spmd as run

    arrays = {name: np.ascontiguousarray(v) for name, v in inputs.items()}
    arrays["const_f32"] = constants()
    nc = bacc.Bacc("TRN2", target_bir_lowering=False, num_devices=1)
    aps = {name: nc.dram_tensor(f"in_{name}", v.shape, mybir.dt.from_np(v.dtype), kind="ExternalInput").ap()
           for name, v in arrays.items()}
    out = nc.dram_tensor("out", (1, S, D), F32, kind="ExternalOutput").ap()
    two_block_kernel(nc, aps, out)
    r = run(nc, [{f"in_{name}": v for name, v in arrays.items()}], core_ids=[0])
    return r.results[0]["out"]
```
